# Optimizing a Trainium2 kernel written in Bass

```python
import math
import jax, jax.numpy as jnp
from jax import lax
import numpy as np

D_MODEL = 1024
BATCH = 1
SEQ = 512
DEPTH = 2
DEC_BATCH = 8
DEC_SEQ = 4
PAST_LEN = 1024
PAGE_SIZE = 128

N_MIXERS = 2
N_SSM_LAYERS = (DEPTH + 1) // 2
N_ATTN_LAYERS = DEPTH // 2
SSM_GROUP = 16
SSM_GROUPS = D_MODEL // SSM_GROUP
SSM_STATE = 64
SWA_GROUPS = ((128, 1), (512, 4), (2048, 16))
N_SWA_GROUPS = len(SWA_GROUPS)
SWA_HEADS = 8
SWA_HEAD_DIM = 64
SWA_WIDTH = SWA_HEADS * SWA_HEAD_DIM
Q_BLOCK = 128
N_MEM = 256
MEM_HEADS = 4
MEM_HEAD_DIM = D_MODEL // MEM_HEADS
D_FF = -(-8 * D_MODEL // (3 * 256)) * 256
RMS_EPS = 1e-6
LOG_STEP_MIN = math.log(1e-3)
LOG_STEP_MAX = math.log(1e-1)

kernel_name = 'hybrid_s5_dilated_swa_memxattn_step'

def rms_norm(x, g):
    xf = x.astype(jnp.float32)
    y = xf * lax.rsqrt(jnp.mean(xf * xf, -1, keepdims=True) + RMS_EPS) * g.astype(jnp.float32)
    return y.astype(x.dtype)

def ssm_mixer(u, h0_re, h0_im, lam_re, lam_im, b_re, b_im, c_re, c_im, d_skip, log_step, w_glu, b_glu):
    f32 = jnp.float32
    bt, L, _ = u.shape
    uf = u.astype(f32)
    ug = uf.reshape(bt, L, SSM_GROUPS, SSM_GROUP)
    lr, li = lam_re.astype(f32), lam_im.astype(f32)
    step = jnp.exp(log_step.astype(f32))[:, None]
    mag = jnp.exp(lr * step)
    ar, ai = mag * jnp.cos(li * step), mag * jnp.sin(li * step)
    den = lr * lr + li * li
    fr = ((ar - 1.0) * lr + ai * li) / den
    fi = (ai * lr - (ar - 1.0) * li) / den
    br, bi = b_re.astype(f32), b_im.astype(f32)
    bbr = fr[..., None] * br - fi[..., None] * bi
    bbi = fr[..., None] * bi + fi[..., None] * br
    bur = jnp.einsum('blgc,gpc->blgp', ug, bbr)
    bui = jnp.einsum('blgc,gpc->blgp', ug, bbi)
    a_r = jnp.broadcast_to(ar, (L,) + ar.shape)
    a_i = jnp.broadcast_to(ai, (L,) + ai.shape)

    def combine(e1, e2):
        a1r, a1i, b1r, b1i = e1
        a2r, a2i, b2r, b2i = e2
        return (a2r * a1r - a2i * a1i, a2r * a1i + a2i * a1r,
                a2r * b1r - a2i * b1i + b2r, a2r * b1i + a2i * b1r + b2i)

    def scan_one(xr, xi, yr, yi):
        return lax.associative_scan(combine, (xr, xi, yr, yi), axis=0)

    pr, pi_, hr, hi = jax.vmap(scan_one, in_axes=(None, None, 0, 0))(a_r, a_i, bur, bui)
    h0r = h0_re.astype(f32)[:, None]
    h0i = h0_im.astype(f32)[:, None]
    hr = hr + pr * h0r - pi_ * h0i
    hi = hi + pr * h0i + pi_ * h0r
    yc = (jnp.einsum('blgp,gcp->blgc', hr, c_re.astype(f32))
          - jnp.einsum('blgp,gcp->blgc', hi, c_im.astype(f32)))
    y = yc.reshape(bt, L, D_MODEL) + d_skip.astype(f32) * uf
    g = jax.nn.gelu(y)
    out = g * jax.nn.sigmoid(g @ w_glu.astype(f32) + b_glu.astype(f32))
    return out.astype(u.dtype), hr[:, -1], hi[:, -1]

def dilated_group_attn(q, k_all, v_all, offset, dil, n_keys):
    bt, L, nh, hd = q.shape
    blk = Q_BLOCK if L % Q_BLOCK == 0 else L
    nb = L // blk
    tap = jnp.arange(n_keys) * dil
    scale = hd ** -0.5

    def block(b):
        qb = lax.dynamic_slice_in_dim(q, b * blk, blk, axis=1)
        pos = offset + b * blk + jnp.arange(blk)
        idx = pos[:, None] - tap[None, :]
        valid = idx >= 0
        idx = jnp.maximum(idx, 0)
        kb = jnp.take(k_all, idx, axis=1)
        vb = jnp.take(v_all, idx, axis=1)
        s = jnp.einsum('bqhd,bqjhd->bqhj', qb, kb).astype(jnp.float32) * scale
        s = jnp.where(valid[None, :, None, :], s, -jnp.inf)
        m = jnp.max(s, -1, keepdims=True)
        p = jnp.exp(s - m)
        den = jnp.sum(p, -1, keepdims=True)
        o = jnp.einsum('bqhj,bqjhd->bqhd', (p / den).astype(vb.dtype), vb)
        lse = (m + jnp.log(den))[..., 0]
        return o, lse

    if nb == 1:
        return block(0)
    o, lse = lax.map(block, jnp.arange(nb))
    o = jnp.moveaxis(o, 0, 1).reshape(bt, L, nh, hd)
    lse = jnp.moveaxis(lse, 0, 1).reshape(bt, L, nh)
    return o, lse

def attn_mixer(h, past_k, past_v, w_qkv, q_g, k_g, w_o):
    bt, L, _ = h.shape
    qkv = (h @ w_qkv).reshape(bt, L, 3, N_SWA_GROUPS, SWA_HEADS, SWA_HEAD_DIM)
    q = rms_norm(qkv[:, :, 0], q_g[:, None, :])
    k = rms_norm(qkv[:, :, 1], k_g[:, None, :])
    v = qkv[:, :, 2]
    outs, lses, new_k, new_v = [], [], [], []
    for g, (win, dil) in enumerate(SWA_GROUPS):
        kg, vg = k[:, :, g], v[:, :, g]
        if past_k is None:
            k_all, v_all, off = kg, vg, 0
            keep = min(win, L)
            new_k.append(kg[:, L - keep:])
            new_v.append(vg[:, L - keep:])
        else:
            k_all = jnp.concatenate([past_k[g].astype(kg.dtype), kg], axis=1)
            v_all = jnp.concatenate([past_v[g].astype(vg.dtype), vg], axis=1)
            off = past_k[g].shape[1]
            new_k.append(kg)
            new_v.append(vg)
        o, lse = dilated_group_attn(q[:, :, g], k_all, v_all, off, dil, win // dil + 1)
        outs.append(o)
        lses.append(lse)
    w = jax.nn.softmax(jnp.stack(lses, 0), axis=0)
    o = jnp.einsum('gblh,gblhd->blhd', w, jnp.stack(outs, 0).astype(jnp.float32))
    y = o.astype(h.dtype).reshape(bt, L, SWA_WIDTH) @ w_o
    return y, new_k, new_v

def mem_kv(mem, g_in, w_kv, k_g):
    bt = mem.shape[0]
    kv = (rms_norm(mem, g_in) @ w_kv).reshape(bt, N_MEM, 2, MEM_HEADS, MEM_HEAD_DIM)
    return rms_norm(kv[:, :, 0], k_g), kv[:, :, 1]

def mem_attn(h, mk, mv, w_q, q_g, w_o):
    bt, L, _ = h.shape
    q = rms_norm((h @ w_q).reshape(bt, L, MEM_HEADS, MEM_HEAD_DIM), q_g)
    s = jnp.einsum('blhd,bmhd->bhlm', q, mk.astype(q.dtype)).astype(jnp.float32) * MEM_HEAD_DIM ** -0.5
    p = jax.nn.softmax(s, axis=-1)
    o = jnp.einsum('bhlm,bmhd->blhd', p.astype(mv.dtype), mv)
    return o.astype(h.dtype).reshape(bt, L, MEM_HEADS * MEM_HEAD_DIM) @ w_o

def swiglu(h, w_in, w_out):
    gu = h @ w_in
    return (jax.nn.silu(gu[..., :D_FF]) * gu[..., D_FF:]) @ w_out

def trunk(x, mem_k, mem_v, h0_re, h0_im, swa_k_cache, swa_v_cache, p):
    ssm_re, ssm_im = [], []
    swa_k = [[] for _ in SWA_GROUPS]
    swa_v = [[] for _ in SWA_GROUPS]
    for i in range(DEPTH):
        j = i // N_MIXERS
        h = rms_norm(x, p['norm_mix_g'][i])
        if i % N_MIXERS == 0:
            y, hr, hi = ssm_mixer(h, h0_re[j], h0_im[j], p['ssm_lambda_re'][j], p['ssm_lambda_im'][j],
                                  p['ssm_b_re'][j], p['ssm_b_im'][j], p['ssm_c_re'][j], p['ssm_c_im'][j],
                                  p['ssm_d'][j], p['ssm_log_step'][j], p['ssm_w_glu'][j], p['ssm_b_glu'][j])
            ssm_re.append(hr)
            ssm_im.append(hi)
        else:
            pk = None if swa_k_cache is None else [c[j] for c in swa_k_cache]
            pv = None if swa_v_cache is None else [c[j] for c in swa_v_cache]
            y, nk, nv = attn_mixer(h, pk, pv, p['attn_w_qkv'][j], p['attn_q_norm_g'][j],
                                   p['attn_k_norm_g'][j], p['attn_w_o'][j])
            for g in range(N_SWA_GROUPS):
                swa_k[g].append(nk[g])
                swa_v[g].append(nv[g])
        x = x + y.astype(x.dtype)
        x = x + mem_attn(rms_norm(x, p['norm_mem_g'][i]), mem_k[i], mem_v[i], p['mem_w_q'][i],
                         p['mem_q_norm_g'][i], p['mem_w_o'][i])
        x = x + swiglu(rms_norm(x, p['norm_ffn_g'][i]), p['ffn_w_in'][i], p['ffn_w_out'][i])
    return (x, jnp.stack(ssm_re, 0), jnp.stack(ssm_im, 0),
            [jnp.stack(a, 0) for a in swa_k], [jnp.stack(a, 0) for a in swa_v])

def setup_inputs(seed: int = 0) -> dict:
    key = jax.random.key(seed)
    ks = iter(jax.random.split(key, 48))
    f32 = jnp.float32

    def nrm(shape, scale):
        return jax.random.normal(next(ks), shape, f32) * scale

    d = {}
    d['x_prompt'] = nrm((BATCH, SEQ, D_MODEL), 1.0)
    d['x_sample'] = nrm((DEC_BATCH, DEC_SEQ, D_MODEL), 1.0)
    d['mem_prompt'] = nrm((BATCH, N_MEM, D_MODEL), 1.0)
    d['state_ssm_re'] = nrm((N_SSM_LAYERS, DEC_BATCH, SSM_GROUPS, SSM_STATE), 0.2)
    d['state_ssm_im'] = nrm((N_SSM_LAYERS, DEC_BATCH, SSM_GROUPS, SSM_STATE), 0.2)
    for g, (win, dil) in enumerate(SWA_GROUPS):
        rows = min(win, PAST_LEN)
        d['cache_swa%d_k' % g] = nrm((N_ATTN_LAYERS, DEC_BATCH, rows, SWA_HEADS, SWA_HEAD_DIM), 1.0)
        d['cache_swa%d_v' % g] = nrm((N_ATTN_LAYERS, DEC_BATCH, rows, SWA_HEADS, SWA_HEAD_DIM), 1.0)
    d['cache_mem_k'] = nrm((DEPTH, DEC_BATCH, N_MEM, MEM_HEADS, MEM_HEAD_DIM), 1.0)
    d['cache_mem_v'] = nrm((DEPTH, DEC_BATCH, N_MEM, MEM_HEADS, MEM_HEAD_DIM), 1.0)
    d['norm_mix_g'] = 1.0 + nrm((DEPTH, D_MODEL), 0.02)
    d['norm_mem_g'] = 1.0 + nrm((DEPTH, D_MODEL), 0.02)
    d['norm_memin_g'] = 1.0 + nrm((DEPTH, D_MODEL), 0.02)
    d['norm_ffn_g'] = 1.0 + nrm((DEPTH, D_MODEL), 0.02)
    sshape = (N_SSM_LAYERS, SSM_GROUPS, SSM_STATE)
    d['ssm_lambda_re'] = -0.5 + nrm(sshape, 0.01)
    d['ssm_lambda_im'] = jnp.pi * jnp.arange(SSM_STATE, dtype=f32) + nrm(sshape, 0.01)
    d['ssm_b_re'] = nrm(sshape + (SSM_GROUP,), (2.0 * SSM_GROUP) ** -0.5)
    d['ssm_b_im'] = nrm(sshape + (SSM_GROUP,), (2.0 * SSM_GROUP) ** -0.5)
    d['ssm_c_re'] = nrm((N_SSM_LAYERS, SSM_GROUPS, SSM_GROUP, SSM_STATE), 4.0 * (2.0 * SSM_STATE) ** -0.5)
    d['ssm_c_im'] = nrm((N_SSM_LAYERS, SSM_GROUPS, SSM_GROUP, SSM_STATE), 4.0 * (2.0 * SSM_STATE) ** -0.5)
    d['ssm_d'] = nrm((N_SSM_LAYERS, D_MODEL), 0.5)
    d['ssm_log_step'] = jax.random.uniform(next(ks), (N_SSM_LAYERS, SSM_GROUPS), f32,
                                           LOG_STEP_MIN, LOG_STEP_MAX)
    d['ssm_w_glu'] = nrm((N_SSM_LAYERS, D_MODEL, D_MODEL), D_MODEL ** -0.5)
    d['ssm_b_glu'] = nrm((N_SSM_LAYERS, D_MODEL), 0.01)
    d['attn_w_qkv'] = nrm((N_ATTN_LAYERS, D_MODEL, 3 * N_SWA_GROUPS * SWA_WIDTH), D_MODEL ** -0.5)
    d['attn_q_norm_g'] = 1.0 + nrm((N_ATTN_LAYERS, N_SWA_GROUPS, SWA_HEAD_DIM), 0.02)
    d['attn_k_norm_g'] = 1.0 + nrm((N_ATTN_LAYERS, N_SWA_GROUPS, SWA_HEAD_DIM), 0.02)
    d['attn_w_o'] = nrm((N_ATTN_LAYERS, SWA_WIDTH, D_MODEL), SWA_WIDTH ** -0.5)
    d['mem_w_q'] = nrm((DEPTH, D_MODEL, MEM_HEADS * MEM_HEAD_DIM), D_MODEL ** -0.5)
    d['mem_w_kv'] = nrm((DEPTH, D_MODEL, 2 * MEM_HEADS * MEM_HEAD_DIM), D_MODEL ** -0.5)
    d['mem_q_norm_g'] = 1.0 + nrm((DEPTH, MEM_HEAD_DIM), 0.02)
    d['mem_k_norm_g'] = 1.0 + nrm((DEPTH, MEM_HEAD_DIM), 0.02)
    d['mem_w_o'] = nrm((DEPTH, MEM_HEADS * MEM_HEAD_DIM, D_MODEL), (MEM_HEADS * MEM_HEAD_DIM) ** -0.5)
    d['ffn_w_in'] = nrm((DEPTH, D_MODEL, 2 * D_FF), D_MODEL ** -0.5)
    d['ffn_w_out'] = nrm((DEPTH, D_FF, D_MODEL), D_FF ** -0.5)
    return d

def reference(x_prompt, x_sample, mem_prompt, state_ssm_re, state_ssm_im,
              cache_swa0_k, cache_swa0_v, cache_swa1_k, cache_swa1_v, cache_swa2_k, cache_swa2_v,
              cache_mem_k, cache_mem_v,
              norm_mix_g, norm_mem_g, norm_memin_g, norm_ffn_g,
              ssm_lambda_re, ssm_lambda_im, ssm_b_re, ssm_b_im, ssm_c_re, ssm_c_im, ssm_d,
              ssm_log_step, ssm_w_glu, ssm_b_glu,
              attn_w_qkv, attn_q_norm_g, attn_k_norm_g, attn_w_o,
              mem_w_q, mem_w_kv, mem_q_norm_g, mem_k_norm_g, mem_w_o,
              ffn_w_in, ffn_w_out):
    p = dict(norm_mix_g=norm_mix_g, norm_mem_g=norm_mem_g, norm_ffn_g=norm_ffn_g,
             ssm_lambda_re=ssm_lambda_re, ssm_lambda_im=ssm_lambda_im, ssm_b_re=ssm_b_re,
             ssm_b_im=ssm_b_im, ssm_c_re=ssm_c_re, ssm_c_im=ssm_c_im, ssm_d=ssm_d,
             ssm_log_step=ssm_log_step, ssm_w_glu=ssm_w_glu, ssm_b_glu=ssm_b_glu,
             attn_w_qkv=attn_w_qkv, attn_q_norm_g=attn_q_norm_g, attn_k_norm_g=attn_k_norm_g,
             attn_w_o=attn_w_o, mem_w_q=mem_w_q, mem_q_norm_g=mem_q_norm_g, mem_w_o=mem_w_o,
             ffn_w_in=ffn_w_in, ffn_w_out=ffn_w_out)

    pmk, pmv = [], []
    for i in range(DEPTH):
        k_i, v_i = mem_kv(mem_prompt, norm_memin_g[i], mem_w_kv[i], mem_k_norm_g[i])
        pmk.append(k_i)
        pmv.append(v_i)
    p_mem_k = jnp.stack(pmk, 0)
    p_mem_v = jnp.stack(pmv, 0)
    zeros_state = jnp.zeros((N_SSM_LAYERS, x_prompt.shape[0], SSM_GROUPS, SSM_STATE), jnp.float32)
    y_prompt, p_ssm_re, p_ssm_im, p_swa_k, p_swa_v = trunk(
        x_prompt, p_mem_k, p_mem_v, zeros_state, zeros_state, None, None, p)

    y_sample, s_ssm_re, s_ssm_im, s_swa_k, s_swa_v = trunk(
        x_sample, cache_mem_k, cache_mem_v, state_ssm_re, state_ssm_im,
        [cache_swa0_k, cache_swa1_k, cache_swa2_k], [cache_swa0_v, cache_swa1_v, cache_swa2_v], p)

    p_swa0_k, p_swa1_k, p_swa2_k = p_swa_k
    p_swa0_v, p_swa1_v, p_swa2_v = p_swa_v
    s_swa0_k, s_swa1_k, s_swa2_k = s_swa_k
    s_swa0_v, s_swa1_v, s_swa2_v = s_swa_v
    return (y_prompt, y_sample,
            p_ssm_re, p_ssm_im, p_swa0_k, p_swa0_v, p_swa1_k, p_swa1_v, p_swa2_k, p_swa2_v,
            p_mem_k, p_mem_v,
            s_ssm_re, s_ssm_im, s_swa0_k, s_swa0_v, s_swa1_k, s_swa1_v, s_swa2_k, s_swa2_v)


_drawn_inputs = setup_inputs


def setup_inputs(seed=0):
    import zlib

    import numpy as np

    out = dict(_drawn_inputs(seed))
    spreads = {}
    factors = {'norm_mem_g': 8.0,
     'norm_memin_g': 2.749,
     'norm_ffn_g': 2.799,
     'ssm_lambda_re': 3.849,
     'ssm_b_glu': 8.0,
     'attn_q_norm_g': 8.0,
     'attn_k_norm_g': 2.738,
     'mem_q_norm_g': 8.0,
     'mem_k_norm_g': 2.733}
    for name, (base, spread) in spreads.items():
        noise = np.random.default_rng([zlib.crc32(name.encode()), seed]).standard_normal(out[name].shape)
        drawn = base * np.exp(spread * noise) if base else spread * noise
        out[name] = __import__('jax').numpy.asarray(drawn.astype(out[name].dtype))
    for name, factor in factors.items():
        out[name] = (out[name] * factor).astype(out[name].dtype)
    return out
```

```python
from contextlib import ExitStack

import numpy as np

import concourse.bass as bass
from concourse import mybir

F32 = mybir.dt.float32
I32 = mybir.dt.int32
ALU = mybir.AluOpType
ACT = mybir.ActivationFunctionType
AX = mybir.AxisListType.X

P = 128
D = 1024
KT = D // P
SEQ, DB, DS = 512, 8, 4
NS = DB * DS
T = SEQ + NS
HT = T // 2
NM, MH, MD = 256, 4, 256
G, GC, GS = 64, 16, 64
CH = 8
NC = SEQ // CH
NCC = NC + DB
GP = G // 2
NB, BG = 4, 8
FF = 2816
FT = FF // P
SH, SD, SW = 8, 64, 512
NG = 3
RUNIT = 256
EPS = 1e-6
BIG = -1e30
UW = 11 * RUNIT


def hybrid_step(nc, a, o):
    with ExitStack() as ctx:
        names = {}

        def S(name):
            if name not in names:
                names[name] = ctx.enter_context(nc.semaphore(name))
            return names[name]

        class Lane:

            def __init__(self, eng, own):
                self.e, self.own, self.n, self.last = eng, own, {}, None

            def did(self, ins, sem=None):
                sem = sem or self.own
                ins.then_inc(S(sem), 1)
                self.n[sem] = self.n.get(sem, 0) + 1
                self.last = (sem, self.n[sem])

            def settle(self):
                if self.last:
                    self.e.wait_ge(S(self.last[0]), self.last[1])

            def need(self, sem, value):
                self.e.wait_ge(S(sem), value)

        def sb(name, n, dt=F32):
            return ctx.enter_context(nc.sbuf_tensor(name, [P, n], dt))

        ps = ctx.enter_context(nc.psum_tensor("ps", [P, 8, 512], F32))
        ident = sb("ident", P)
        ones = sb("ones", P)
        epst = sb("epst", 1)
        gcol = sb("gcol", 96)
        xT = sb("xT", KT * T)[:].rearrange("p (k t) -> p k t", k=KT)
        hT = sb("hT", KT * T)[:].rearrange("p (k t) -> p k t", k=KT)
        ring = sb("ring", 2 * UW)
        mKT0 = sb("mKT", 2 * KT * NM)
        mV0 = sb("mV", 2 * 2 * D)
        mKT = mKT0[:].rearrange("p (l f m) -> p l f m", l=2, f=KT)
        mV = mV0[:].rearrange("p (l c n) -> p l c n", l=2, c=2)
        rstd = sb("rstd", T)
        AR = 26700
        arena = sb("arena", AR)

        class Space:
            def __init__(self, base, size, at=0):
                self.b, self.size, self.at = base, size, at

            def take(self, n, pat=None, **kw):
                v = self.b[:, self.at:self.at + n]
                self.at += n
                assert self.at <= self.size, (self.at, self.size)
                return v.rearrange(pat, **kw) if pat else v

        items, units = {}, {}

        def item(*key):
            items[key] = len(items)

        unit_end = {}

        def unit(*key):
            units[key] = len(units)

        def ends(n=None):
            m = len(items) - 1
            unit_end[len(units) - 1] = (f"bank_full{m % 8}", m // 8 + 1)

        def fill(pe, key):
            n = items[key]
            if n >= 8:
                pe.wait_ge(S(f"bank_free{n % 8}"), n // 8)
            return ps[:, n % 8, :]

        def filled(key, ins):
            ins.then_inc(S(f"bank_full{items[key] % 8}"), 1)

        def full(L, key):
            n = items[key]
            L.e.wait_ge(S(f"bank_full{n % 8}"), n // 8 + 1)
            return ps[:, n % 8, :]

        def free(L, key, ins):
            n = items[key]
            ins.then_inc(S(f"bank_free{n % 8}"), 1)
            L.last = (f"bank_free{n % 8}", n // 8 + 1)

        def landed(e, key):
            n = items[key]
            e.wait_ge(S(f"bank_free{n % 8}"), n // 8 + 1)

        def uslot(key, kt):
            n = units[key]
            return ring[:, (n % 2) * UW:(n % 2) * UW + kt * RUNIT].rearrange("p (k c) -> p k c", k=kt)

        def uready(pe, key):
            n = units[key]
            pe.wait_ge(S(f"w_full{n % 2}"), wcount(n))

        for i in range(3):
            item("par", i)
        for i in range(2):
            item("cT", i)
        for f in range(KT):
            item("xT", f)
        for f in range(2):
            item("xsT", f)

        def plan_memkv(l):
            for f in range(KT // 2):
                item("memT", l, f)
            for j in range(8):
                item("kv", l, j)
                unit("kv", l, j)
                ends()
                if 1 <= j <= 4:
                    item("mkT", l, j - 1)
        plan_memkv(0)
        for k in range(NB):
            for i in range(4):
                item("U", k, i)
            for i in range(4):
                item("K", k, i)
            for i in range(4):
                item("Q", k, i)
            for i in range(4):
                item("W", k, i)
            for i in range(4):
                item("Y", k, i)
            for f in range(2):
                for i in range(2):
                    item("yT", k, f, i)
        for i in range(2):
            item("fin", i)

        halves = [0]

        def plan_resid(name, nu):
            for j in range(4):
                for s in range(nu):
                    unit(name, j, s)
                    if s < nu - 1:
                        halves[0] += 1
                        unit_end[len(units) - 1] = ("w_half", halves[0])
                for m in range(2):
                    for h in range(2):
                        item(name, 2 * j + m, h)
                ends()
        plan_resid("glu", 1)
        plan_memkv(1)

        def plan_norm(k):
            item("ssq", k, 0)
            item("ssq", k, 1)

        def plan_memattn(l):
            for h in range(MH):
                unit("mq", l, h)
                for i in range(3):
                    item("mq", l, h, i)
                ends()
                if h >= 1:
                    for i in range(3):
                        item("mqT", l, h - 1, i)
            for i in range(3):
                item("mqT", l, MH - 1, i)
            for h in range(MH + 1):
                if h < MH:
                    item("ms", l, h, 0)
                    item("ms", l, h, 1)
                if h >= 1:
                    item("mp", l, h - 1, 0)
                    item("mp", l, h - 1, 1)
                    item("mo", l, h - 1, 0)
                    item("mo", l, h - 1, 1)
            for b in range(DB):
                for i in range(4):
                    item("skT", l, b, i)
                item("ssT", l, b)
            item("ss", l)
            item("sp", l)
            item("so", l)
            plan_resid(f"mo{l}", 1)

        def plan_ffn(l):
            for u in range(FT):
                unit("fi", l, u)
                for j in range(4):
                    item("fi", l, u, j)
                ends()
            plan_resid(f"fo{l}", 2)

        def plan_swa():
            for u in range(18):
                unit("qkv", u)
                for i in range(3):
                    item("qkv", u, i)
                ends()
                if 1 <= u <= 12:
                    for i in range(3):
                        item("qkT", u - 1, i)
            for n in range(SH * 4 + 1):
                if n < SH * 4:
                    item("as", n, 0)
                    item("as", n, 1)
                if n >= 1:
                    item("ap", n - 1, 0)
                    item("ap", n - 1, 1)
                    item("ao", n - 1)
            for b in range(DB):
                for i in range(7):
                    item("bkT", b, i)
                item("bs", b)
            item("bn", 0)
            item("bn", 1)
            for R in range(2):
                item("br", R)
            for i in range(3):
                item("bp", i)
            for b in range(DB):
                item("bo", b)
            item("bo", "new")
            plan_resid("wo", 1)

        plan_norm(0)
        plan_memattn(0)
        plan_norm(1)
        plan_ffn(0)
        plan_norm(2)
        plan_swa()
        plan_norm(3)
        plan_memattn(1)
        plan_norm(4)
        plan_ffn(1)
        for t in range(5):
            item("out", t, 0)
            item("out", t, 1)

        A = Space(arena, AR)
        x8 = A.take(CH * 256, "p (s n) -> p s n", s=CH)
        ub = A.take(CH * 256, "p (g s c) -> p g s c", g=16, s=CH)
        Ub = A.take(16 * NCC, "p (g n) -> p g n", g=16)
        CAr = A.take(BG * 9 * GC, "p (g t c) -> p g t c", g=BG, t=9)
        CAi = A.take(BG * 9 * GC, "p (g t c) -> p g t c", g=BG, t=9)
        QBr = A.take(BG * CH * GC, "p (g s c) -> p g s c", g=BG, s=CH)
        QBi = A.take(BG * CH * GC, "p (g s c) -> p g s c", g=BG, s=CH)
        Qt = A.take(2 * BG * P, "p (i g n) -> p i g n", i=2, g=BG)
        early = A.at
        Tt = A.take(16 * P, "p (g n) -> p g n", g=16)
        Kp = Qt.rearrange("p i g n -> p (i g n)")[:, 0:8 * 15 * GC].rearrange("p (g n) -> p g n", g=8)
        E0 = Space(arena, AR, early)
        Rr = A.take(GP * NC, "p (g n) -> p g n", g=GP)
        Ri = A.take(GP * NC, "p (g n) -> p g n", g=GP)
        Sr = A.take(BG * (NC + 1), "p (g n) -> p g n", g=BG)
        Si = A.take(BG * (NC + 1), "p (g n) -> p g n", g=BG)
        Bb = A.take(2 * GP * GC, "p (i g c) -> p i g c", i=2, g=GP)
        Ct = A.take(2 * GP * GC, "p (i g c) -> p i g c", i=2, g=GP)
        h0 = A.take(2 * GP * DB, "p (i g b) -> p i g b", i=2, g=GP)
        ws = A.take(2 * GP * DB, "p (i g b) -> p i g b", i=2, g=GP)
        tA = A.take(1024)
        tB = A.take(1024)
        apw = A.take(2 * 9 * GP, "p (i t g) -> p i t g", i=2, t=9)
        arev = A.take(2 * 8 * GP, "p (i t g) -> p i t g", i=2, t=8)
        prm = A.take(12 * GP, "p (i g) -> p i g", i=12)
        gainU = A.take(G)
        Dd = A.take(G)
        ss8 = A.take(NB * CH, "p (k s) -> p k s", k=NB)
        r8 = A.take(CH)
        mss = A.take(16)
        fst = A.take(2 * GP, "p (i g) -> p i g", i=2)
        D0 = rstd[:, 0:BG * NC].rearrange("p (g n) -> p g n", g=BG)
        craw = E0.take(2 * 4 * P, "p (i t n) -> p i t n", i=2, t=4)
        braw = E0.take(2 * GP * GC, "p (i g c) -> p i g c", i=2, g=GP)
        lrow = E0.take(3 * P, "p (i n) -> p i n", i=3)
        prow = E0.take(P)
        hraw = E0.take(4 * P, "p (i n) -> p i n", i=4)
        lstep = E0.take(2)
        drow = E0.take(2 * GC)
        grep = E0.take(CH * GC, "p (s c) -> p s c", s=CH)
        hflat = hT.rearrange("p k t -> p (k t)")
        xnat = hflat[:, 0:4 * D].rearrange("p (t n) -> p t n", t=4)
        xsn = arena[:, CH * 256:CH * 256 + D]
        memT = mKT0[:, KT * NM:].rearrange("p (f m) -> p f m", f=KT)
        mnat = mV0[:, 2 * D:].rearrange("p (c n) -> p c n", c=2)
        mkg = sb("mkg", 2 * MD)
        kgb = sb("kgb", NG * SD)

        def g_mix(l, f):
            return gcol[:, 8 * l + f:8 * l + f + 1]

        def g_mem(l, f):
            return gcol[:, 16 + 8 * l + f:17 + 8 * l + f]

        def g_memin(l, f):
            return gcol[:, 32 + 8 * l + f:33 + 8 * l + f]

        def g_ffn(l, f):
            return gcol[:, 48 + 8 * l + f:49 + 8 * l + f]

        def g_mq(l, d):
            return gcol[:, 64 + 2 * l + d:65 + 2 * l + d]

        def b_glu(f):
            return gcol[:, 68 + f:69 + f]

        def g_sq(g):
            return gcol[:, 76 + g:77 + g]

        def half(h):
            return slice(HT * h, HT * h + HT)

        def load_unit(sp, src, key, kt, rows, cols):
            n = units[key]
            if n >= 2:
                sp.wait_ge(S(unit_end[n - 2][0]), unit_end[n - 2][1])
            sp.dma_start(uslot(key, kt), src[rows, cols].rearrange("(k p) n -> p k n", p=P)) \
              .then_inc(S(f"w_full{n % 2}"), 16)

        def cols(j):
            return slice(j * RUNIT, (j + 1) * RUNIT)

        def sp_params(sp):
            q = S("ld_par")
            n = 0
            for r, name in ((0, "norm_mix_g"), (16, "norm_mem_g"), (32, "norm_memin_g"), (48, "norm_ffn_g")):
                sp.dma_start(prow[r:r + 16, :], a[name].rearrange("l (k p) -> (l k) p", p=P)).then_inc(q, 16)
            sp.dma_start(prow[64:68, :], a["mem_q_norm_g"].rearrange("l (k p) -> (l k) p", p=P)).then_inc(q, 16)
            sp.dma_start(prow[68:76, :], a["ssm_b_glu"].rearrange("l (k p) -> (l k) p", p=P)).then_inc(q, 16)
            for i in range(2):
                sp.dma_start(prow[76:79, i * SD:(i + 1) * SD], a["attn_q_norm_g"][0]).then_inc(q, 16)
            sp.dma_start(lrow[0:GP, 0, :], a["ssm_lambda_re"][0].rearrange("(g r) p -> g (r p)", r=2)).then_inc(q, 16)
            sp.dma_start(lrow[0:GP, 1, :], a["ssm_lambda_im"][0].rearrange("(g r) p -> g (r p)", r=2)).then_inc(q, 16)
            sp.dma_start(lstep[0:GP, :], a["ssm_log_step"][0].rearrange("(g r) -> g r", r=2)).then_inc(q, 16)
            sp.dma_start(drow[0:G, 0:GC], a["ssm_d"][0].rearrange("(g c) -> g c", c=GC)).then_inc(q, 16)
            sp.dma_start(drow[0:G, GC:], a["norm_mix_g"][0].rearrange("(g c) -> g c", c=GC)).then_inc(q, 16)
            for i, name in enumerate(("ssm_b_re", "ssm_b_im")):
                for r in range(2):
                    sp.dma_start(braw[64 * r:64 * r + 64, i], a[name][0].rearrange("(g r) p c -> r p g c", r=2)[r]) \
                      .then_inc(q, 16)
            for i, name in enumerate(("state_ssm_re", "state_ssm_im")):
                v = a[name][0].rearrange("b (g r) p -> (b g) (r p)", r=2)
                for t in range(2):
                    sp.dma_start(hraw[:, 2 * i + t, :], v[P * t:P * t + P]).then_inc(q, 16)
            for i, name in enumerate(("ssm_c_re", "ssm_c_im")):
                v = a[name][0].rearrange("(t g r) c p -> t g r c p", t=4, r=2)
                for t in range(4):
                    for g in range(8):
                        sp.dma_start(craw[16 * g:16 * g + 16, i, t, :].rearrange("q (r p) -> q r p", r=2),
                                     v[t, g].rearrange("r c p -> c r p")).then_inc(q, 16)

        N_PAR = 8 + 5 + 4 + 4 + 64

        def act_loads(sc):
            sc.dma_start(mnat, a["mem_prompt"][0].rearrange("(c p) n -> p c n", p=P)).then_inc(S("ld_mem"), 16)
            sc.dma_start(xnat, a["x_prompt"][0].rearrange("(t p) n -> p t n", p=P)).then_inc(S("ld_x"), 16)
            sc.dma_start(xsn[0:NS], a["x_sample"].rearrange("b t n -> (b t) n")).then_inc(S("ld_x"), 16)
            sc.dma_start(mkg[:], a["mem_k_norm_g"].rearrange("l n -> (l n)").unsqueeze(0).to_broadcast([P, 2 * MD])) \
              .then_inc(S("ld_bc"), 16)
            sc.dma_start(kgb[:], a["attn_k_norm_g"][0].rearrange("l n -> (l n)").unsqueeze(0)
                         .to_broadcast([P, NG * SD])).then_inc(S("ld_bc"), 16)

        def sp_memkv(sp, l):
            for j in range(8):
                load_unit(sp, a["mem_w_kv"][l], ("kv", l, j), KT, slice(0, D), cols(j))

        xv = a["x_prompt"][0].rearrange("(c s) n -> c s n", s=CH)

        def sp_x8(sp, pas, k):
            n = pas * NB + k
            if 1 <= n <= NB:
                sp.wait_ge(S("x8_sq"), n)
            if n > NB:
                sp.wait_ge(S("x8_used"), n - NB)
            if n == 0:
                sp.wait_ge(S("x8_zero"), 1)
            sl = slice(256 * k, 256 * k + 256)
            sp.dma_start(x8[0:NC], xv[:, :, sl]).then_inc(S("ld_x8"), 16)
            sp.dma_start(x8[NC:NCC, DS:CH], a["x_sample"][:, :, sl]).then_inc(S("ld_x8"), 16)

        def x8_ready(e, pas, k):
            n = pas * NB + k
            e.wait_ge(S("ld_x8"), 32 * (n + 1))

        def sp_toeplitz(sp, k):
            for hf in range(2):
                landed(sp, ("K", k, 2 * hf))
                landed(sp, ("K", k, 2 * hf + 1))
                if hf == 0 and k > 0:
                    landed(sp, ("Y", k - 1, 3))
                for s in range(CH):
                    c = (CH - 1 - s) * GC
                    sp.dma_start(Tt[GC * s:GC * s + GC, 8 * hf:8 * hf + 8, :],
                                 Kp[0:GC, :, c:c + P]).then_inc(S("toep"), 16)

        def pool_consts(L):
            L.settle()
            L.did(nc.gpsimd.memset(ident[:], 0.0))
            L.settle()
            L.did(nc.gpsimd.affine_select(out=ident[:], in_=ident[:], compare_op=ALU.not_equal, fill=1.0, base=0,
                                          pattern=[[-1, P]], channel_multiplier=1), "ident_ready")
            L.settle()
            L.did(nc.gpsimd.memset(ones[:], 1.0))
            L.settle()
            L.did(nc.gpsimd.memset(epst[:], EPS))
            L.settle()
            L.did(nc.gpsimd.memset(x8[64:NCC, 0:DS, :], 0.0), "x8_zero")
            L.settle()
            L.did(nc.gpsimd.memset(Sr[:, :, 0:1], 0.0))
            L.settle()
            L.did(nc.gpsimd.memset(Si[:, :, 0:1], 0.0), "consts_ready")

        def vec(L):
            v = nc.vector

            def tt(out, x, y, op, sem=None, dep=True):
                if dep:
                    L.settle()
                L.did(v.tensor_tensor(out, x, y, op), sem)

            def ts(out, x, s1, s2, op0, op1=None, sem=None, dep=True):
                if dep:
                    L.settle()
                if op1 is None:
                    L.did(v.tensor_scalar(out, x, s1, None, op0), sem)
                else:
                    L.did(v.tensor_scalar(out, x, s1, s2, op0, op1), sem)

            def stt(out, x, s, y, op0, op1, sem=None, dep=True):
                if dep:
                    L.settle()
                L.did(v.scalar_tensor_tensor(out=out, in0=x, scalar=s, in1=y, op0=op0, op1=op1), sem)

            def cp(out, x, sem=None, dep=True):
                if dep:
                    L.settle()
                L.did(v.tensor_copy(out, x), sem)

            def recip(out, x, sem=None):
                L.settle()
                L.did(v.reciprocal(out, x), sem)

            def cmul(or_, oi, ar, ai, br, bi, t1, t2):
                tt(t1, ar, br, ALU.mult)
                tt(t2, ai, bi, ALU.mult, dep=False)
                tt(or_, t1, t2, ALU.subtract)
                tt(t1, ar, bi, ALU.mult)
                tt(t2, ai, br, ALU.mult, dep=False)
                tt(oi, t1, t2, ALU.add)

            L.tt, L.ts, L.stt, L.cp, L.recip, L.cmul = tt, ts, stt, cp, recip, cmul

        MAGIC = 1.5 * 2.0 ** 23
        LN2H = float(np.float32(0.693359375))
        LN2L = float(np.float32(np.log(2.0) - 0.693359375))

        def v_exp(L, out, x, n, r, ii):
            L.ts(r, x, 88.0, -87.0, ALU.min, ALU.max)
            L.ts(n, r, 1.0 / float(np.log(2.0)), MAGIC, ALU.mult, ALU.add)
            L.ts(n, n, -MAGIC, None, ALU.add)
            L.stt(r, n, -LN2H, r, ALU.mult, ALU.add)
            L.stt(r, n, -LN2L, r, ALU.mult, ALU.add)
            f = [1.0]
            for k in range(1, 9):
                f.append(f[-1] / k)
            L.ts(out, r, f[8], f[7], ALU.mult, ALU.add)
            for k in range(6, -1, -1):
                L.tt(out, out, r, ALU.mult)
                L.ts(out, out, f[k], None, ALU.add)
            L.ts(ii, n, 127.0, float(2 ** 23), ALU.add, ALU.mult)
            L.tt(out, out, ii.bitcast(F32), ALU.mult)

        TP1 = 6.28125
        TP2 = float(np.float32(np.floor((2 * np.pi - TP1) * 2.0 ** 21) / 2.0 ** 21))
        TP3 = float(np.float32(2 * np.pi - TP1 - TP2))

        def v_sincos(L, sn, cs, x, n, r, r2):
            L.ts(n, x, float(1 / (2 * np.pi)), MAGIC, ALU.mult, ALU.add)
            L.ts(n, n, -MAGIC, None, ALU.add)
            L.stt(r, n, -TP1, x, ALU.mult, ALU.add)
            L.stt(r, n, -TP2, r, ALU.mult, ALU.add)
            L.stt(r, n, -TP3, r, ALU.mult, ALU.add)
            L.ts(r, r, 0.5, None, ALU.mult)
            L.tt(r2, r, r, ALU.mult)
            fac = [1.0]
            for k in range(1, 18):
                fac.append(fac[-1] * k)
            sc = [(-1) ** k / fac[2 * k + 1] for k in range(8)]
            cc = [(-1) ** k / fac[2 * k] for k in range(9)]
            for out, c in ((sn, sc), (cs, cc)):
                L.ts(out, r2, c[-1], None, ALU.mult)
                for k in range(len(c) - 2, 0, -1):
                    L.stt(out, out, c[k], r2, ALU.add, ALU.mult)
                L.ts(out, out, c[0], None, ALU.add)
            L.tt(sn, sn, r, ALU.mult)
            L.tt(cs, cs, sn, ALU.mult)
            L.tt(r2, sn, sn, ALU.mult)
            L.ts(sn, cs, 2.0, None, ALU.mult)
            L.ts(cs, r2, -2.0, 1.0, ALU.mult, ALU.add)

        def v_params_early(L):
            L.need("ld_par", 16 * N_PAR)
            L.cp(lrow[0:GP, 2, :].rearrange("g (r p) -> g r p", r=2),
                 lstep[0:GP, :].unsqueeze(2).to_broadcast([GP, 2, GS]), dep=False)
            L.cp(grep[0:G], drow[0:G, GC:].unsqueeze(1).to_broadcast([G, CH, GC]), "par_rows", dep=False)

        def v_params(L):
            b = full(L, ("par", 0))
            free(L, ("par", 0), nc.vector.tensor_copy(gcol[:, 0:79], b[:, 0:79]))
            b = full(L, ("par", 1))
            lr, li, st, th, mg, sn, cs, t1, t2, t3, fr, fi = [prm[:, i] for i in range(12)]
            L.cp(lr, b[:, 0:GP], dep=False)
            L.cp(li, b[:, GP:2 * GP], dep=False)
            L.cp(st, b[:, 2 * GP:3 * GP], dep=False)
            L.cp(gainU, b[:, 96:160], dep=False)
            free(L, ("par", 1), nc.vector.tensor_copy(Dd[0:GC], b[0:GC, 160:224]))
            b = full(L, ("par", 2))
            for i in range(2):
                L.did(nc.vector.tensor_copy(h0[:, i].rearrange("p g b -> p b g"),
                                            b[:, 256 * i:256 * i + 256].rearrange("p (b g) -> p b g", b=DB)))
            free(L, ("par", 2), nc.vector.memset(tA[:, 0:1], 0.0))
            for i in range(2):
                b = full(L, ("cT", i))
                free(L, ("cT", i), nc.vector.tensor_copy(Ct[:, i].rearrange("p g c -> p (g c)"), b[:, :]))
            v_exp(L, st, st, t1, t2, t3.bitcast(I32))
            L.tt(th, li, st, ALU.mult)
            L.tt(t3, lr, st, ALU.mult)
            v_exp(L, mg, t3, t1, t2, fr.bitcast(I32))
            v_sincos(L, sn, cs, th, t1, t2, t3)
            L.settle()
            L.did(nc.vector.memset(apw[:, 0, 0], 1.0))
            L.did(nc.vector.memset(apw[:, 1, 0], 0.0))
            L.tt(apw[:, 0, 1], mg, cs, ALU.mult)
            L.tt(apw[:, 1, 1], mg, sn, ALU.mult)
            for k in (1, 2, 4):
                w = tA[:, 0:k * GP].rearrange("p (t g) -> p t g", t=k)
                w2 = tB[:, 0:k * GP].rearrange("p (t g) -> p t g", t=k)
                L.cmul(apw[:, 0, k + 1:2 * k + 1], apw[:, 1, k + 1:2 * k + 1],
                       apw[:, 0, 1:k + 1], apw[:, 1, 1:k + 1],
                       apw[:, 0, k].unsqueeze(1).to_broadcast([P, k, GP]),
                       apw[:, 1, k].unsqueeze(1).to_broadcast([P, k, GP]), w, w2)
            for s in range(8):
                L.cp(arev[:, 0, s], apw[:, 0, 7 - s], dep=(s == 0))
                L.cp(arev[:, 1, s], apw[:, 1, 7 - s], dep=False)
            L.tt(t1, lr, lr, ALU.mult)
            L.tt(t2, li, li, ALU.mult)
            L.tt(t1, t1, t2, ALU.add)
            L.recip(t3, t1)
            L.ts(t1, apw[:, 0, 1], -1.0, None, ALU.add)
            L.tt(fr, t1, lr, ALU.mult)
            L.tt(t2, apw[:, 1, 1], li, ALU.mult)
            L.tt(fr, fr, t2, ALU.add)
            L.tt(fr, fr, t3, ALU.mult)
            L.tt(fi, apw[:, 1, 1], lr, ALU.mult)
            L.tt(t2, t1, li, ALU.mult)
            L.tt(fi, fi, t2, ALU.subtract)
            L.tt(fi, fi, t3, ALU.mult)
            frb = fr.unsqueeze(2).to_broadcast([P, GP, GC])
            fib = fi.unsqueeze(2).to_broadcast([P, GP, GC])
            w = tA[:, 0:512].rearrange("p (g c) -> p g c", g=GP)
            w2 = tB[:, 0:512].rearrange("p (g c) -> p g c", g=GP)
            L.cmul(Bb[:, 0], Bb[:, 1], braw[:, 0], braw[:, 1], frb, fib, w, w2)
            L.settle()
            L.did(nc.vector.memset(tA[:, 0:1], 0.0), "bbar_ready")
            for _ in range(3):
                L.tt(mg, mg, mg, ALU.mult)

            def square():
                L.tt(t1, cs, cs, ALU.mult)
                L.tt(t2, sn, sn, ALU.mult)
                L.tt(t3, cs, sn, ALU.mult)
                L.tt(cs, t1, t2, ALU.subtract)
                L.ts(sn, t3, 2.0, None, ALU.mult)
            for _ in range(3):
                square()
            L.settle()
            L.did(nc.vector.memset(Rr[:, :, 0:1], 1.0))
            L.did(nc.vector.memset(Ri[:, :, 0:1], 0.0))
            for j in range(6):
                k = 1 << j
                w = tA[:, 0:k * GP].rearrange("p (g n) -> p g n", g=GP)
                w2 = tB[:, 0:k * GP].rearrange("p (g n) -> p g n", g=GP)
                L.cmul(Rr[:, :, k:2 * k], Ri[:, :, k:2 * k], Rr[:, :, 0:k], Ri[:, :, 0:k],
                       cs.unsqueeze(2).to_broadcast([P, GP, k]), sn.unsqueeze(2).to_broadcast([P, GP, k]), w, w2)
                if j < 5:
                    square()

        def pool_qb(L, k):
            gs = slice(BG * k, BG * k + BG)
            if k == 0:
                L.need("bbar_ready", 1)
            else:
                landed(L.e, ("Q", k - 1, 3))
            g = nc.gpsimd
            t = pt[:].rearrange("p (g s c) -> p g s c", g=4, s=CH)
            for q in range(2):
                g4 = slice(4 * q, 4 * q + 4)
                G4 = slice(BG * k + 4 * q, BG * k + 4 * q + 4)
                B = [Bb[:, i, G4].unsqueeze(2).to_broadcast([P, 4, CH, GC]) for i in range(2)]
                R = [arev[:, i, :, G4].rearrange("p t g -> p g t").unsqueeze(3).to_broadcast([P, 4, CH, GC])
                     for i in range(2)]
                L.settle()
                L.did(g.tensor_tensor(QBr[:, g4], R[0], B[0], ALU.mult))
                L.settle()
                L.did(g.tensor_tensor(t, R[1], B[1], ALU.mult))
                L.settle()
                L.did(g.tensor_tensor(QBr[:, g4], QBr[:, g4], t, ALU.subtract))
                L.settle()
                L.did(g.tensor_tensor(QBi[:, g4], R[0], B[1], ALU.mult))
                L.settle()
                L.did(g.tensor_tensor(t, R[1], B[0], ALU.mult))
                L.settle()
                L.did(g.tensor_tensor(QBi[:, g4], QBi[:, g4], t, ALU.add), "qb_ready" if q else None)

        pt = sb("pt", 512)

        def v_ca(L, k):
            gs = slice(BG * k, BG * k + BG)
            C = [Ct[:, i, gs].unsqueeze(2).to_broadcast([P, BG, 9, GC]) for i in range(2)]
            R = [apw[:, i, :, gs].rearrange("p t g -> p g t").unsqueeze(3).to_broadcast([P, BG, 9, GC])
                 for i in range(2)]
            if k > 0:
                landed(L.e, ("Y", k - 1, 3))
            for t0, t1 in ((0, 5), (5, 9)):
                n = t1 - t0
                w = tA[:, 0:BG * n * GC].rearrange("p (g t c) -> p g t c", g=BG, t=n)
                c0, c1, a0, a1 = [x[:, :, t0:t1] for x in (C[0], C[1], R[0], R[1])]
                o0, o1 = CAr[:, :, t0:t1], CAi[:, :, t0:t1]
                L.tt(o0, c0, a0, ALU.mult, dep=(t0 == 0))
                L.tt(w, c1, a1, ALU.mult)
                L.tt(o0, o0, w, ALU.subtract)
                L.tt(o1, c0, a1, ALU.mult, dep=False)
                L.tt(w, c1, a0, ALU.mult)
                L.settle()
                L.did(nc.vector.scalar_tensor_tensor(out=o1.rearrange("p g t c -> p g (t c)"),
                                                     in0=o1.rearrange("p g t c -> p g (t c)"), scalar=-1.0,
                                                     in1=w.rearrange("p g t c -> p g (t c)"),
                                                     op0=ALU.mult, op1=ALU.subtract),
                      "ca_ready" if t1 == 9 else None)

        def v_stats8(L):
            L.need("ss8_ready", 1)
            L.settle()
            L.did(nc.vector.tensor_reduce(r8[0:NCC], ss8[0:NCC].rearrange("p k s -> p s k"), AX, ALU.add))
            L.ts(r8[0:NCC], r8[0:NCC], 1.0 / D, EPS, ALU.mult, ALU.add, sem="r8_ms")

        def v_norm8(L, k):
            if k == 0:
                L.need("r8_sqrt", 1)
                L.recip(r8[0:NCC], r8[0:NCC])
                landed(L.e, ("xsT", 1))
            else:
                landed(L.e, ("yT", k - 1, 1, 1))
            x8_ready(L.e, 1, k)
            L.settle()
            for s in range(CH):
                ins = nc.vector.tensor_scalar(ub[0:NCC, :, s, :],
                                              x8[0:NCC, s, :].rearrange("p (g c) -> p g c", g=16),
                                              r8[0:NCC, s:s + 1], None, ALU.mult)
                L.did(ins, "x8_used" if s == CH - 1 else None)

        def v_batch(L, k):
            gs = slice(BG * k, BG * k + BG)
            for i in range(4):
                b = full(L, ("U", k, i))
                g0 = 16 * k + 4 * i
                free(L, ("U", k, i), nc.vector.tensor_tensor(
                    Ub[:, 4 * i:4 * i + 4, :], b[:, 0:4 * NCC].rearrange("p (g n) -> p g n", g=4),
                    gainU[:, g0:g0 + 4].unsqueeze(2).to_broadcast([P, 4, NCC]), ALU.mult))
            if k == 0:
                L.need("consts_ready", 1)
            L.settle()
            L.did(nc.vector.memset(Kp[0:GC, :, 0:7 * GC], 0.0))
            for i in range(4):
                b = full(L, ("K", k, i))
                if i % 2 == 0 and (k > 0 or i > 0):
                    L.need("toep", 16 * CH * (2 * k + i // 2))
                o4 = Kp[0:GC, i % 2::2]
                L.did(nc.vector.tensor_copy(o4[:, :, 8 * GC:], b[0:GC, :].rearrange("p (g n) -> p g n", g=4)[:, :, GC:]))
                w = tB[0:GC, 0:64].rearrange("p (g c) -> p g c", g=4)
                g0 = 16 * k + 8 * (i // 2) + i % 2
                L.tt(w, ident[0:GC, 0:GC].unsqueeze(1).to_broadcast([GC, 4, GC]),
                     Dd[0:GC, g0:g0 + 7:2].unsqueeze(2).to_broadcast([GC, 4, GC]), ALU.mult)
                L.settle()
                free(L, ("K", k, i), nc.vector.tensor_tensor(
                    o4[:, :, 7 * GC:8 * GC], b[0:GC, :].rearrange("p (g n) -> p g n", g=4)[:, :, 0:GC], w, ALU.add))
            L.need("toep", 16 * CH * 2 * (k + 1))
            for i in range(4):
                b = full(L, ("Q", k, i))
                free(L, ("Q", k, i), nc.vector.tensor_copy(
                    Qt[:, i // 2, 4 * (i % 2):4 * (i % 2) + 4].rearrange("p g n -> p (g n)"), b[:, :]))
            L.cp(D0, prm[:, 4, gs].unsqueeze(2).to_broadcast([P, BG, NC]))
            L.settle()
            L.did(nc.vector.memset(D0[:, :, 0:1], 0.0))
            W = [full(L, ("W", k, i))[:, 0:4 * NCC].rearrange("p (g n) -> p g n", g=4) for i in range(4)]
            fr_, fi_ = tA[:, 0:512].rearrange("p (g n) -> p g n", g=BG), tA[:, 512:].rearrange("p (g n) -> p g n", g=BG)
            w_, w2_ = tB[:, 0:512].rearrange("p (g n) -> p g n", g=BG), tB[:, 512:].rearrange("p (g n) -> p g n", g=BG)
            for q in range(2):
                wr, wi = W[2 * q], W[2 * q + 1]
                g4 = slice(4 * q, 4 * q + 4)
                G4 = slice(BG * k + 4 * q, BG * k + 4 * q + 4)
                L.tt(fr_[:, g4], wr[:, :, 0:NC], Rr[:, G4], ALU.mult)
                L.tt(w_[:, g4], wi[:, :, 0:NC], Ri[:, G4], ALU.mult)
                L.tt(fi_[:, g4], wi[:, :, 0:NC], Rr[:, G4], ALU.mult)
                L.tt(w2_[:, g4], wr[:, :, 0:NC], Ri[:, G4], ALU.mult)
                free(L, ("W", k, 2 * q), nc.vector.tensor_copy(ws[:, 0, G4], wr[:, :, NC:]))
                free(L, ("W", k, 2 * q + 1), nc.vector.tensor_copy(ws[:, 1, G4], wi[:, :, NC:]))
            L.tt(fr_, fr_, w_, ALU.add)
            L.tt(fi_, fi_, w2_, ALU.subtract)
            D0f = D0.rearrange("p g n -> p (g n)")
            L.settle()
            L.did(nc.vector.tensor_tensor_scan(tB[:, 0:512], D0f, tA[:, 0:512], 0.0, ALU.mult, ALU.add))
            L.did(nc.vector.tensor_tensor_scan(tB[:, 512:], D0f, tA[:, 512:], 0.0, ALU.mult, ALU.add))
            L.tt(fr_, w_, Rr[:, gs], ALU.mult)
            L.tt(fi_, w2_, Ri[:, gs], ALU.mult)
            L.tt(Sr[:, :, 1:], fr_, fi_, ALU.subtract)
            L.tt(fr_, w_, Ri[:, gs], ALU.mult)
            L.tt(fi_, w2_, Rr[:, gs], ALU.mult)
            L.tt(Si[:, :, 1:], fr_, fi_, ALU.add, sem="states_ready")
            L.cp(fst[:, 0, gs], Sr[:, :, NC:].squeeze(2) if False else Sr[:, :, NC])
            L.cp(fst[:, 1, gs], Si[:, :, NC])

        def a_batch(L, k):
            s = nc.scalar
            for i in range(4):
                b = full(L, ("Y", k, i))
                free(L, ("Y", k, i), s.activation(
                    yb[0:NCC, :, P * (i // 2):P * (i // 2) + P].rearrange("p s (g r c) -> p g s r c", g=4,
                                                                          r=2)[:, :, :, i % 2],
                    b[0:NCC, :].rearrange("p (g s c) -> p g s c", g=4, s=CH), ACT.Gelu_apprx_tanh))
            for f in range(2):
                for q in range(2):
                    b = full(L, ("yT", k, f, q))
                    v4 = b[:, 0:4 * NCC].rearrange("p (s n) -> p s n", s=4)
                    ft = 2 * k + f
                    ins = s.activation(hT[:, ft, 0:SEQ].rearrange("p (c s) -> p s c", s=CH)[:, 4 * q:4 * q + 4],
                                       v4[:, :, 0:NC], ACT.Copy)
                    if q == 0:
                        free(L, ("yT", k, f, q), ins)
                    else:
                        L.did(ins)
                        free(L, ("yT", k, f, q), s.activation(
                            hT[:, ft, SEQ:].rearrange("p (b s) -> p s b", s=DS), v4[:, :, NC:], ACT.Copy))

        yb = ub.rearrange("p g s c -> p (g s c)").rearrange("p (s n) -> p s n", s=CH)

        def a_stats(L):
            s = nc.scalar
            L.need("ld_mem", 16)
            for c in range(8):
                L.settle()
                L.did(s.activation(scr[:], mnat[:, c // 4, 256 * (c % 4):256 * (c % 4) + 256], ACT.Square,
                                   accum_out=mss[:, c:c + 1]))
            L.settle()
            L.did(s.activation(scr[0:1, 0:1], epst[0:1], ACT.Copy), "mss_ready")
            for k in range(NB):
                x8_ready(L.e, 0, k)
                for i in range(CH):
                    L.settle()
                    L.did(s.activation(scr[0:NCC, 0:256], x8[0:NCC, i], ACT.Square,
                                       accum_out=ss8[0:NCC, k, i:i + 1]),
                          ("x8_sq" if i == CH - 1 else None))
            L.settle()
            L.did(s.activation(scr[0:1, 0:1], epst[0:1], ACT.Copy), "ss8_ready")
            L.need("mss_ms", 1)
            L.did(s.activation(mss[:, 8:10], mss[:, 8:10], ACT.Sqrt), "mss_sqrt")
            L.need("r8_ms", 1)
            L.did(s.activation(r8[0:NCC], r8[0:NCC], ACT.Sqrt), "r8_sqrt")

        scr = sb("scr", 256)

        def pe_setup(pe):
            t = nc.tensor
            pe.wait_ge(S("ident_ready"), 1)
            pe.wait_ge(S("par_rows"), 1)
            pe.wait_ge(S("ld_par"), 16 * N_PAR)
            b = fill(pe, ("par", 0))
            filled(("par", 0), t.transpose(b[:, 0:79], prow[0:79, :], ident[0:79, 0:79]))
            b = fill(pe, ("par", 1))
            for i in range(3):
                t.transpose(b[:, GP * i:GP * i + GP], lrow[0:GP, i, :], ident[0:GP, 0:GP])
            t.transpose(b[:, 96:160], grep[0:G].rearrange("p s c -> p (s c)"), ident[0:G, 0:G])
            filled(("par", 1), t.transpose(b[0:GC, 160:224], drow[0:G, 0:GC], ident[0:G, 0:G]))
            b = fill(pe, ("par", 2))
            for i in range(4):
                ins = t.transpose(b[:, P * i:P * i + P], hraw[:, i, :], ident[:])
            filled(("par", 2), ins)
            for i in range(2):
                b = fill(pe, ("cT", i))
                for q in range(4):
                    ins = t.transpose(b[:, P * q:P * q + P], craw[:, i, q, :], ident[:])
                filled(("cT", i), ins)
            pe.wait_ge(S("ld_x"), 32)
            for f in range(KT):
                b = fill(pe, ("xT", f))
                for q in range(4):
                    ins = t.transpose(b[:, P * q:P * q + P], xnat[:, q, P * f:P * f + P], ident[:])
                filled(("xT", f), ins)
            for f2 in range(2):
                b = fill(pe, ("xsT", f2))
                for f in range(4):
                    ins = t.transpose(b[:, NS * f:NS * f + NS], xsn[0:NS, P * (4 * f2 + f):P * (4 * f2 + f) + P],
                                      ident[0:NS, 0:NS])
                filled(("xsT", f2), ins)

        def a_xT(L):
            for f in range(KT):
                b = full(L, ("xT", f))
                free(L, ("xT", f), nc.scalar.activation(xT[:, f, 0:SEQ], b[:, :], ACT.Copy))
            for q in range(2):
                b = full(L, ("xsT", q))
                free(L, ("xsT", q), nc.scalar.activation(xT[:, 4 * q:4 * q + 4, SEQ:],
                                                         b[:, 0:4 * NS].rearrange("p (f n) -> p f n", f=4), ACT.Copy))

        def pe_batch(pe, k):
            t = nc.tensor
            pe.wait_ge(S("x8_used"), k + 1)
            for i in range(4):
                b = fill(pe, ("U", k, i))
                for g in range(4):
                    ins = t.transpose(b[:, NCC * g:NCC * g + NCC],
                                      ub[0:NCC, 4 * i + g].rearrange("p s c -> p (s c)"), ident[0:NCC, 0:NCC])
                filled(("U", k, i), ins)
            pe.wait_ge(S("ca_ready"), k + 1)
            pe.wait_ge(S("bbar_ready"), 1)
            for i in range(4):
                b = fill(pe, ("K", k, i))
                for g in range(4):
                    gp, r = 4 * (i // 2) + g, i % 2
                    q = slice(64 * r, 64 * r + 64)
                    for j, ca in enumerate((CAr, CAi)):
                        ins = t.matmul(b[0:GC, P * g:P * g + P], Bb[q, j, BG * k + gp, :],
                                       ca[q, gp, 0:CH].rearrange("p t c -> p (t c)"), start=(j == 0), stop=(j == 1))
                filled(("K", k, i), ins)
            pe.wait_ge(S("qb_ready"), k + 1)
            for i in range(4):
                b = fill(pe, ("Q", k, i))
                for g in range(4):
                    ins = t.transpose(b[:, P * g:P * g + P],
                                      (QBr, QBi)[i // 2][:, 4 * (i % 2) + g].rearrange("p s c -> p (s c)"), ident[:])
                filled(("Q", k, i), ins)
            for i in range(4):
                landed(pe, ("Q", k, i))
                landed(pe, ("U", k, i))
            for i in range(4):
                b = fill(pe, ("W", k, i))
                for g in range(4):
                    gp = 4 * (i // 2) + g
                    for r in range(2):
                        ins = t.matmul(b[64 * r:64 * r + 64, NCC * g:NCC * g + NCC],
                                       Qt[:, i % 2, gp, 64 * r:64 * r + 64], Ub[:, 2 * gp + r, :],
                                       start=True, stop=True)
                filled(("W", k, i), ins)
            pe.wait_ge(S("toep"), 16 * CH * 2 * (k + 1))
            if k == 0:
                landed(pe, ("par", 2))
            pe.wait_ge(S("states_ready"), k + 1)
            for i in range(4):
                b = fill(pe, ("Y", k, i))
                for g in range(4):
                    gp, r = 4 * (i // 2) + g, i % 2
                    n = 2 * gp + r
                    q = slice(64 * r, 64 * r + 64)
                    t.matmul(b[0:NCC, P * g:P * g + P], Ub[:, n, :], Tt[:, n, :], start=True, stop=False,
                             skip_group_check=True)
                    for j, (s_, ca) in enumerate(((Sr, CAr), (Si, CAi))):
                        t.matmul(b[0:NC, P * g:P * g + P], s_[q, gp, 0:NC],
                                 ca[q, gp, 1:9].rearrange("p t c -> p (t c)"), start=False, stop=False,
                                 skip_group_check=True)
                        ins = t.matmul(b[NC:NCC, P * g + 64:P * g + P], h0[q, j, BG * k + gp, :],
                                       ca[q, gp, 1:5].rearrange("p t c -> p (t c)"), start=False, stop=(j == 1),
                                       skip_group_check=True)
                filled(("Y", k, i), ins)
            for i in range(4):
                landed(pe, ("Y", k, i))
            for f in range(2):
                for q in range(2):
                    b = fill(pe, ("yT", k, f, q))
                    for s in range(4):
                        ins = t.transpose(b[:, NCC * s:NCC * s + NCC],
                                          yb[0:NCC, 4 * q + s, P * f:P * f + P], ident[0:NCC, 0:NCC])
                    filled(("yT", k, f, q), ins)

        def v_final(L):
            m, w, w2 = [x.rearrange("p (g b) -> p g b", g=GP) for x in (tA[:, 0:256], tA[:, 256:512], tA[:, 512:768])]
            a4 = [apw[:, i, 4].unsqueeze(2).to_broadcast([P, GP, DB]) for i in range(2)]
            L.cmul(m, w2, h0[:, 0], h0[:, 1], a4[0], a4[1], w, tB[:, 0:256].rearrange("p (g b) -> p g b", g=GP))
            L.tt(ws[:, 0], ws[:, 0], m, ALU.add)
            L.tt(ws[:, 1], ws[:, 1], w2, ALU.add)
            L.cp(tB[:, 0:256].rearrange("p (b g) -> p g b", b=DB), ws[:, 0])
            L.cp(tB[:, 256:512].rearrange("p (b g) -> p g b", b=DB), ws[:, 1], sem="fin_ready")
            b = full(L, ("fin", 0))
            free(L, ("fin", 0), nc.vector.tensor_copy(tA[0:GP, 0:2 * P], b[0:GP, 0:2 * P]))
            b = full(L, ("fin", 1))
            free(L, ("fin", 1), nc.vector.tensor_copy(tA[:, 2 * P:6 * P], b[:, :]))

        def pe_final(pe):
            t = nc.tensor
            pe.wait_ge(S("fin_ready"), 1)
            b = fill(pe, ("fin", 0))
            for i in range(2):
                ins = t.transpose(b[0:GP, P * i:P * i + P], fst[:, i], ident[:])
            filled(("fin", 0), ins)
            b = fill(pe, ("fin", 1))
            for i in range(4):
                ins = t.transpose(b[:, P * i:P * i + P], tB[:, P * i:P * i + P], ident[:])
            filled(("fin", 1), ins)

        def sp_final(sp):
            q = S("out")
            landed(sp, ("fin", 0))
            for i in range(2):
                sp.dma_start(o[2 + i][0, 0].rearrange("(g r) p -> g (r p)", r=2), tA[0:GP, P * i:P * i + P]) \
                  .then_inc(q, 16)
            landed(sp, ("fin", 1))
            for i in range(2):
                v = o[12 + i][0].rearrange("b (g r) p -> (b g) (r p)", r=2)
                for t in range(2):
                    sp.dma_start(v[P * t:P * t + P], tA[:, P * (2 + 2 * i + t):P * (3 + 2 * i + t)]).then_inc(q, 16)
            n_out[0] += 6

        n_out = [0]
        sq = arena[:, 0:KT * T].rearrange("p (k t) -> p k t", k=KT)
        memT1 = arena[:, 4352:4352 + KT * NM].rearrange("p (f m) -> p f m", f=KT)
        kk = sb("kk", 1024)
        kraw = kk[:, 0:512].rearrange("p (c n) -> p c n", c=2)
        kout = kk[:, 512:1024].rearrange("p (c n) -> p c n", c=2)
        st = sb("st", 64)

        def mT(l):
            return (memT, memT1)[l]

        def v_mem_norm(L):
            L.need("mss_ready", 1)
            L.did(nc.vector.tensor_reduce(mss[:, 8:10], mss[:, 0:8].rearrange("p (c k) -> p c k", c=2), AX, ALU.add))
            L.ts(mss[:, 8:10], mss[:, 8:10], 1.0 / D, EPS, ALU.mult, ALU.add, sem="mss_ms")
            L.need("mss_sqrt", 1)
            L.recip(mss[:, 8:10], mss[:, 8:10])
            L.settle()
            for c in range(2):
                L.did(nc.vector.tensor_scalar(mnat[:, c], mnat[:, c], mss[:, 8 + c:9 + c], None, ALU.mult),
                      "mnat_ready" if c else None)

        def pe_memkv(pe, l):
            t = nc.tensor
            pe.wait_ge(S("mnat_ready"), 1)
            for f2 in range(KT // 2):
                b = fill(pe, ("memT", l, f2))
                for q in range(4):
                    f, c = 2 * f2 + q // 2, q % 2
                    ins = t.transpose(b[:, P * q:P * q + P], mnat[:, c, P * f:P * f + P], ident[:])
                filled(("memT", l, f2), ins)
            for f2 in range(KT // 2):
                landed(pe, ("memT", l, f2))
            for j in range(8):
                b = fill(pe, ("kv", l, j))
                uready(pe, ("kv", l, j))
                w = uslot(("kv", l, j), KT)
                for c in range(2):
                    for k in range(KT):
                        ins = t.matmul(b[:, 256 * c:256 * c + 256], mT(l)[:, k, P * c:P * c + P], w[:, k, :],
                                       start=(k == 0), stop=(k == KT - 1))
                filled(("kv", l, j), ins)
                if 1 <= j <= 4:
                    pe.wait_ge(S("mk_ready"), 4 * l + j)
                    b = fill(pe, ("mkT", l, j - 1))
                    for q in range(4):
                        ins = t.transpose(b[:, P * q:P * q + P], kout[:, q % 2, P * (q // 2):P * (q // 2) + P], ident[:])
                    filled(("mkT", l, j - 1), ins)

        def a_memkv(L, l):
            s = nc.scalar
            if l == 0:
                landed(L.e, ("par", 0))
            for f2 in range(KT // 2):
                b = full(L, ("memT", l, f2))
                L.did(s.activation(mT(l)[:, 2 * f2], b[:, 0:256], ACT.Copy, scale=g_memin(l, 2 * f2)))
                free(L, ("memT", l, f2), s.activation(mT(l)[:, 2 * f2 + 1], b[:, 256:512], ACT.Copy,
                                                      scale=g_memin(l, 2 * f2 + 1)))
            for j in range(8):
                b = full(L, ("kv", l, j))
                if j < 4:
                    if 4 * l + j > 0:
                        L.need("mk_ready", 4 * l + j)
                    free(L, ("kv", l, j), s.activation(kraw.rearrange("p c n -> p (c n)"), b[:, :], ACT.Copy))
                    L.settle()
                    for c in range(2):
                        L.settle()
                        L.did(s.activation(scr[:], kraw[:, c], ACT.Square, accum_out=st[:, c:c + 1]))
                    L.settle()
                    L.did(s.activation(st[:, 2:4], st[:, 0:2], ACT.Sqrt, bias=epst[:], scale=1.0 / MD), "mk_sqrt")
                else:
                    jj = j - 4
                    free(L, ("kv", l, j), s.activation(
                        mV[:, l, :, 256 * jj:256 * jj + 256], b[:, :].rearrange("p (c n) -> p c n", c=2), ACT.Copy))

        def v_memkv(L, l):
            v = nc.vector
            for j in range(4):
                L.need("mk_sqrt", 4 * l + j + 1)
                L.did(v.reciprocal(st[:, 4:6], st[:, 2:4]))
                if j + l > 0:
                    L.need("mk_out", 16 * (4 * l + j))
                    n = items[("mkT", l, j - 1) if j else ("mkT", 0, 3)]
                if l == 0 and j == 0:
                    L.need("ld_bc", 32)
                L.settle()
                for c in range(2):
                    L.did(v.scalar_tensor_tensor(out=kout[:, c], in0=kraw[:, c], scalar=st[:, 4 + c:5 + c],
                                                 in1=mkg[:, MD * l:MD * l + MD], op0=ALU.mult, op1=ALU.mult),
                          "mk_ready" if c else None)
                b = full(L, ("mkT", l, j))
                free(L, ("mkT", l, j), v.tensor_copy(mKT[:, l, 2 * j:2 * j + 2].rearrange("p f m -> p (f m)"), b[:, :]))

        def sp_memout(sp, l):
            for j in range(4):
                sp.wait_ge(S("mk_ready"), 4 * l + j + 1)
                sp.dma_start(o[10][l, 0].rearrange("(c p) h n -> p c h n", p=P)[:, :, j], kout).then_inc(S("mk_out"), 16)
            for j in range(4, 8):
                landed(sp, ("kv", l, j))
            sp.dma_start(o[11][l, 0].rearrange("(c p) h n -> p c (h n)", p=P), mV[:, l]).then_inc(S("out"), 16)
            n_out[0] += 1

        def load_resid(sp, w, name, nu, kt):
            for j in range(4):
                for s in range(nu):
                    load_unit(sp, w, (name, j, s), kt, slice(P * kt * s, P * kt * (s + 1)), cols(j))

        def pe_resid(pe, name, nu, kt, src):
            t = nc.tensor
            for j in range(4):
                b = [None] * 4
                for s in range(nu):
                    uready(pe, (name, j, s))
                    w = uslot((name, j, s), kt)
                    for m in range(2):
                        for h in range(2):
                            key = (name, 2 * j + m, h)
                            if s == 0:
                                b[2 * m + h] = fill(pe, key)
                            for k in range(kt):
                                ins = t.matmul(b[2 * m + h][:, 0:HT], w[:, k, P * m:P * m + P],
                                               src[:, kt * s + k, half(h)],
                                               start=(s == 0 and k == 0), stop=(s == nu - 1 and k == kt - 1))
                            if s == nu - 1:
                                filled(key, ins)
                    if s < nu - 1:
                        ins.then_inc(S("w_half"), 1)

        def v_resid(L, name):
            for m in range(KT):
                for h in range(2):
                    b = full(L, (name, m, h))
                    free(L, (name, m, h), nc.vector.tensor_tensor(xT[:, m, half(h)], xT[:, m, half(h)], b[:, 0:HT],
                                                                  ALU.add))

        def a_squares(L, name, k):
            for m in range(KT):
                if name == "glu":
                    L.need("x_glu", 2 * m + 2)
                else:
                    landed(L.e, (name, m, 0))
                    landed(L.e, (name, m, 1))
                L.did(nc.scalar.activation(sq[:, m], xT[:, m], ACT.Square), "sq_ready")

        def pe_norm(pe, k):
            t = nc.tensor
            for h in range(2):
                b = fill(pe, ("ssq", k, h))
                for m in range(KT):
                    if h == 0:
                        pe.wait_ge(S("sq_ready"), KT * k + m + 1)
                    ins = t.matmul(b[:, 0:HT], ones[:], sq[:, m, half(h)], start=(m == 0), stop=(m == KT - 1))
                filled(("ssq", k, h), ins)

        def a_norm(L, k):
            for h in range(2):
                b = full(L, ("ssq", k, h))
                free(L, ("ssq", k, h), nc.scalar.activation(rstd[:, half(h)], b[:, 0:HT], ACT.Sqrt, bias=epst[:],
                                                            scale=1.0 / D))

        def v_norm(L, k, gain):
            landed(L.e, ("ssq", k, 0))
            landed(L.e, ("ssq", k, 1))
            L.did(nc.vector.reciprocal(rstd[:], rstd[:]))
            L.settle()
            for m in range(KT):
                L.did(nc.vector.scalar_tensor_tensor(out=hT[:, m], in0=xT[:, m], scalar=gain(m), in1=rstd[:],
                                                     op0=ALU.mult, op1=ALU.mult), "h_ready")

        def a_glu(L):
            for m in range(KT):
                for h in range(2):
                    b = full(L, ("glu", m, h))
                    n = 2 * m + h
                    if n >= 2:
                        L.need("x_glu", n - 1)
                    free(L, ("glu", m, h), nc.scalar.activation(sgb[:, h, 0:HT], b[:, 0:HT], ACT.Sigmoid, bias=b_glu(m)))

        sgb = kk[:, 0:0] if False else arena[:, 24592:24592 + 2 * T].rearrange("p (i t) -> p i t", i=2)

        def v_glu(L):
            for m in range(KT):
                for h in range(2):
                    landed(L.e, ("glu", m, h))
                    L.tt(sgb[:, h, 0:HT], sgb[:, h, 0:HT], hT[:, m, half(h)], ALU.mult, dep=False)
                    L.tt(xT[:, m, half(h)], xT[:, m, half(h)], sgb[:, h, 0:HT], ALU.add, sem="x_glu")

        act = arena[:, 4352:4352 + FT * T].rearrange("p (k t) -> p k t", k=FT)

        def iv(eng, sem, base, i):
            eng.wait_ge(S(sem), i + base)

        def sp_ffn(sp, l):
            wv = a["ffn_w_in"][l].rearrange("(k p) (h n) -> p k h n", p=P, h=2)

            def put(u, n, i=None):
                lo = u * P if i is None else (2 * i + u) * P
                src = wv[:, :, :, lo:lo + P] if i is None else wv[:, :, :, bass.ts(2 * i + u, P)]
                for h in range(2):
                    sp.dma_start(ring[:, (n % 2) * UW:(n % 2) * UW + KT * RUNIT].rearrange(
                        "p (k h c) -> p k h c", k=KT, h=2)[:, :, h], src[:, :, h]).then_inc(S(f"w_full{n % 2}"), 8 * 2)
            for u in range(2):
                n = units[("fi", l, u)]
                sp.wait_ge(S(unit_end[n - 2][0]), unit_end[n - 2][1])
                put(u, n)
            with sp.Fori(1, FT // 2) as i:
                for u in range(2):
                    n = units[("fi", l, u)]
                    sem, v = unit_end[n]
                    sp.wait_ge(S(sem), i + (v - 1))
                    put(u, n, i)
            load_resid(sp, a["ffn_w_out"][l], f"fo{l}", 2, 11)

        def pe_ffn(pe, l):
            t = nc.tensor
            pe.wait_ge(S("h_ready"), KT * (2 * l + 2 if l == 0 else 5))
            with pe.Fori(0, FT // 2) as i:
                for u in range(2):
                    n = units[("fi", l, u)]
                    pe.wait_ge(S(f"w_full{n % 2}"), 32 * i + wcount(n))
                    w = uslot(("fi", l, u), KT)
                    for j in range(4):
                        key = ("fi", l, u, j)
                        m = items[key]
                        pe.wait_ge(S(f"bank_free{m % 8}"), i + m // 8)
                        b = ps[:, m % 8, :]
                        for k in range(KT):
                            ins = t.matmul(b[:, 0:HT], w[:, k, P * (j // 2):P * (j // 2) + P], hT[:, k, half(j % 2)],
                                           start=(k == 0), stop=(k == KT - 1))
                        ins.then_inc(S(f"bank_full{m % 8}"), 1)
            for j in (2, 3):
                landed(pe, ("fi", l, FT - 1, j))
                landed(pe, ("fi", l, FT - 2, j))
            pe_resid(pe, f"fo{l}", 2, 11, act)

        def a_ffn(L, l):
            with L.e.Fori(0, FT // 2) as i:
                for u in range(2):
                    for h in range(2):
                        m, m2 = items[("fi", l, u, h)], items[("fi", l, u, 2 + h)]
                        L.e.wait_ge(S(f"bank_full{m % 8}"), i + (m // 8 + 1))
                        L.e.wait_ge(S(f"bank_free{m2 % 8}"), i + m2 // 8)
                        nc.scalar.activation(sgf[:, u, half(h)], ps[:, m % 8, 0:HT], ACT.Silu) \
                          .then_inc(S(f"bank_free{m % 8}"), 1)
            m = items[("fi", l, FT - 1, 1)]
            L.last = (f"bank_free{m % 8}", m // 8 + 1)

        sgf = sgb

        def v_ffn(L, l):
            with L.e.Fori(0, FT // 2) as i:
                for u in range(2):
                    for h in range(2):
                        m, m2 = items[("fi", l, u, h)], items[("fi", l, u, 2 + h)]
                        L.e.wait_ge(S(f"bank_free{m % 8}"), i + (m // 8 + 1))
                        L.e.wait_ge(S(f"bank_full{m2 % 8}"), i + (m2 // 8 + 1))
                        nc.vector.tensor_tensor(act[:, 2 * i + u, half(h)], ps[:, m2 % 8, 0:HT], sgf[:, u, half(h)],
                                                ALU.mult).then_inc(S(f"bank_free{m2 % 8}"), 1)
            m = items[("fi", l, FT - 1, 3)]
            L.last = (f"bank_free{m % 8}", m // 8 + 1)

        wsum = {}

        def wcount(n):
            if not wsum:
                tot = [0, 0]
                for key, q in units.items():
                    tot[q % 2] += 32 if key[0] == "fi" else 16
                    wsum[q] = tot[q % 2]
            return wsum[n]

        M = Space(arena, AR, 0)
        qT = M.take(KT * T, "p (f t) -> p f t", f=KT)
        qraw = M.take(2 * 5 * MD, "p (i t n) -> p i t n", i=2, t=5)
        pm = M.take(2 * 4 * NM, "p (i t n) -> p i t n", i=2, t=4)
        pmT = M.take(2 * 2 * SEQ, "p (i c t) -> p i c t", i=2, c=2)
        KTs = M.take(2 * KT * NM, "p (i f m) -> p i f m", i=2, f=KT)
        sTs = M.take(2 * P, "p (c n) -> p c n", c=2)
        psm = M.take(2 * P)
        pTs = M.take(2 * P, "p (c n) -> p c n", c=2)
        qs = M.take(2 * 16, "p (i n) -> p i n", i=2)
        ms = M.take(2 * 16, "p (i n) -> p i n", i=2)
        M.at = 16400
        ck = M.take(4 * 2 * D, "p (i c n) -> p i c n", i=4, c=2)
        SC = float(MD) ** -0.5

        def rows(t):
            return P if t < 4 else NS

        def tsl(t):
            return slice(P * t, P * t + P) if t < 4 else slice(SEQ, T)

        def ck_ready(e, l, n):
            e.wait_ge(S(f"ck{n % 4}"), 16 * (4 * l + n // 4 + 1))

        def sp_cache(sp, l):
            for n in range(2 * DB):
                b = n % DB
                if n >= 4:
                    if n - 4 < DB:
                        m = items[("skT", l, n - 4, 3)]
                        sp.wait_ge(S(f"bank_full{m % 8}"), m // 8 + 1)
                    else:
                        sp.wait_ge(S("sv_used"), DB * l + n - 4 - DB + 1)
                elif n == 0 and l == 0:
                    for i in range(4):
                        landed(sp, ("yT", NB - 1, i // 2, i % 2))
                    landed(sp, ("fin", 1))
                elif n == 0:
                    landed(sp, ("wo", KT - 1, 1))
                src = a["cache_mem_k" if n < DB else "cache_mem_v"][l, b].rearrange("(c p) h n -> p c (h n)", p=P)
                sp.dma_start(ck[:, n % 4], src).then_inc(S(f"ck{n % 4}"), 16)

        def pe_memattn(pe, l):
            t = nc.tensor
            nrm = 0 if l == 0 else 3
            pe.wait_ge(S("h_ready"), KT * (nrm + 1))

            def turn(h):
                pe.wait_ge(S("qn_ready"), MH * l + h + 1)
                for d in range(2):
                    b = fill(pe, ("mqT", l, h, d))
                    for q in range(4):
                        ins = t.transpose(b[:, P * q:P * q + P], qraw[:, h % 2, q, P * d:P * d + P], ident[:])
                    filled(("mqT", l, h, d), ins)
                b = fill(pe, ("mqT", l, h, 2))
                for d in range(2):
                    ins = t.transpose(b[:, NS * d:NS * d + NS], qraw[0:NS, h % 2, 4, P * d:P * d + P],
                                      ident[0:NS, 0:NS])
                filled(("mqT", l, h, 2), ins)

            for h in range(MH):
                w = uslot(("mq", l, h), KT)
                for i in range(3):
                    b = fill(pe, ("mq", l, h, i))
                    if i == 0:
                        uready(pe, ("mq", l, h))
                    for c, tt in enumerate((2 * i, 2 * i + 1) if i < 2 else (4,)):
                        for k in range(KT):
                            ins = t.matmul(b[0:rows(tt), 256 * c:256 * c + 256], hT[:, k, tsl(tt)], w[:, k, :],
                                           start=(k == 0), stop=(k == KT - 1))
                    filled(("mq", l, h, i), ins)
                if h >= 1:
                    turn(h - 1)
            turn(MH - 1)
            for h in range(MH):
                for i in range(3):
                    landed(pe, ("mqT", l, h, i))
                landed(pe, ("mkT", l, h))
                landed(pe, ("kv", l, 4 + h))
            for h in range(MH + 1):
                if h < MH:
                    for q in range(2):
                        b = fill(pe, ("ms", l, h, q))
                        for c in range(2):
                            for d in range(2):
                                ins = t.matmul(b[:, 256 * c:256 * c + 256], qT[:, 2 * h + d, tsl(2 * q + c)],
                                               mKT[:, l, 2 * h + d, :], start=(d == 0), stop=(d == 1))
                        filled(("ms", l, h, q), ins)
                if h >= 1:
                    g = h - 1
                    pe.wait_ge(S("mp_ready"), MH * l + h)
                    for c in range(2):
                        b = fill(pe, ("mp", l, g, c))
                        for q in range(4):
                            ins = t.transpose(b[:, P * q:P * q + P], pm[:, g % 2, q, P * c:P * c + P], ident[:])
                        filled(("mp", l, g, c), ins)
                    landed(pe, ("mp", l, g, 0))
                    landed(pe, ("mp", l, g, 1))
                    for d in range(2):
                        b = fill(pe, ("mo", l, g, d))
                        for c in range(2):
                            ins = t.matmul(b[:, :], mV[:, l, c, 256 * g + P * d:256 * g + P * d + P],
                                           pmT[:, g % 2, c, :], start=(c == 0), stop=(c == 1))
                        filled(("mo", l, g, d), ins)
            for bb in range(DB):
                ck_ready(pe, l, bb)
                for i in range(4):
                    b = fill(pe, ("skT", l, bb, i))
                    for q in range(4):
                        f, c = 2 * i + q // 2, q % 2
                        ins = t.transpose(b[:, P * q:P * q + P], ck[:, bb % 4, c, P * f:P * f + P], ident[:])
                    filled(("skT", l, bb, i), ins)
                for i in range(4):
                    landed(pe, ("skT", l, bb, i))
                b = fill(pe, ("ssT", l, bb))
                for c in range(2):
                    for h in range(MH):
                        for d in range(2):
                            ins = t.matmul(b[:, 4 * (MH * c + h):4 * (MH * c + h) + 4],
                                           KTs[:, bb % 2, 2 * h + d, P * c:P * c + P],
                                           qT[:, 2 * h + d, SEQ + DS * bb:SEQ + DS * bb + DS],
                                           start=(d == 0), stop=(d == 1))
                filled(("ssT", l, bb), ins)
            for bb in range(DB):
                landed(pe, ("ssT", l, bb))
            b = fill(pe, ("ss", l))
            for c in range(2):
                ins = t.transpose(b[:, P * c:P * c + P], sTs[:, c, :], ident[:])
            filled(("ss", l), ins)
            pe.wait_ge(S("sp_ready"), l + 1)
            b = fill(pe, ("sp", l))
            for c in range(2):
                ins = t.transpose(b[:, P * c:P * c + P], psm[:, P * c:P * c + P], ident[:])
            filled(("sp", l), ins)
            landed(pe, ("sp", l))
            b = fill(pe, ("so", l))
            for bb in range(DB):
                n = DB + bb
                ck_ready(pe, l, n)
                for f in range(KT):
                    for c in range(2):
                        h = f // 2
                        ins = t.matmul(b[:, NS * f + DS * bb:NS * f + DS * bb + DS],
                                       ck[:, n % 4, c, P * f:P * f + P],
                                       pTs[:, c, NS * h + DS * bb:NS * h + DS * bb + DS],
                                       start=(c == 0), stop=(c == 1))
                ins.then_inc(S("sv_used"), 1)
            pe.wait_ge(S("sv_used"), DB * (l + 1))
            t.transpose(b[:, 256:384], ident[:], ident[:]).then_inc(S(f"bank_full{items[('so', l)] % 8}"), 1)
            landed(pe, ("so", l))
            for g in range(MH):
                for d in range(2):
                    landed(pe, ("mo", l, g, d))
            pe_resid(pe, f"mo{l}", 1, KT, hT)

        def a_memattn(L, l):
            s = nc.scalar
            L.need("qs_init", l + 1)
            for h in range(MH):
                if h >= 2:
                    landed(L.e, ("mqT", l, h - 2, 2))
                for i in range(3):
                    b = full(L, ("mq", l, h, i))
                    if i < 2:
                        free(L, ("mq", l, h, i), s.activation(qraw[:, h % 2, 2 * i:2 * i + 2].rearrange("p t n -> p (t n)"),
                                                              b[:, :], ACT.Copy))
                    else:
                        free(L, ("mq", l, h, i), s.activation(qraw[0:NS, h % 2, 4], b[0:NS, 0:256], ACT.Copy))
                L.settle()
                for tt in range(5):
                    r = rows(tt)
                    L.settle()
                    L.did(s.activation(scr[0:r], qraw[0:r, h % 2, tt], ACT.Square, accum_out=qs[0:r, h % 2, tt:tt + 1]))
                L.settle()
                L.did(s.activation(qs[:, h % 2, 5:10], qs[:, h % 2, 0:5], ACT.Sqrt, bias=epst[:], scale=1.0 / MD),
                      "qs_sqrt")
                if h >= 1:
                    b = full(L, ("mqT", l, h - 1, 1))
                    free(L, ("mqT", l, h - 1, 1), s.activation(qT[:, 2 * h - 1, 0:SEQ], b[:, :], ACT.Copy,
                                                               scale=g_mq(l, 1)))
            b = full(L, ("mqT", l, MH - 1, 1))
            free(L, ("mqT", l, MH - 1, 1), s.activation(qT[:, 2 * MH - 1, 0:SEQ], b[:, :], ACT.Copy, scale=g_mq(l, 1)))

            def finish(g):
                b = full(L, ("mp", l, g, 1))
                free(L, ("mp", l, g, 1), s.activation(pmT[:, g % 2, 1], b[:, :], ACT.Copy))
                b = full(L, ("mo", l, g, 1))
                free(L, ("mo", l, g, 1), s.activation(hT[:, 2 * g + 1, 0:SEQ], b[:, :], ACT.Copy))
            for h in range(MH):
                L.need("nmx_ready", MH * l + h + 1)
                for q in range(4):
                    b = full(L, ("ms", l, h, q // 2))
                    ins = s.activation(pm[:, h % 2, q], b[:, 256 * (q % 2):256 * (q % 2) + 256], ACT.Exp,
                                       bias=ms[:, h % 2, q:q + 1], scale=SC, accum_out=ms[:, h % 2, 4 + q:5 + q])
                    if q % 2:
                        free(L, ("ms", l, h, q // 2), ins)
                    else:
                        L.did(ins)
                if h >= 1:
                    finish(h - 1)
            finish(MH - 1)
            for bb in range(DB):
                if bb >= 2:
                    landed(L.e, ("ssT", l, bb - 2))
                for i in (1, 3):
                    b = full(L, ("skT", l, bb, i))
                    free(L, ("skT", l, bb, i), s.activation(KTs[:, bb % 2, 2 * i:2 * i + 2].rearrange("p f m -> p (f m)"),
                                                            b[:, :], ACT.Copy))
            L.need("snmx_ready", l + 1)
            b = full(L, ("ss", l))
            free(L, ("ss", l), s.activation(psm[:], b[:, 0:256], ACT.Exp, bias=st[:, 8:9], scale=SC,
                                            accum_out=st[:, 9:10]))
            b = full(L, ("so", l))
            free(L, ("so", l), s.activation(hT[:, :, SEQ:], b[:, 0:256].rearrange("p (f n) -> p f n", f=KT), ACT.Copy))

        def v_memattn(L, l):
            v = nc.vector
            L.did(v.memset(qs, 1.0), "qs_init")

            def turned(h):
                b = full(L, ("mqT", l, h, 0))
                free(L, ("mqT", l, h, 0), v.tensor_scalar(qT[:, 2 * h, 0:SEQ], b[:, :], g_mq(l, 0), None, ALU.mult))
                b = full(L, ("mqT", l, h, 2))
                L.did(v.tensor_scalar(qT[:, 2 * h, SEQ:], b[:, 0:NS], g_mq(l, 0), None, ALU.mult))
                free(L, ("mqT", l, h, 2), v.tensor_scalar(qT[:, 2 * h + 1, SEQ:], b[:, NS:2 * NS], g_mq(l, 1), None,
                                                          ALU.mult))
            for h in range(MH):
                L.need("qs_sqrt", MH * l + h + 1)
                L.did(v.reciprocal(qs[:, h % 2, 10:15], qs[:, h % 2, 5:10]))
                L.settle()
                for tt in range(5):
                    r = rows(tt)
                    L.did(v.tensor_scalar(qraw[0:r, h % 2, tt], qraw[0:r, h % 2, tt], qs[0:r, h % 2, 10 + tt:11 + tt],
                                          None, ALU.mult), "qn_ready" if tt == 4 else None)
                if h >= 1:
                    turned(h - 1)
            turned(MH - 1)

            def finish(g):
                L.recip(ms[:, g % 2, 8:12], ms[:, g % 2, 4:8])
                L.settle()
                for q in range(4):
                    L.did(v.tensor_scalar(pm[:, g % 2, q], pm[:, g % 2, q], ms[:, g % 2, 8 + q:9 + q], None, ALU.mult),
                          "mp_ready" if q == 3 else None)
                b = full(L, ("mp", l, g, 0))
                free(L, ("mp", l, g, 0), v.tensor_copy(pmT[:, g % 2, 0], b[:, :]))
                b = full(L, ("mo", l, g, 0))
                free(L, ("mo", l, g, 0), v.tensor_copy(hT[:, 2 * g, 0:SEQ], b[:, :]))
            for h in range(MH):
                for q in range(2):
                    b = full(L, ("ms", l, h, q))
                    L.did(v.tensor_reduce(ms[:, h % 2, 12 + 2 * q:14 + 2 * q], b[:, :].rearrange("p (c n) -> p c n", c=2),
                                          AX, ALU.max))
                L.ts(ms[:, h % 2, 0:4], ms[:, h % 2, 12:16], -SC, None, ALU.mult, sem="nmx_ready")
                if h >= 1:
                    landed(L.e, ("ms", l, h - 1, 1))
                    finish(h - 1)
            landed(L.e, ("ms", l, MH - 1, 1))
            finish(MH - 1)
            for bb in range(DB):
                if bb >= 2:
                    landed(L.e, ("ssT", l, bb - 2))
                for i in (0, 2):
                    b = full(L, ("skT", l, bb, i))
                    free(L, ("skT", l, bb, i), v.tensor_copy(KTs[:, bb % 2, 2 * i:2 * i + 2].rearrange("p f m -> p (f m)"),
                                                             b[:, :]))
                b = full(L, ("ssT", l, bb))
                free(L, ("ssT", l, bb), v.tensor_copy(
                    sTs.rearrange("p c (h n) -> p (c h) n", h=MH)[:, :, DS * bb:DS * bb + DS],
                    b[:, 0:32].rearrange("p (n t) -> p n t", t=DS)))
            b = full(L, ("ss", l))
            L.did(v.tensor_reduce(st[:, 10:11], b[:, 0:256], AX, ALU.max))
            L.ts(st[:, 8:9], st[:, 10:11], -SC, None, ALU.mult, sem="snmx_ready")
            landed(L.e, ("ss", l))
            L.recip(st[:, 11:12], st[:, 9:10])
            L.ts(psm[:], psm[:], st[:, 11:12], None, ALU.mult, sem="sp_ready")
            b = full(L, ("sp", l))
            free(L, ("sp", l), v.tensor_copy(pTs.rearrange("p c n -> p (c n)"), b[:, 0:256]))

        W_ = Space(arena, AR, 0)
        q2 = W_.take(NG * 4 * T, "p (g f t) -> p g f t", g=NG, f=4)
        k2 = W_.take(NG * 4 * T, "p (g f t) -> p g f t", g=NG, f=4)
        Vt = W_.take(5 * NG * SW, "p (t g n) -> p t g n", t=5, g=NG)
        u0 = W_.at
        raw = W_.take(2 * 5 * RUNIT, "p (i t n) -> p i t n", i=2, t=5)
        sqr = W_.take(5 * RUNIT, "p (t n) -> p t n", t=5)
        W2 = Space(arena, AR, u0)
        sc2 = W2.take(2 * 6 * P, "p (i n) -> p i n", i=2)
        pT2 = W2.take(2 * 6 * P, "p (i n) -> p i n", i=2)
        W3 = Space(arena, AR, u0)
        cb = W3.take(2 * 5 * SW, "p (i n) -> p i n", i=2)
        qbd = W3.take(NG * 4 * DB * 2 * DS, "p (g f b h t) -> p g f b h t", g=NG, f=4, b=DB, h=2)
        M0 = mKT0[:, 0:515]
        M12 = mKT0[:, 516:516 + 256]
        m4 = mKT0[:, 780:784]
        KT1 = mKT0[:, 0:2048].rearrange("p (t f j) -> p t f j", t=4, f=4)
        KT0 = mV0[:, 0:512].rearrange("p (f j) -> p f j", f=4)
        KT2 = mV0[:, 512:1536].rearrange("p (t f j) -> p t f j", t=4, f=4)
        tail = Space(hflat, KT * T, 4 * T)
        sT = tail.take(2 * 256, "p (g n) -> p g n", g=2)
        sT2 = tail.take(256)
        sTn = tail.take(NG * 256, "p (g n) -> p g n", g=NG)
        pT2s = tail.take(256)
        pR = kk[:, 0:832].rearrange("p (r n) -> p r n", r=2)
        pTc = pt[:].rearrange("p (g n) -> p g n", g=2)
        pTn = arena[:, u0 + 5120:u0 + 5120 + 768].rearrange("p (g n) -> p g n", g=NG)
        mk0 = sb("mk0", DS)
        mkn = sb("mkn", 2 * NS)
        sa = sb("sa", 64)
        q20 = sb("q20", 2 * 60)
        q20v = q20[:].rearrange("p (i n) -> p i n", i=2)
        SS = float(SD) ** -0.5

        def qcols(u):
            kind, g, hh = u // 6, (u % 6) // 2, u % 2
            return kind, g, hh, (kind * NG + g) * SW + RUNIT * hh

        def sp_qkv(sp):
            for u in range(18):
                kind, g, hh, c0 = qcols(u)
                load_unit(sp, a["attn_w_qkv"][0], ("qkv", u), KT, slice(0, D), slice(c0, c0 + RUNIT))

        def store_rows(sp, dst, g, hh, get, sem):
            c = slice(RUNIT * hh, RUNIT * hh + RUNIT)
            if g == 0:
                sp.dma_start(dst[0, 0].rearrange("p h n -> p (h n)")[:, c], get(slice(3, 4)).rearrange("p t n -> p (t n)")) \
                  .then_inc(S(sem), 16)
            else:
                sp.dma_start(dst[0, 0].rearrange("(j r) h n -> j r (h n)", r=4)[:, :, c], get(slice(0, 4))) \
                  .then_inc(S(sem), 16)

        def store_kv(sp, us):
            for u in us:
                kind, g, hh, c0 = qcols(u)
                c = slice(RUNIT * hh, RUNIT * hh + RUNIT)
                dst = o[4 + 2 * g + kind - 1]
                dsts = o[14 + 2 * g + kind - 1][0].rearrange("b t h n -> (b t) (h n)")[:, c]
                if kind == 1:
                    sp.wait_ge(S("k_ready"), u - 5)
                    get = lambda t, i=u % 2: raw[:, i, t]
                    srcs = raw[0:NS, u % 2, 4]
                else:
                    for i in range(3):
                        landed(sp, ("qkv", u, i))
                    get = lambda t, c=c, g=g: Vt[:, t, g, c]
                    srcs = Vt[0:NS, 4, g, c]
                sem = f"k_stored{u % 2}" if kind == 1 else "v_stored"
                store_rows(sp, dst, g, hh, get, sem)
                sp.dma_start(dsts, srcs).then_inc(S(sem), 16)

        def pool_masks(L):
            g = nc.gpsimd
            for h in range(MH):
                landed(L.e, ("mo", 0, h, 1))
            for i in range(2):
                landed(L.e, ("ms", 0, MH - 1, i))
            L.settle()
            L.did(g.memset(M0, 0.0))
            L.settle()
            L.did(g.memset(M12, 0.0))
            L.settle()
            L.did(g.memset(mk0[:], 0.0))
            L.settle()
            L.did(g.memset(mkn[:], 0.0))
            L.settle()
            L.settle()
            L.did(g.affine_select(out=M0, in_=M0, compare_op=ALU.is_ge, fill=BIG, base=3, pattern=[[-1, 515]],
                                  channel_multiplier=4))
            L.settle()
            L.did(g.affine_select(out=M12[:, 0:P], in_=M12[:, 0:P], compare_op=ALU.is_ge, fill=BIG, base=0,
                                  pattern=[[-1, P]], channel_multiplier=1))
            L.settle()
            L.did(g.affine_select(out=mk0[:], in_=mk0[:], compare_op=ALU.is_ge, fill=BIG, base=0,
                                  pattern=[[-1, DS]], channel_multiplier=1))
            n0 = mkn[0:NS, 0:NS].rearrange("p (b t) -> p b t", b=DB)
            L.settle()
            L.did(g.affine_select(out=n0, in_=n0, compare_op=ALU.is_ge, fill=BIG, base=0,
                                  pattern=[[-DS, DB], [0, DS]], channel_multiplier=1))
            n1 = mkn[0:NS, NS:2 * NS]
            L.settle()
            L.did(g.affine_select(out=n1, in_=n1, compare_op=ALU.is_equal, fill=BIG, base=0,
                                  pattern=[[-1, NS]], channel_multiplier=1))
            L.settle()
            L.did(g.affine_select(out=M0, in_=M0, compare_op=ALU.is_ge, fill=BIG, base=P - 3, pattern=[[1, 515]],
                                  channel_multiplier=-4))
            L.settle()
            L.did(g.affine_select(out=n0, in_=n0, compare_op=ALU.is_ge, fill=BIG, base=0,
                                  pattern=[[DS, DB], [1, DS]], channel_multiplier=-1), "masks_ready")

        def v_masks(L):
            L.need("masks_ready", 1)
            L.settle()
            L.did(nc.vector.tensor_reduce(m4, ident[:].rearrange("p (j r) -> p r j", r=4), AX, ALU.add))
            L.ts(m4, m4, -BIG, BIG, ALU.mult, ALU.add)
            L.tt(M12[:, P:].rearrange("p (j r) -> p j r", r=4), M12[:, 0:P].rearrange("p (j r) -> p j r", r=4),
                 m4.unsqueeze(1).to_broadcast([P, 32, 4]), ALU.add)

        def pe_qkv(pe):
            t = nc.tensor
            pe.wait_ge(S("h_ready"), KT * 3)

            def turn(u):
                kind = u // 6
                if kind == 0:
                    pe.wait_ge(S("q_ready"), u + 1)
                else:
                    pe.wait_ge(S("k_ready"), u - 5)
                for d in range(2):
                    b = fill(pe, ("qkT", u, d))
                    for q in range(4):
                        ins = t.transpose(b[:, P * q:P * q + P], raw[:, u % 2, q, P * d:P * d + P], ident[:])
                    filled(("qkT", u, d), ins)
                b = fill(pe, ("qkT", u, 2))
                for d in range(2):
                    ins = t.transpose(b[:, NS * d:NS * d + NS], raw[0:NS, u % 2, 4, P * d:P * d + P], ident[0:NS, 0:NS])
                filled(("qkT", u, 2), ins)

            for u in range(18):
                kind, g, hh, _ = qcols(u)
                w = uslot(("qkv", u), KT)
                for i in range(3):
                    b = fill(pe, ("qkv", u, i))
                    if i == 0:
                        uready(pe, ("qkv", u))
                    for c, tt in enumerate((2 * i, 2 * i + 1) if i < 2 else (4,)):
                        sl = tsl(tt) if tt == 4 or (kind > 0 and g == 0) else slice(tt, SEQ, 4)
                        for k in range(KT):
                            ins = t.matmul(b[0:rows(tt), 256 * c:256 * c + 256], hT[:, k, sl], w[:, k, :],
                                           start=(k == 0), stop=(k == KT - 1))
                    filled(("qkv", u, i), ins)
                if 1 <= u <= 12:
                    turn(u - 1)

        def a_qkv(L):
            s = nc.scalar
            L.need("q20_init", 1)

            def turned(u):
                kind, g, hh, _ = qcols(u)
                b = full(L, ("qkT", u, 1))
                if kind == 0:
                    ins = s.activation(q2[:, g, 2 * hh + 1, 0:SEQ], b[:, :], ACT.Copy, scale=g_sq(g))
                else:
                    ins = s.activation(k2[:, g, 2 * hh + 1, 0:SEQ], b[:, :], ACT.Copy)
                free(L, ("qkT", u, 1), ins)
            for u in range(18):
                kind, g, hh, _ = qcols(u)
                if kind < 2:
                    if u >= 2:
                        landed(L.e, ("qkT", u - 2, 2))
                        if u - 2 >= 6:
                            L.need(f"k_stored{u % 2}", 32 * ((u - 8) // 2 + 1))
                    dst = raw[:, u % 2]
                else:
                    dst = Vt[:, :, g, RUNIT * hh:RUNIT * hh + RUNIT]
                for i in range(3):
                    b = full(L, ("qkv", u, i))
                    if i < 2:
                        free(L, ("qkv", u, i), s.activation(dst[:, 2 * i:2 * i + 2],
                                                            b[:, :].rearrange("p (t n) -> p t n", t=2), ACT.Copy))
                    else:
                        free(L, ("qkv", u, i), s.activation(dst[0:NS, 4], b[0:NS, 0:256], ACT.Copy))
                if kind < 2:
                    L.settle()
                    if u >= 1:
                        L.need("sq_used", u)
                    L.did(s.activation(sqr[:, 0:4], raw[:, u % 2, 0:4], ACT.Square))
                    L.did(s.activation(sqr[0:NS, 4], raw[0:NS, u % 2, 4], ACT.Square), "sqr_ready")
                    L.need("sq_used", u + 1)
                    L.did(s.activation(q20v[:, u % 2, 20:40], q20v[:, u % 2, 0:20], ACT.Sqrt, bias=epst[:],
                                       scale=1.0 / SD), "q20_sqrt")
                if 1 <= u <= 12:
                    turned(u - 1)

        def v_qkv(L):
            v = nc.vector
            L.did(v.memset(q20[:], 1.0), "q20_init")

            def turned(u):
                kind, g, hh, _ = qcols(u)
                b = full(L, ("qkT", u, 0))
                b2 = None
                dst = (q2, k2)[kind]
                if kind == 0:
                    free(L, ("qkT", u, 0), v.tensor_scalar(dst[:, g, 2 * hh, 0:SEQ], b[:, :], g_sq(g), None, ALU.mult))
                else:
                    free(L, ("qkT", u, 0), v.tensor_copy(dst[:, g, 2 * hh, 0:SEQ], b[:, :]))
                b = full(L, ("qkT", u, 2))
                src = b[:, 0:2 * NS].rearrange("p (f n) -> p f n", f=2)
                if kind == 0:
                    free(L, ("qkT", u, 2), v.tensor_scalar(dst[:, g, 2 * hh:2 * hh + 2, SEQ:], src, g_sq(g), None, ALU.mult))
                else:
                    free(L, ("qkT", u, 2), v.tensor_copy(dst[:, g, 2 * hh:2 * hh + 2, SEQ:], src))
            for u in range(13):
                if u < 12:
                    L.need("sqr_ready", u + 1)
                    qv = q20v[:, u % 2]
                    L.settle()
                    L.did(v.tensor_reduce(qv[:, 0:16], sqr[:, 0:4].rearrange("p t (h n) -> p (t h) n", h=4), AX, ALU.add))
                    L.did(v.tensor_reduce(qv[0:NS, 16:20], sqr[0:NS, 4].rearrange("p (h n) -> p h n", h=4), AX, ALU.add),
                          "sq_used")
                    L.need("q20_sqrt", u + 1)
                    L.recip(qv[:, 40:60], qv[:, 20:40])
                    L.settle()
                    x = raw[:, u % 2, 0:4].rearrange("p t (h n) -> p (t h) n", h=4)
                    L.did(v.tensor_tensor(x, x, qv[:, 40:56].unsqueeze(2).to_broadcast([P, 16, SD]), ALU.mult))
                    x = raw[0:NS, u % 2, 4].rearrange("p (h n) -> p h n", h=4)
                    L.did(v.tensor_tensor(x, x, qv[0:NS, 56:60].unsqueeze(2).to_broadcast([NS, 4, SD]), ALU.mult),
                          "q_ready" if u < 6 else "kn_ready")
                if u >= 1:
                    turned(u - 1)

        def pool_keys(L):
            g_ = nc.gpsimd
            for u in range(6, 12):
                _, g, hh, _ = qcols(u)
                L.need("kn_ready", u - 5)
                kb = kgb[:, SD * g:SD * g + SD]
                x = raw[:, u % 2, 0:4].rearrange("p t (h n) -> p (t h) n", h=4)
                L.settle()
                L.did(g_.tensor_tensor(x, x, kb.unsqueeze(1).to_broadcast([P, 16, SD]), ALU.mult))
                x = raw[0:NS, u % 2, 4].rearrange("p (h n) -> p h n", h=4)
                L.settle()
                L.did(g_.tensor_tensor(x, x, kb[0:NS].unsqueeze(1).to_broadcast([NS, 4, SD]), ALU.mult), "k_ready")
                store_kv(L.e, [u])
            store_kv(L.e, range(12, 18))

        def step(n):
            return n // 8, (n % 8) // 2, n % 2

        NA = SH * 4

        def pe_attn(pe):
            t = nc.tensor
            for u in range(12):
                for i in range(3):
                    landed(pe, ("qkT", u, i))
            for u in range(12, 18):
                for i in range(3):
                    landed(pe, ("qkv", u, i))
            for n in range(NA + 1):
                if n < NA:
                    f, r, e = step(n)
                    q = slice(64 * e, 64 * e + 64)
                    b = fill(pe, ("as", n, 0))
                    ins = t.matmul(b[:, :], q2[q, 0, f, P * r:P * r + P], k2[q, 0, f, 0:SEQ], start=True, stop=True)
                    filled(("as", n, 0), ins)
                    b = fill(pe, ("as", n, 1))
                    for g in (1, 2):
                        ins = t.matmul(b[:, P * (g - 1):P * g], q2[q, g, f, P * r:P * r + P],
                                       k2[q, g, f, P * r:P * r + P], start=True, stop=True)
                    filled(("as", n, 1), ins)
                if n >= 1:
                    m = n - 1
                    f, r, e = step(m)
                    pe.wait_ge(S("ap_ready"), m + 1)
                    b = fill(pe, ("ap", m, 0))
                    for c in range(4):
                        ins = t.transpose(b[:, P * c:P * c + P], sc2[:, m % 2, P * c:P * c + P], ident[:])
                    filled(("ap", m, 0), ins)
                    b = fill(pe, ("ap", m, 1))
                    for c in range(2):
                        ins = t.transpose(b[:, P * c:P * c + P], sc2[:, m % 2, P * (4 + c):P * (5 + c)], ident[:])
                    filled(("ap", m, 1), ins)
                    landed(pe, ("ap", m, 0))
                    landed(pe, ("ap", m, 1))
                    b = fill(pe, ("ao", m))
                    hc = slice(SD * (2 * f + e), SD * (2 * f + e) + SD)
                    for c in range(6):
                        vv = Vt[:, c, 0, hc] if c < 4 else Vt[:, r, c - 3, hc]
                        ins = t.matmul(b[64 * e:64 * e + 64, 0:P], vv, pT2[:, m % 2, P * c:P * c + P],
                                       start=(c == 0), stop=(c == 5))
                    filled(("ao", m), ins)

        def v_attn(L):
            v = nc.vector
            for n in range(NA + 1):
                if n < NA:
                    f, r, e = step(n)
                    x = 16 * (n % 2)
                    if n >= 2:
                        m = items[("ap", n - 2, 1)]
                        L.e.wait_ge(S(f"bank_full{m % 8}"), m // 8 + 1)
                    elif n == 0:
                        L.need("k_stored0", 32 * 3)
                        L.need("k_stored1", 32 * 3)
                        L.settle()
                    b = full(L, ("as", n, 0))
                    free(L, ("as", n, 0), v.tensor_tensor_reduce(sc2[:, n % 2, 0:512], b[:, :], M0[:, 3 - r:515 - r],
                                                                 1.0, -3e38, ALU.add, ALU.max, sa[:, x:x + 1]))
                    b = full(L, ("as", n, 1))
                    free(L, ("as", n, 1), v.tensor_tensor_reduce(sc2[:, n % 2, 512:768], b[:, 0:256], M12, 1.0, -3e38,
                                                                 ALU.add, ALU.max, sa[:, x + 1:x + 2]))
                    L.tt(sa[:, x + 2:x + 3], sa[:, x:x + 1], sa[:, x + 1:x + 2], ALU.max)
                    L.ts(sa[:, x + 3:x + 4], sa[:, x + 2:x + 3], -SS, None, ALU.mult, sem="anmx_ready")
                if n >= 1:
                    m = n - 1
                    f, r, e = step(m)
                    x = 16 * (m % 2)
                    L.need("aexp", m + 1)
                    L.did(v.reciprocal(sa[:, x + 5:x + 6], sa[:, x + 4:x + 5]))
                    L.ts(sc2[:, m % 2], sc2[:, m % 2], sa[:, x + 5:x + 6], None, ALU.mult, sem="ap_ready")
                    b = full(L, ("ap", m, 1))
                    free(L, ("ap", m, 1), v.tensor_copy(pT2[:, m % 2, 512:768], b[:, 0:256]))
                    b = full(L, ("ao", m))
                    h = slice(64 * e, 64 * e + 64)
                    free(L, ("ao", m), v.tensor_copy(hT[h, f, slice(r, SEQ, 4)], b[h, 0:P]))

        def a_attn(L):
            s = nc.scalar
            for n in range(NA + 1):
                if n < NA:
                    x = 16 * (n % 2)
                    L.need("anmx_ready", n + 1)
                    L.did(s.activation(sc2[:, n % 2], sc2[:, n % 2], ACT.Exp, bias=sa[:, x + 3:x + 4], scale=SS,
                                       accum_out=sa[:, x + 4:x + 5]), "aexp")
                if n >= 1:
                    m = n - 1
                    b = full(L, ("ap", m, 0))
                    free(L, ("ap", m, 0), s.activation(pT2[:, m % 2, 0:512], b[:, :], ACT.Copy))

        GR = (1, 4, 4)

        def sp_swacache(sp):
            for n in range(4 * DB):
                kv, b, part = n // (2 * DB), (n // 2) % DB, n % 2
                c = "kv"[kv]
                if n < 2:
                    for i in range(2):
                        landed(sp, ("ap", NA - 1, i))
                    landed(sp, ("ao", NA - 1))
                elif (n - 2) // (2 * DB) == 0:
                    m = items[("bkT", ((n - 2) // 2) % DB, 4 if part == 0 else 6)]
                    sp.wait_ge(S(f"bank_full{m % 8}"), m // 8 + 1)
                else:
                    m = items[("bo", ((n - 2) // 2) % DB)]
                    sp.wait_ge(S(f"bank_full{m % 8}"), m // 8 + 1)
                if part == 0:
                    sp.dma_start(cb[:, n % 2, 0:SW], a[f"cache_swa0_{c}"][0, b].rearrange("p h n -> p (h n)")) \
                      .then_inc(S(f"cb{n % 2}"), 16)
                    sp.dma_start(cb[:, n % 2, SW:5 * SW].rearrange("p (t n) -> p t n", t=4),
                                 a[f"cache_swa1_{c}"][0, b].rearrange("(j t) h n -> j t (h n)", t=4)) \
                      .then_inc(S(f"cb{n % 2}"), 16)
                else:
                    sp.dma_start(cb[0:64, n % 2, 0:4 * SW].rearrange("p (t n) -> p t n", t=4),
                                 a[f"cache_swa2_{c}"][0, b].rearrange("(j t) h n -> j t (h n)", t=16)[:, 0:4]) \
                      .then_inc(S(f"cb{n % 2}"), 16)

        def cb_ready(e, kv, b, part):
            e.wait_ge(S(f"cb{part}"), (32, 16)[part] * (DB * kv + b + 1))

        def pe_sattn(pe):
            t = nc.tensor
            pe.wait_ge(S("qbd_ready"), 1)
            for b_ in range(DB):
                cb_ready(pe, 0, b_, 0)
                for i in range(5):
                    b = fill(pe, ("bkT", b_, i))
                    for f in range(4):
                        ins = t.transpose(b[:, P * f:P * f + P], cb[:, 0, SW * i + P * f:SW * i + P * f + P], ident[:])
                    filled(("bkT", b_, i), ins)
                cb_ready(pe, 0, b_, 1)
                for i in range(2):
                    b = fill(pe, ("bkT", b_, 5 + i))
                    for q in range(8):
                        tt, f = 2 * i + q // 4, q % 4
                        ins = t.transpose(b[:, 64 * q:64 * q + 64], cb[0:64, 1, SW * tt + P * f:SW * tt + P * f + P],
                                          ident[0:64, 0:64])
                    filled(("bkT", b_, 5 + i), ins)
                for i in range(7):
                    landed(pe, ("bkT", b_, i))
                b = fill(pe, ("bs", b_))
                for f in range(4):
                    t.matmul(b[:, 8 * f:8 * f + 8], KT0[:, f, :], qbd[:, 0, f, b_].rearrange("p h t -> p (h t)"),
                             start=True, stop=True)
                    for tt in range(4):
                        c = 32 + 8 * f + tt
                        t.matmul(b[:, c:c + 5:4], KT1[:, tt, f, :], qbd[:, 1, f, b_, :, tt], start=True, stop=True)
                        c += 32
                        ins = t.matmul(b[0:64, c:c + 5:4], KT2[:, tt, f, :], qbd[:, 2, f, b_, :, tt],
                                       start=True, stop=True)
                filled(("bs", b_), ins)
            for i in range(2):
                b = fill(pe, ("bn", i))
                for g in range(NG):
                    for f in range(4):
                        q = slice(64 * i, 64 * i + 64)
                        c = P * g + NS * f
                        ins = t.matmul(b[0:NS, c:c + NS], k2[q, g, f, SEQ:], q2[q, g, f, SEQ:],
                                       start=True, stop=True)
                filled(("bn", i), ins)
            for b_ in range(DB):
                landed(pe, ("bs", b_))
            landed(pe, ("bn", 0))
            landed(pe, ("bn", 1))
            for R in range(2):
                b = fill(pe, ("br", R))
                rc = slice(P * R, P * R + P)
                for g in range(2):
                    t.transpose(b[:, P * g:P * g + P], sT[:, g, rc], ident[:])
                t.transpose(b[:, 256:320], sT2[0:64, rc], ident[0:64, 0:64])
                for g in range(NG):
                    ins = t.transpose(b[:, 320 + NS * g:320 + NS * g + NS], sTn[0:NS, g, rc], ident[0:NS, 0:NS])
                filled(("br", R), ins)
            pe.wait_ge(S("bp_ready"), 2)
            b = fill(pe, ("bp", 0))
            for g in range(2):
                for R in range(2):
                    ins = t.transpose(b[:, 256 * g + P * R:256 * g + P * R + P], pR[:, R, P * g:P * g + P], ident[:])
            filled(("bp", 0), ins)
            b = fill(pe, ("bp", 1))
            for R in range(2):
                t.transpose(b[0:64, P * R:P * R + P], pR[:, R, 256:320], ident[:])
            for R in range(2):
                ins = t.transpose(b[0:NS, 256 + P * R:256 + P * R + P], pR[:, R, 320:352], ident[:])
            filled(("bp", 1), ins)
            b = fill(pe, ("bp", 2))
            for g in range(2):
                for R in range(2):
                    ins = t.transpose(b[0:NS, 256 * g + P * R:256 * g + P * R + P],
                                      pR[:, R, 352 + NS * g:352 + NS * g + NS], ident[:])
            filled(("bp", 2), ins)
            for i in range(3):
                landed(pe, ("bp", i))

            def pcols(x, f, b_):
                return x.rearrange("p (h b t) -> p h b t", h=SH, b=DB)[:, 2 * f:2 * f + 2, b_]
            for b_ in range(DB):
                b = fill(pe, ("bo", b_))
                cb_ready(pe, 1, b_, 0)
                cb_ready(pe, 1, b_, 1)
                for f in range(4):
                    fc = slice(P * f, P * f + P)
                    for tt in range(4):
                        c = 8 * f + tt
                        v1 = cb[:, 0, SW * (1 + tt) + P * f:SW * (1 + tt) + P * f + P]
                        v2 = cb[0:64, 1, SW * tt + P * f:SW * tt + P * f + P]
                        t.matmul(b[:, c:c + 5:4], v1, pcols(pTc[:, 1], f, b_)[:, :, tt], start=(tt == 0),
                                 stop=False, skip_group_check=True)
                        t.matmul(b[:, c:c + 5:4], v2, pcols(pT2s[0:64], f, b_)[:, :, tt], start=False,
                                 stop=False, skip_group_check=True)
                    ins = t.matmul(b[:, 8 * f:8 * f + 8], cb[:, 0, fc], pcols(pTc[:, 0], f, b_), start=False,
                                   stop=True, skip_group_check=True)
                filled(("bo", b_), ins)
            b = fill(pe, ("bo", "new"))
            for f in range(4):
                for g in range(NG):
                    ins = t.matmul(b[:, 64 * f:64 * f + 64], Vt[0:NS, 4, g, P * f:P * f + P],
                                   pTn[0:NS, g, 64 * f:64 * f + 64], start=(g == 0), stop=(g == NG - 1))
            filled(("bo", "new"), ins)
            for b_ in list(range(DB)) + ["new"]:
                landed(pe, ("bo", b_))
            for n in range(NA):
                if n >= NA - 8:
                    landed(pe, ("ao", n))

        def v_sattn(L):
            v = nc.vector
            L.did(v.memset(qbd.rearrange("p g f b h t -> p (g f b h t)"), 0.0))
            L.settle()
            for g in range(NG):
                for h in range(2):
                    q = slice(64 * h, 64 * h + 64)
                    L.did(v.tensor_copy(qbd[q, g, :, :, h, :], q2[q, g, :, SEQ:].rearrange("p f (b t) -> p f b t", b=DB)),
                          "qbd_ready" if (g, h) == (NG - 1, 1) else None)

            def cols3(x, b_):
                return x.rearrange("p (h b t) -> p h b t", h=SH, b=DB)[:, :, b_]
            for b_ in range(DB):
                if b_ >= 1:
                    full(L, ("bs", b_ - 1))
                else:
                    L.settle()
                for i in (0, 2, 4, 6):
                    b = full(L, ("bkT", b_, i))
                    dst = (KT0[:, :] if i == 0 else KT1[:, i - 1] if i < 5 else KT2[:, 2:4])
                    pat = "p f j -> p (f j)" if i < 5 else "p t f j -> p (t f j)"
                    free(L, ("bkT", b_, i), v.tensor_copy(dst.rearrange(pat), b[:, :]))
                b = full(L, ("bs", b_))

                def src(c, q=P):
                    return b[0:q, 32 * c:32 * c + 32].rearrange("p (h t) -> p h t", t=DS)
                L.did(v.tensor_tensor(cols3(sT[:, 0], b_), src(0), mk0[:].unsqueeze(1).to_broadcast([P, SH, DS]), ALU.add))
                L.did(v.tensor_copy(cols3(sT[:, 1], b_), src(1)))
                free(L, ("bs", b_), v.tensor_copy(cols3(sT2[0:64], b_), src(2, 64)))
            for i in range(2):
                b = full(L, ("bn", i))
                for g in range(NG):
                    mk = mkn[0:NS, 0:NS] if g == 0 else mkn[0:NS, NS:]
                    ins = v.tensor_tensor(sTn[0:NS, g].rearrange("p (f e n) -> p f e n", f=4, e=2)[:, :, i],
                                          b[0:NS, P * g:P * g + P].rearrange("p (f n) -> p f n", f=4),
                                          mk.unsqueeze(1).to_broadcast([NS, 4, NS]), ALU.add)
                    if g < NG - 1:
                        L.did(ins)
                    else:
                        free(L, ("bn", i), ins)
            for R in range(2):
                b = full(L, ("br", R))
                L.did(v.tensor_reduce(sa[:, 40 + R:41 + R], b[:, 0:416], AX, ALU.max))
            L.ts(sa[:, 42:44], sa[:, 40:42], -SS, None, ALU.mult, sem="bnmx_ready")
            landed(L.e, ("br", 0))
            landed(L.e, ("br", 1))
            L.recip(sa[:, 46:48], sa[:, 44:46])
            L.settle()
            for R in range(2):
                L.did(v.tensor_scalar(pR[:, R], pR[:, R], sa[:, 46 + R:47 + R], None, ALU.mult), "bp_ready")
            b = full(L, ("bp", 0))
            free(L, ("bp", 0), v.tensor_copy(pTc.rearrange("p g n -> p (g n)"), b[:, :]))
            b = full(L, ("bp", 1))
            L.did(v.tensor_copy(pT2s[0:64], b[0:64, 0:256]))
            free(L, ("bp", 1), v.tensor_copy(pTn[0:NS, 0], b[0:NS, 256:512]))
            b = full(L, ("bp", 2))
            free(L, ("bp", 2), v.tensor_copy(pTn[0:NS, 1:3].rearrange("p g n -> p (g n)"), b[0:NS, :]))
            for b_ in range(DB):
                b = full(L, ("bo", b_))
                for h in range(2):
                    q = slice(64 * h, 64 * h + 64)
                    ins = v.tensor_copy(hT[q, 0:4, SEQ + DS * b_:SEQ + DS * b_ + DS],
                                        b[q, 0:32].rearrange("p (f h t) -> p f h t", f=4, h=2)[:, :, h])
                    if h:
                        free(L, ("bo", b_), ins)
                    else:
                        L.did(ins)
            b = full(L, ("bo", "new"))
            L.settle()
            for h in range(2):
                q = slice(64 * h, 64 * h + 64)
                x = hT[q, 0:4, SEQ:]
                ins = v.tensor_tensor(x, x, b[q, 0:256].rearrange("p (f h n) -> p f h n", f=4, h=2)[:, :, h], ALU.add)
                if h:
                    free(L, ("bo", "new"), ins)
                else:
                    L.did(ins)

        def a_sattn(L):
            s = nc.scalar
            landed(L.e, ("as", NA - 1, 0))
            landed(L.e, ("as", NA - 1, 1))
            for b_ in range(DB):
                if b_ >= 1:
                    full(L, ("bs", b_ - 1))
                for i in (1, 3, 5):
                    b = full(L, ("bkT", b_, i))
                    dst = KT1[:, i - 1] if i < 5 else KT2[:, 0:2]
                    pat = "p f j -> p (f j)" if i < 5 else "p t f j -> p (t f j)"
                    free(L, ("bkT", b_, i), s.activation(dst.rearrange(pat), b[:, :], ACT.Copy))
            L.need("bnmx_ready", 1)
            for R in range(2):
                b = full(L, ("br", R))
                free(L, ("br", R), s.activation(pR[:, R], b[:, 0:416], ACT.Exp, bias=sa[:, 42 + R:43 + R], scale=SS,
                                                accum_out=sa[:, 44 + R:45 + R]))

        yo = arena[:, 17000:17000 + 2 * D].rearrange("p (i n) -> p i n", i=2)

        def pe_out(pe):
            for m in range(KT):
                for h in range(2):
                    landed(pe, ("fo1", m, h))
            for tt in range(5):
                for q in range(2):
                    b = fill(pe, ("out", tt, q))
                    for f in range(4):
                        ins = nc.tensor.transpose(b[0:rows(tt), P * f:P * f + P], xT[:, 4 * q + f, tsl(tt)], ident[:])
                    filled(("out", tt, q), ins)

        def a_out(L):
            for tt in range(5):
                if tt >= 2:
                    L.need(f"y_out{tt % 2}", 16 * (tt // 2))
                b = full(L, ("out", tt, 0))
                free(L, ("out", tt, 0), nc.scalar.activation(yo[0:rows(tt), tt % 2, 0:512], b[0:rows(tt), :], ACT.Copy))

        def v_out(L):
            for tt in range(5):
                if tt >= 2:
                    L.need(f"y_out{tt % 2}", 16 * (tt // 2))
                b = full(L, ("out", tt, 1))
                free(L, ("out", tt, 1), nc.vector.tensor_copy(yo[0:rows(tt), tt % 2, 512:], b[0:rows(tt), :]))

        def sp_out(sp):
            for tt in range(5):
                landed(sp, ("out", tt, 0))
                landed(sp, ("out", tt, 1))
                dst = o[0][0, P * tt:P * tt + P] if tt < 4 else o[1].rearrange("b t n -> (b t) n")
                sp.dma_start(dst, yo[0:rows(tt), tt % 2]).then_inc(S(f"y_out{tt % 2}"), 16)

        block = ctx.enter_context(nc.Block())

        @block.sync
        def _(sp):
            sp_params(sp)
            sp_x8(sp, 0, 0)
            load_unit(sp, a["mem_w_kv"][0], ("kv", 0, 0), KT, slice(0, D), cols(0))
            load_unit(sp, a["mem_w_kv"][0], ("kv", 0, 1), KT, slice(0, D), cols(1))
            for k in range(1, NB):
                sp_x8(sp, 0, k)
            sp_x8(sp, 1, 0)
            for j in range(2, 8):
                load_unit(sp, a["mem_w_kv"][0], ("kv", 0, j), KT, slice(0, D), cols(j))
                if j < 6:
                    sp.wait_ge(S("mk_ready"), j - 1)
                    sp.dma_start(o[10][0, 0].rearrange("(c p) h n -> p c h n", p=P)[:, :, j - 2], kout) \
                      .then_inc(S("mk_out"), 16)
            load_unit(sp, a["ssm_w_glu"][0], ("glu", 0, 0), KT, slice(0, D), cols(0))
            load_unit(sp, a["ssm_w_glu"][0], ("glu", 1, 0), KT, slice(0, D), cols(1))
            for k in range(NB):
                sp_toeplitz(sp, k)
                if k + 1 < NB:
                    sp_x8(sp, 1, k + 1)
            sp_final(sp)
            for j in (2, 3):
                load_unit(sp, a["ssm_w_glu"][0], ("glu", j, 0), KT, slice(0, D), cols(j))
            for j in range(8):
                load_unit(sp, a["mem_w_kv"][1], ("kv", 1, j), KT, slice(0, D), cols(j))
                if 2 <= j < 6:
                    sp.wait_ge(S("mk_ready"), 4 + j - 1)
                    sp.dma_start(o[10][1, 0].rearrange("(c p) h n -> p c h n", p=P)[:, :, j - 2], kout) \
                      .then_inc(S("mk_out"), 16)
            for l in range(2):
                if l == 1:
                    sp_qkv(sp)
                    load_resid(sp, a["attn_w_o"][0], "wo", 1, 4)
                for h in range(MH):
                    load_unit(sp, a["mem_w_q"][l], ("mq", l, h), KT, slice(0, D), cols(h))
                load_resid(sp, a["mem_w_o"][l], f"mo{l}", 1, KT)
                sp_ffn(sp, l)
            sp_out(sp)
            sp.wait_ge(S("y_out0"), 16 * 3)
            sp.wait_ge(S("y_out1"), 16 * 2)
            sp.wait_ge(S("out"), 16 * n_out[0])
            sp.wait_ge(S("mk_out"), 16 * 8)

        @block.gpsimd
        def _(pool):
            L = Lane(pool, "pool_done")
            pool_consts(L)
            for k in range(NB):
                pool_qb(L, k)
            for l in range(2):
                for j in range(4, 8):
                    landed(pool, ("kv", l, j))
                pool.dma_start(o[11][l, 0].rearrange("(c p) h n -> p c (h n)", p=P), mV[:, l]).then_inc(S("mv_out"), 16)
            sp_cache(pool, 0)
            pool.wait_ge(S("mv_out"), 32)
            pool_masks(L)
            pool_keys(L)
            sp_swacache(pool)
            sp_cache(pool, 1)
            pool.wait_ge(S("v_stored"), 32 * 6)
            pool.wait_ge(S("k_stored0"), 32 * 3)
            pool.wait_ge(S("k_stored1"), 32 * 3)

        @block.scalar
        def _(sc):
            L = Lane(sc, "act_done")
            act_loads(sc)
            L.need("consts_ready", 1)
            a_stats(L)
            a_xT(L)
            a_memkv(L, 0)
            for k in range(NB):
                a_batch(L, k)
            a_glu(L)
            a_memkv(L, 1)
            a_squares(L, "glu", 0)
            a_norm(L, 0)
            a_memattn(L, 0)
            a_squares(L, "mo0", 1)
            a_norm(L, 1)
            a_ffn(L, 0)
            a_squares(L, "fo0", 2)
            a_norm(L, 2)
            a_qkv(L)
            a_attn(L)
            a_sattn(L)
            a_squares(L, "wo", 3)
            a_norm(L, 3)
            a_memattn(L, 1)
            a_squares(L, "mo1", 4)
            a_norm(L, 4)
            a_ffn(L, 1)
            a_out(L)

        @block.vector
        def _(vv):
            L = Lane(vv, "dve_done")
            vec(L)
            v_params_early(L)
            v_mem_norm(L)
            v_stats8(L)
            v_params(L)
            v_memkv(L, 0)
            for k in range(NB):
                v_norm8(L, k)
                v_ca(L, k)
                v_batch(L, k)
            v_final(L)
            v_glu(L)
            v_memkv(L, 1)
            v_norm(L, 0, lambda m: g_mem(0, m))
            v_memattn(L, 0)
            v_resid(L, "mo0")
            v_norm(L, 1, lambda m: g_ffn(0, m))
            v_ffn(L, 0)
            v_resid(L, "fo0")
            v_norm(L, 2, lambda m: g_mix(1, m))
            v_masks(L)
            v_qkv(L)
            v_attn(L)
            v_sattn(L)
            v_resid(L, "wo")
            v_norm(L, 3, lambda m: g_mem(1, m))
            v_memattn(L, 1)
            v_resid(L, "mo1")
            v_norm(L, 4, lambda m: g_ffn(1, m))
            v_ffn(L, 1)
            v_resid(L, "fo1")
            v_out(L)

        @block.tensor
        def _(pe):
            pe.wait_ge(S("consts_ready"), 1)
            pe_setup(pe)
            pe_memkv(pe, 0)
            for k in range(NB):
                pe_batch(pe, k)
            pe_final(pe)
            for f in range(2):
                for i in range(2):
                    landed(pe, ("yT", NB - 1, f, i))
            pe_resid(pe, "glu", 1, KT, hT)
            pe_memkv(pe, 1)
            pe_norm(pe, 0)
            pe_memattn(pe, 0)
            pe_norm(pe, 1)
            pe_ffn(pe, 0)
            pe_norm(pe, 2)
            pe_qkv(pe)
            pe_attn(pe)
            pe_sattn(pe)
            pe_resid(pe, "wo", 1, 4, hT)
            pe_norm(pe, 3)
            pe_memattn(pe, 1)
            pe_norm(pe, 4)
            pe_ffn(pe, 1)
            pe_out(pe)


_SWA_OUT = [(1, 1, 128, 8, 64)] * 2 + [(1, 1, 512, 8, 64)] * 4
_OUTS = ([(1, 512, 1024), (8, 4, 1024), (1, 1, 64, 64), (1, 1, 64, 64)] + _SWA_OUT
         + [(2, 1, 256, 4, 256)] * 2 + [(1, 8, 64, 64)] * 2 + [(1, 8, 4, 8, 64)] * 6)


def kernel(**inputs):
    import numpy as _np
    import concourse.bacc as _bacc
    from concourse import mybir as _mybir
    from concourse.bass_utils import run_bass_kernel_spmd as _run

    nc = _bacc.Bacc("TRN2", target_bir_lowering=False, num_devices=1)
    arrays, args = {}, {}
    for name, value in inputs.items():
        v = _np.ascontiguousarray(value)
        arrays[f"in_{name}_dram"] = v
        args[name] = nc.dram_tensor(f"in_{name}_dram", v.shape, _mybir.dt.from_np(v.dtype), kind="ExternalInput").ap()
    outs = [nc.dram_tensor(f"out_{i}_dram", shape, _mybir.dt.float32, kind="ExternalOutput").ap()
            for i, shape in enumerate(_OUTS)]
    hybrid_step(nc, args, outs)
    r = _run(nc, [arrays], core_ids=[0])
    return tuple(r.results[0][f"out_{i}_dram"] for i in range(len(_OUTS)))
```

```python
from contextlib import ExitStack

import numpy as np

import concourse.bass as bass
from concourse import mybir

F32 = mybir.dt.float32
F32R = mybir.dt.float32r
I32 = mybir.dt.int32
ALU = mybir.AluOpType
ACT = mybir.ActivationFunctionType
AX = mybir.AxisListType.X

P = 128
D = 1024
KT = D // P
SEQ, DB, DS = 512, 8, 4
NS = DB * DS
T = SEQ + NS
HT = T // 2
NM, MH, MD = 256, 4, 256
G, GC, GS = 64, 16, 64
CH = 8
NC = SEQ // CH
NCC = NC + DB
GP = G // 2
NB, BG = 4, 8
FF = 2816
FT = FF // P
SH, SD, SW = 8, 64, 512
NG = 3
RUNIT = 256
EPS = 1e-6
BIG = -1e30
UW = 11 * RUNIT


def hybrid_step(nc, a, o):
    with ExitStack() as ctx:
        names = {}

        def S(name):
            if name not in names:
                names[name] = ctx.enter_context(nc.semaphore(name))
            return names[name]

        class Lane:

            def __init__(self, eng, own):
                self.e, self.own, self.n, self.last = eng, own, {}, None

            def did(self, ins, sem=None):
                sem = sem or self.own
                ins.then_inc(S(sem), 1)
                self.n[sem] = self.n.get(sem, 0) + 1
                self.last = (sem, self.n[sem])

            def settle(self):
                if self.last:
                    self.e.wait_ge(S(self.last[0]), self.last[1])

            def need(self, sem, value):
                self.e.wait_ge(S(sem), value)

        at = {}

        def sb(name, n, dt=F32):
            at[name] = -(-nc.sbuf_base // 32) * 32
            return ctx.enter_context(nc.sbuf_tensor(name, [P, n], dt))

        def rounded(name, buf, n, first=0):
            return nc.alloc_sbuf_tensor_at(name, [P, n], F32R, offset=at[buf] + 4 * first)

        ps = ctx.enter_context(nc.psum_tensor("ps", [P, 8, 512], F32))
        ident = sb("ident", P)
        ones = sb("ones", P)
        epst = sb("epst", 1)
        gcol = sb("gcol", 96)
        xT = sb("xT", KT * T)[:].rearrange("p (k t) -> p k t", k=KT)
        hT = sb("hT", KT * T)[:].rearrange("p (k t) -> p k t", k=KT)
        ring = sb("ring", 2 * UW)
        mKT0 = sb("mKT", 2 * KT * NM)
        mV0 = sb("mV", 2 * 2 * D)
        mKT = mKT0[:].rearrange("p (l f m) -> p l f m", l=2, f=KT)
        mV = mV0[:].rearrange("p (l c n) -> p l c n", l=2, c=2)
        rstd = sb("rstd", T)
        AR = 26944
        arena = sb("arena", AR)

        class Space:
            def __init__(self, base, size, at=0):
                self.b, self.size, self.at = base, size, at

            def take(self, n, pat=None, **kw):
                v = self.b[:, self.at:self.at + n]
                self.at += n
                assert self.at <= self.size, (self.at, self.size)
                return v.rearrange(pat, **kw) if pat else v

        items, units = {}, {}

        def item(*key):
            items[key] = len(items)

        PIECES = FT + 16

        def piece(l, key):
            return PIECES * l + (key[0] if len(key) == 1 else FT + 4 * key[0] + 2 * key[1] + key[2])

        unit_end = {}

        def unit(*key):
            units[key] = len(units)

        def ends(n=None):
            m = len(items) - 1
            unit_end[len(units) - 1] = (f"bank_full{m % 8}", m // 8 + 1)

        def split_ends(q):
            unit_end[len(units) - 1] = (f"w_split{q % 2}", q // 2 + 1)

        def fill(pe, key):
            n = items[key]
            if n >= 8:
                pe.wait_ge(S(f"bank_free{n % 8}"), n // 8)
            return ps[:, n % 8, :]

        def filled(key, ins):
            ins.then_inc(S(f"bank_full{items[key] % 8}"), 1)

        def full(L, key):
            n = items[key]
            L.e.wait_ge(S(f"bank_full{n % 8}"), n // 8 + 1)
            return ps[:, n % 8, :]

        def free(L, key, ins):
            n = items[key]
            ins.then_inc(S(f"bank_free{n % 8}"), 1)
            L.last = (f"bank_free{n % 8}", n // 8 + 1)

        def landed(e, key):
            n = items[key]
            e.wait_ge(S(f"bank_free{n % 8}"), n // 8 + 1)

        def uslot(key, kt):
            n = units[key]
            return ring[:, (n % 2) * UW:(n % 2) * UW + kt * RUNIT].rearrange("p (k c) -> p k c", k=kt)

        def uready(pe, key):
            n = units[key]
            pe.wait_ge(S(f"w_full{n % 2}"), wcount(n))

        for i in range(3):
            item("par", i)
        for i in range(2):
            item("cT", i)
        for f in range(KT):
            item("xT", f)
        for f in range(2):
            item("xsT", f)

        def plan_memkv(l):
            for f in range(KT // 2):
                item("memT", l, f)
            for j in range(8):
                item("kv", l, j)
                unit("kv", l, j)
                ends()
                if 1 <= j <= 4:
                    item("mkT", l, j - 1)
        plan_memkv(0)
        for k in range(NB):
            for i in range(4):
                item("U", k, i)
            for i in range(4):
                item("Q", k, i)
            for i in range(4):
                item("W", k, i)
            for i in range(4):
                item("K", k, i)
            for i in range(4):
                item("Y", k, i)
            for f in range(2):
                for i in range(2):
                    item("yT", k, f, i)
        for i in range(2):
            item("fin", i)

        def plan_resid(name):
            for j in range(4):
                unit(name, j, 0)
                for m in range(2):
                    for h in range(2):
                        item(name, 2 * j + m, h)
                ends()
        plan_resid("glu")
        plan_memkv(1)

        def plan_norm(k):
            item("ssq", k, 0)
            item("ssq", k, 1)

        def plan_memattn(l):
            for h in range(MH):
                unit("mq", l, h)
                for i in range(3):
                    item("mq", l, h, i)
                ends()
                if h >= 1:
                    for i in range(3):
                        item("mqT", l, h - 1, i)
            for i in range(3):
                item("mqT", l, MH - 1, i)
            for h in range(MH + 1):
                if h < MH:
                    item("ms", l, h, 0)
                if h >= 1:
                    item("mp", l, h - 1, 0)
                    item("mp", l, h - 1, 1)
                if h < MH:
                    item("ms", l, h, 1)
                if h >= 1:
                    item("mo", l, h - 1, 0)
                    item("mo", l, h - 1, 1)
            for b in range(DB + 1):
                if b < DB:
                    for i in range(4):
                        item("skT", l, b, i)
                if b >= 1:
                    item("ssT", l, b - 1)
            item("ss", l)
            item("sp", l)
            item("so", l)
            plan_resid(f"mo{l}")

        def plan_ffn(l):
            for u in range(FT):
                unit("fi", l, u)
                for j in range(4):
                    item("fi", l, u, j)
                split_ends(piece(l, (u,)))
            for j in range(4):
                for s in range(2):
                    unit(f"fo{l}", j, s)
                    split_ends(piece(l, (j, s, 1)))
                for m in range(2):
                    for h in range(2):
                        item(f"fo{l}", 2 * j + m, h)

        def plan_swa():
            for u in range(18):
                unit("qkv", u)
                for i in range(3):
                    item("qkv", u, i)
                ends()
                if 1 <= u <= 12:
                    for i in range(3):
                        item("qkT", u - 1, i)
            for n in range(SH * 4 + 2):
                if n >= 2:
                    item("ap", n - 2, 0)
                    item("ap", n - 2, 1)
                if n < SH * 4:
                    item("as", n, 0)
                    item("as", n, 1)
                if n >= 2:
                    item("ao", n - 2)
            item("bn", 0)
            item("bn", 1)
            for b in range(DB + 1):
                if b < DB:
                    for i in range(7):
                        item("bkT", b, i)
                if b >= 1:
                    item("bs", b - 1)
            for R in range(2):
                item("br", R)
            for i in range(3):
                item("bp", i)
            for b in range(DB):
                item("bo", b)
            item("bo", "new")
            plan_resid("wo")

        plan_norm(0)
        plan_memattn(0)
        plan_norm(1)
        plan_ffn(0)
        plan_norm(2)
        plan_swa()
        plan_norm(3)
        plan_memattn(1)
        plan_norm(4)
        plan_ffn(1)
        for t in range(5):
            item("out", t, 0)
            item("out", t, 1)

        A = Space(arena, AR)
        x8 = A.take(CH * 256, "p (s n) -> p s n", s=CH)
        ub = A.take(CH * 256, "p (g s c) -> p g s c", g=16, s=CH)
        Ub = A.take(16 * NCC, "p (g n) -> p g n", g=16)
        CAr = A.take(BG * 9 * GC, "p (g t c) -> p g t c", g=BG, t=9)
        CAi = A.take(BG * 9 * GC, "p (g t c) -> p g t c", g=BG, t=9)
        QBr = A.take(BG * CH * GC, "p (g s c) -> p g s c", g=BG, s=CH)
        QBi = A.take(BG * CH * GC, "p (g s c) -> p g s c", g=BG, s=CH)
        Qt = A.take(2 * BG * P, "p (i g n) -> p i g n", i=2, g=BG)
        early = A.at
        Tt = A.take(16 * P, "p (g n) -> p g n", g=16)
        Kp = [mKT0[32 * h:32 * h + GC, KT * NM:KT * NM + 8 * 15 * GC].rearrange("p (g n) -> p g n", g=8)
              for h in range(2)]
        skip = mKT0[0:GC, KT * NM + 8 * 15 * GC:KT * NM + 8 * 15 * GC + 4 * GC].rearrange("p (g c) -> p g c", g=4)
        E0 = Space(arena, AR, early)
        Rr = A.take(GP * NC, "p (g n) -> p g n", g=GP)
        Ri = A.take(GP * NC, "p (g n) -> p g n", g=GP)
        Sr = A.take(BG * (NC + 1), "p (g n) -> p g n", g=BG)
        Si = A.take(BG * (NC + 1), "p (g n) -> p g n", g=BG)
        Bb = A.take(2 * GP * GC, "p (i g c) -> p i g c", i=2, g=GP)
        Ct = A.take(2 * GP * GC, "p (i g c) -> p i g c", i=2, g=GP)
        h0 = A.take(2 * GP * DB, "p (i g b) -> p i g b", i=2, g=GP)
        ws = A.take(2 * GP * DB, "p (i g b) -> p i g b", i=2, g=GP)
        tA = A.take(1024)
        tB = A.take(1024)
        apw = A.take(2 * 9 * GP, "p (i t g) -> p i t g", i=2, t=9)
        arev = A.take(2 * 8 * GP, "p (i t g) -> p i t g", i=2, t=8)
        prm = A.take(12 * GP, "p (i g) -> p i g", i=12)
        gainU = A.take(G)
        Dd = A.take(G)
        ss8 = A.take(NB * CH, "p (k s) -> p k s", k=NB)
        r8 = A.take(CH)
        mss = A.take(16)
        fst = A.take(2 * GP, "p (i g) -> p i g", i=2)
        CA = [(CAr, CAi), (A.take(BG * 9 * GC, "p (g t c) -> p g t c", g=BG, t=9),
                           ring[:, KT * RUNIT + CH * 256:KT * RUNIT + CH * 256 + BG * 9 * GC]
                           .rearrange("p (g t c) -> p g t c", g=BG, t=9))]
        yb = ring[:, KT * RUNIT:KT * RUNIT + CH * 256].rearrange("p (s n) -> p s n", s=CH)
        D0 = rstd[:, 0:BG * NC].rearrange("p (g n) -> p g n", g=BG)
        craw = E0.take(2 * 4 * P, "p (i t n) -> p i t n", i=2, t=4)
        braw = E0.take(2 * GP * GC, "p (i g c) -> p i g c", i=2, g=GP)
        lrow = E0.take(3 * P, "p (i n) -> p i n", i=3)
        prow = E0.take(P)
        hraw = E0.take(4 * P, "p (i n) -> p i n", i=4)
        lstep = E0.take(2)
        drow = E0.take(2 * GC)
        grep = E0.take(CH * GC, "p (s c) -> p s c", s=CH)
        hflat = hT.rearrange("p k t -> p (k t)")
        xnat = hflat[:, 0:4 * D].rearrange("p (t n) -> p t n", t=4)
        xsn = arena[:, CH * 256:CH * 256 + D]
        memT = mKT0[:, KT * NM:].rearrange("p (f m) -> p f m", f=KT)
        mnat = mV0[:, 2 * D:].rearrange("p (c n) -> p c n", c=2)
        mkg = sb("mkg", 2 * MD)
        kgb = sb("kgb", NG * SD)

        def g_mix(l, f):
            return gcol[:, 8 * l + f:8 * l + f + 1]

        def g_mem(l, f):
            return gcol[:, 16 + 8 * l + f:17 + 8 * l + f]

        def g_memin(l, f):
            return gcol[:, 32 + 8 * l + f:33 + 8 * l + f]

        def g_ffn(l, f):
            return gcol[:, 48 + 8 * l + f:49 + 8 * l + f]

        def g_mq(l, d):
            return gcol[:, 64 + 2 * l + d:65 + 2 * l + d]

        def b_glu(f):
            return gcol[:, 68 + f:69 + f]

        def g_sq(g):
            return gcol[:, 76 + g:77 + g]

        def half(h):
            return slice(HT * h, HT * h + HT)

        def load_unit(sp, src, key, kt, rows, cols):
            n = units[key]
            if n >= 2:
                sp.wait_ge(S(unit_end[n - 2][0]), unit_end[n - 2][1])
            sp.dma_start(uslot(key, kt), src[rows, cols].rearrange("(k p) n -> p k n", p=P)) \
              .then_inc(S(f"w_full{n % 2}"), 16)

        def cols(j):
            return slice(j * RUNIT, (j + 1) * RUNIT)

        def sp_params(sp):
            q = S("ld_par")
            for r, name in ((0, "norm_mix_g"), (16, "norm_mem_g"), (32, "norm_memin_g"), (48, "norm_ffn_g")):
                sp.dma_start(prow[r:r + 16, :], a[name].rearrange("l (k p) -> (l k) p", p=P)).then_inc(q, 16)
            sp.dma_start(prow[64:68, :], a["mem_q_norm_g"].rearrange("l (k p) -> (l k) p", p=P)).then_inc(q, 16)
            sp.dma_start(prow[68:76, :], a["ssm_b_glu"].rearrange("l (k p) -> (l k) p", p=P)).then_inc(q, 16)
            for i in range(2):
                sp.dma_start(prow[76:79, i * SD:(i + 1) * SD], a["attn_q_norm_g"][0]).then_inc(q, 16)
            sp.dma_start(lrow[0:GP, 0, :], a["ssm_lambda_re"][0].rearrange("(g r) p -> g (r p)", r=2)).then_inc(q, 16)
            sp.dma_start(lrow[0:GP, 1, :], a["ssm_lambda_im"][0].rearrange("(g r) p -> g (r p)", r=2)).then_inc(q, 16)
            sp.dma_start(lstep[0:GP, :], a["ssm_log_step"][0].rearrange("(g r) -> g r", r=2)).then_inc(q, 16)
            sp.dma_start(drow[0:G, 0:GC], a["ssm_d"][0].rearrange("(g c) -> g c", c=GC)).then_inc(q, 16)
            sp.dma_start(drow[0:G, GC:], a["norm_mix_g"][0].rearrange("(g c) -> g c", c=GC)).then_inc(q, 16)
            for i, name in enumerate(("ssm_b_re", "ssm_b_im")):
                for r in range(2):
                    sp.dma_start(braw[64 * r:64 * r + 64, i], a[name][0].rearrange("(g r) p c -> r p g c", r=2)[r]) \
                      .then_inc(q, 16)
            for i, name in enumerate(("state_ssm_re", "state_ssm_im")):
                v = a[name][0].rearrange("b (g r) p -> (b g) (r p)", r=2)
                for t in range(2):
                    sp.dma_start(hraw[:, 2 * i + t, :], v[P * t:P * t + P]).then_inc(q, 16)
            for i, name in enumerate(("ssm_c_re", "ssm_c_im")):
                v = a[name][0].rearrange("(t g r) c p -> t g r c p", t=4, r=2)
                for t in range(4):
                    for r in range(2):
                        sp.dma_start(craw[:, i, t, 64 * r:64 * r + 64], v[t, :, r]).then_inc(q, 16)

        N_PAR = 8 + 5 + 4 + 4 + 16

        def act_loads(sc):
            sc.dma_start(mnat, a["mem_prompt"][0].rearrange("(c p) n -> p c n", p=P)).then_inc(S("ld_mem"), 16)
            sc.dma_start(xnat, a["x_prompt"][0].rearrange("(t p) n -> p t n", p=P)).then_inc(S("ld_x"), 16)
            sc.dma_start(xsn[0:NS], a["x_sample"].rearrange("b t n -> (b t) n")).then_inc(S("ld_x"), 16)
            sc.dma_start(mkg[:], a["mem_k_norm_g"].rearrange("l n -> (l n)").unsqueeze(0).to_broadcast([P, 2 * MD])) \
              .then_inc(S("ld_bc"), 16)
            sc.dma_start(kgb[:], a["attn_k_norm_g"][0].rearrange("l n -> (l n)").unsqueeze(0)
                         .to_broadcast([P, NG * SD])).then_inc(S("ld_bc"), 16)

        xv = a["x_prompt"][0].rearrange("(c s) n -> c s n", s=CH)

        def sp_x8(sp, pas, k):
            n = pas * NB + k
            if 1 <= n <= NB:
                sp.wait_ge(S("x8_sq"), n)
            if n > NB:
                sp.wait_ge(S("x8_used"), n - NB)
            if n == 0:
                sp.wait_ge(S("x8_zero"), 1)
            sl = slice(256 * k, 256 * k + 256)
            sp.dma_start(x8[0:NC], xv[:, :, sl]).then_inc(S("ld_x8"), 16)
            sp.dma_start(x8[NC:NCC, DS:CH], a["x_sample"][:, :, sl]).then_inc(S("ld_x8"), 16)

        def x8_ready(e, pas, k):
            n = pas * NB + k
            e.wait_ge(S("ld_x8"), 32 * (n + 1))

        def sp_toeplitz(sp, k):
            for hf in range(2):
                landed(sp, ("K", k, 2 * hf))
                landed(sp, ("K", k, 2 * hf + 1))
                if hf == 0 and k > 0:
                    landed(sp, ("Y", k - 1, 3))
                for s in range(CH):
                    c = (CH - 1 - s) * GC
                    sp.dma_start(Tt[GC * s:GC * s + GC, 8 * hf:8 * hf + 8, :],
                                 Kp[hf][:, :, c:c + P]).then_inc(S(f"toep{hf}"), 16)

        def pool_consts(L):
            L.settle()
            L.did(nc.gpsimd.memset(ident[:], 0.0))
            L.settle()
            L.did(nc.gpsimd.affine_select(out=ident[:], in_=ident[:], compare_op=ALU.not_equal, fill=1.0, base=0,
                                          pattern=[[-1, P]], channel_multiplier=1), "ident_ready")
            L.settle()
            L.did(nc.gpsimd.memset(ones[:], 1.0))
            L.settle()
            L.did(nc.gpsimd.memset(epst[:], EPS))
            L.settle()
            L.did(nc.gpsimd.memset(x8[64:NCC, 0:DS, :], 0.0), "x8_zero")
            L.settle()
            L.did(nc.gpsimd.memset(Sr[:, :, 0:1], 0.0))
            L.settle()
            L.did(nc.gpsimd.memset(Si[:, :, 0:1], 0.0), "consts_ready")

        def vec(L):
            v = nc.vector

            def tt(out, x, y, op, sem=None, dep=True):
                if dep:
                    L.settle()
                L.did(v.tensor_tensor(out, x, y, op), sem)

            def ts(out, x, s1, s2, op0, op1=None, sem=None, dep=True):
                if dep:
                    L.settle()
                if op1 is None:
                    L.did(v.tensor_scalar(out, x, s1, None, op0), sem)
                else:
                    L.did(v.tensor_scalar(out, x, s1, s2, op0, op1), sem)

            def stt(out, x, s, y, op0, op1, sem=None, dep=True):
                if dep:
                    L.settle()
                L.did(v.scalar_tensor_tensor(out=out, in0=x, scalar=s, in1=y, op0=op0, op1=op1), sem)

            def cp(out, x, sem=None, dep=True):
                if dep:
                    L.settle()
                L.did(v.tensor_copy(out, x), sem)

            def recip(out, x, sem=None):
                L.settle()
                L.did(v.reciprocal(out, x), sem)

            def cmul(or_, oi, ar, ai, br, bi, t1, t2):
                tt(t1, ar, br, ALU.mult)
                tt(t2, ai, bi, ALU.mult, dep=False)
                tt(or_, t1, t2, ALU.subtract)
                tt(t1, ar, bi, ALU.mult)
                tt(t2, ai, br, ALU.mult, dep=False)
                tt(oi, t1, t2, ALU.add)

            L.tt, L.ts, L.stt, L.cp, L.recip, L.cmul = tt, ts, stt, cp, recip, cmul

        MAGIC = 1.5 * 2.0 ** 23
        LN2H = float(np.float32(0.693359375))
        LN2L = float(np.float32(np.log(2.0) - 0.693359375))

        def v_exp(L, out, x, n, r, ii):
            L.ts(r, x, 88.0, -87.0, ALU.min, ALU.max)
            L.ts(n, r, 1.0 / float(np.log(2.0)), MAGIC, ALU.mult, ALU.add)
            L.ts(n, n, -MAGIC, None, ALU.add)
            L.stt(r, n, -LN2H, r, ALU.mult, ALU.add)
            L.stt(r, n, -LN2L, r, ALU.mult, ALU.add)
            f = [1.0]
            for k in range(1, 9):
                f.append(f[-1] / k)
            L.ts(out, r, f[8], f[7], ALU.mult, ALU.add)
            for k in range(6, -1, -1):
                L.tt(out, out, r, ALU.mult)
                L.ts(out, out, f[k], None, ALU.add)
            L.ts(ii, n, 127.0, float(2 ** 23), ALU.add, ALU.mult)
            L.tt(out, out, ii.bitcast(F32), ALU.mult)

        TP1 = 6.28125
        TP2 = float(np.float32(np.floor((2 * np.pi - TP1) * 2.0 ** 21) / 2.0 ** 21))
        TP3 = float(np.float32(2 * np.pi - TP1 - TP2))

        def v_sincos(L, sn, cs, x, n, r, r2):
            L.ts(n, x, float(1 / (2 * np.pi)), MAGIC, ALU.mult, ALU.add)
            L.ts(n, n, -MAGIC, None, ALU.add)
            L.stt(r, n, -TP1, x, ALU.mult, ALU.add)
            L.stt(r, n, -TP2, r, ALU.mult, ALU.add)
            L.stt(r, n, -TP3, r, ALU.mult, ALU.add)
            L.ts(r, r, 0.5, None, ALU.mult)
            L.tt(r2, r, r, ALU.mult)
            fac = [1.0]
            for k in range(1, 18):
                fac.append(fac[-1] * k)
            sc = [(-1) ** k / fac[2 * k + 1] for k in range(8)]
            cc = [(-1) ** k / fac[2 * k] for k in range(9)]
            for out, c in ((sn, sc), (cs, cc)):
                L.ts(out, r2, c[-1], None, ALU.mult)
                for k in range(len(c) - 2, 0, -1):
                    L.stt(out, out, c[k], r2, ALU.add, ALU.mult)
                L.ts(out, out, c[0], None, ALU.add)
            L.tt(sn, sn, r, ALU.mult)
            L.tt(cs, cs, sn, ALU.mult)
            L.tt(r2, sn, sn, ALU.mult)
            L.ts(sn, cs, 2.0, None, ALU.mult)
            L.ts(cs, r2, -2.0, 1.0, ALU.mult, ALU.add)

        def v_params_early(L):
            L.need("ld_par", 16 * N_PAR)
            L.cp(lrow[0:GP, 2, :].rearrange("g (r p) -> g r p", r=2),
                 lstep[0:GP, :].unsqueeze(2).to_broadcast([GP, 2, GS]), dep=False)
            L.cp(grep[0:G], drow[0:G, GC:].unsqueeze(1).to_broadcast([G, CH, GC]), "par_rows", dep=False)

        def v_params_turned(L):
            b = full(L, ("par", 0))
            free(L, ("par", 0), nc.vector.tensor_copy(gcol[:, 0:79], b[:, 0:79]))
            b = full(L, ("par", 1))
            lr, li, st = [prm[:, i] for i in range(3)]
            L.cp(lr, b[:, 0:GP], dep=False)
            L.cp(li, b[:, GP:2 * GP], dep=False)
            L.cp(st, b[:, 2 * GP:3 * GP], dep=False)
            L.cp(gainU, b[:, 96:160], dep=False)
            free(L, ("par", 1), nc.vector.tensor_copy(Dd[0:GC], b[0:GC, 160:224]))
            b = full(L, ("par", 2))
            for i in range(2):
                L.did(nc.vector.tensor_copy(h0[:, i].rearrange("p g b -> p b g"),
                                            b[:, 256 * i:256 * i + 256].rearrange("p (b g) -> p b g", b=DB)))
            free(L, ("par", 2), nc.vector.memset(tA[:, 0:1], 0.0))
            for i in range(2):
                b = full(L, ("cT", i))
                free(L, ("cT", i), nc.vector.tensor_copy(Ct[:, i].rearrange("p g c -> p (g c)"), b[:, :]))

        def v_params(L):
            lr, li, st, th, mg, sn, cs, t1, t2, t3, fr, fi = [prm[:, i] for i in range(12)]
            v_exp(L, st, st, t1, t2, t3.bitcast(I32))
            L.tt(th, li, st, ALU.mult)
            L.tt(t3, lr, st, ALU.mult)
            v_exp(L, mg, t3, t1, t2, fr.bitcast(I32))
            v_sincos(L, sn, cs, th, t1, t2, t3)

        def v_powers(L):
            mg, sn, cs = [prm[:, i] for i in (4, 5, 6)]
            L.settle()
            L.did(nc.vector.memset(apw[:, 0, 0], 1.0))
            L.did(nc.vector.memset(apw[:, 1, 0], 0.0))
            L.tt(apw[:, 0, 1], mg, cs, ALU.mult)
            L.tt(apw[:, 1, 1], mg, sn, ALU.mult)
            for k in (1, 2, 4):
                w = tA[:, 0:k * GP].rearrange("p (t g) -> p t g", t=k)
                w2 = tB[:, 0:k * GP].rearrange("p (t g) -> p t g", t=k)
                L.cmul(apw[:, 0, k + 1:2 * k + 1], apw[:, 1, k + 1:2 * k + 1],
                       apw[:, 0, 1:k + 1], apw[:, 1, 1:k + 1],
                       apw[:, 0, k].unsqueeze(1).to_broadcast([P, k, GP]),
                       apw[:, 1, k].unsqueeze(1).to_broadcast([P, k, GP]), w, w2)
            for s in range(8):
                L.cp(arev[:, 0, s], apw[:, 0, 7 - s], dep=(s == 0))
                L.cp(arev[:, 1, s], apw[:, 1, 7 - s], dep=False)

        def v_bbar(L):
            lr, li = prm[:, 0], prm[:, 1]
            t1, t2, t3, fr, fi = [prm[:, i] for i in range(7, 12)]
            L.tt(t1, lr, lr, ALU.mult)
            L.tt(t2, li, li, ALU.mult)
            L.tt(t1, t1, t2, ALU.add)
            L.recip(t3, t1)
            L.ts(t1, apw[:, 0, 1], -1.0, None, ALU.add)
            L.tt(fr, t1, lr, ALU.mult)
            L.tt(t2, apw[:, 1, 1], li, ALU.mult)
            L.tt(fr, fr, t2, ALU.add)
            L.tt(fr, fr, t3, ALU.mult)
            L.tt(fi, apw[:, 1, 1], lr, ALU.mult)
            L.tt(t2, t1, li, ALU.mult)
            L.tt(fi, fi, t2, ALU.subtract)
            L.tt(fi, fi, t3, ALU.mult)
            frb = fr.unsqueeze(2).to_broadcast([P, GP, GC])
            fib = fi.unsqueeze(2).to_broadcast([P, GP, GC])
            w = tA[:, 0:512].rearrange("p (g c) -> p g c", g=GP)
            w2 = tB[:, 0:512].rearrange("p (g c) -> p g c", g=GP)
            L.cmul(Bb[:, 0], Bb[:, 1], braw[:, 0], braw[:, 1], frb, fib, w, w2)
            L.settle()
            L.did(nc.vector.memset(tA[:, 0:1], 0.0), "bbar_ready")

        def v_decay(L):
            mg, sn, cs, t1, t2, t3 = [prm[:, i] for i in range(4, 10)]
            for _ in range(3):
                L.tt(mg, mg, mg, ALU.mult)

            def square():
                L.tt(t1, cs, cs, ALU.mult)
                L.tt(t2, sn, sn, ALU.mult)
                L.tt(t3, cs, sn, ALU.mult)
                L.tt(cs, t1, t2, ALU.subtract)
                L.ts(sn, t3, 2.0, None, ALU.mult)
            for _ in range(3):
                square()

        def v_rotations(L):
            cs, sn, t1, t2, t3 = [prm[:, i] for i in (6, 5, 7, 8, 9)]

            def square():
                L.tt(t1, cs, cs, ALU.mult)
                L.tt(t2, sn, sn, ALU.mult)
                L.tt(t3, cs, sn, ALU.mult)
                L.tt(cs, t1, t2, ALU.subtract)
                L.ts(sn, t3, 2.0, None, ALU.mult)
            L.settle()
            L.did(nc.vector.memset(Rr[:, :, 0:1], 1.0))
            L.did(nc.vector.memset(Ri[:, :, 0:1], 0.0))
            for j in range(6):
                k = 1 << j
                w = tA[:, 0:k * GP].rearrange("p (g n) -> p g n", g=GP)
                w2 = tB[:, 0:k * GP].rearrange("p (g n) -> p g n", g=GP)
                L.cmul(Rr[:, :, k:2 * k], Ri[:, :, k:2 * k], Rr[:, :, 0:k], Ri[:, :, 0:k],
                       cs.unsqueeze(2).to_broadcast([P, GP, k]), sn.unsqueeze(2).to_broadcast([P, GP, k]), w, w2)
                if j < 5:
                    square()

        def pool_qb(L, k):
            gs = slice(BG * k, BG * k + BG)
            if k == 0:
                L.need("bbar_ready", 1)
            else:
                landed(L.e, ("Q", k - 1, 3))
            g = nc.gpsimd
            t = pt[:].rearrange("p (g s c) -> p g s c", g=4, s=CH)
            for q in range(2):
                g4 = slice(4 * q, 4 * q + 4)
                G4 = slice(BG * k + 4 * q, BG * k + 4 * q + 4)
                B = [Bb[:, i, G4].unsqueeze(2).to_broadcast([P, 4, CH, GC]) for i in range(2)]
                R = [arev[:, i, :, G4].rearrange("p t g -> p g t").unsqueeze(3).to_broadcast([P, 4, CH, GC])
                     for i in range(2)]
                L.settle()
                L.did(g.tensor_tensor(QBr[:, g4], R[0], B[0], ALU.mult))
                L.settle()
                L.did(g.tensor_tensor(t, R[1], B[1], ALU.mult))
                L.settle()
                L.did(g.tensor_tensor(QBr[:, g4], QBr[:, g4], t, ALU.subtract))
                L.settle()
                L.did(g.tensor_tensor(QBi[:, g4], R[0], B[1], ALU.mult))
                L.settle()
                L.did(g.tensor_tensor(t, R[1], B[0], ALU.mult))
                L.settle()
                L.did(g.tensor_tensor(QBi[:, g4], QBi[:, g4], t, ALU.add), "qb_ready" if q else None)

        pt = sb("pt", 512)

        def v_ca(L, k):
            gs = slice(BG * k, BG * k + BG)
            C = [Ct[:, i, gs].unsqueeze(2).to_broadcast([P, BG, 9, GC]) for i in range(2)]
            R = [apw[:, i, :, gs].rearrange("p t g -> p g t").unsqueeze(3).to_broadcast([P, BG, 9, GC])
                 for i in range(2)]
            CAr, CAi = CA[k % 2]
            if k >= 2:
                landed(L.e, ("Y", k - 2, 3))
            for t0, t1 in ((0, 5), (5, 9)):
                n = t1 - t0
                w = tA[:, 0:BG * n * GC].rearrange("p (g t c) -> p g t c", g=BG, t=n)
                c0, c1, a0, a1 = [x[:, :, t0:t1] for x in (C[0], C[1], R[0], R[1])]
                o0, o1 = CAr[:, :, t0:t1], CAi[:, :, t0:t1]
                L.tt(o0, c0, a0, ALU.mult, dep=(t0 == 0))
                L.tt(w, c1, a1, ALU.mult)
                L.tt(o0, o0, w, ALU.subtract)
                L.tt(o1, c0, a1, ALU.mult, dep=False)
                L.tt(w, c1, a0, ALU.mult)
                L.settle()
                L.did(nc.vector.scalar_tensor_tensor(out=o1.rearrange("p g t c -> p g (t c)"),
                                                     in0=o1.rearrange("p g t c -> p g (t c)"), scalar=-1.0,
                                                     in1=w.rearrange("p g t c -> p g (t c)"),
                                                     op0=ALU.mult, op1=ALU.subtract),
                      "ca_ready" if t1 == 9 else None)

        def v_stats8(L):
            L.need("ss8_ready", 1)
            L.settle()
            L.did(nc.vector.tensor_reduce(r8[0:NCC], ss8[0:NCC].rearrange("p k s -> p s k"), AX, ALU.add))
            L.ts(r8[0:NCC], r8[0:NCC], 1.0 / D, EPS, ALU.mult, ALU.add, sem="r8_ms")

        def v_norm8(L, k):
            if k == 0:
                L.need("r8_sqrt", 1)
                L.recip(r8[0:NCC], r8[0:NCC])
                landed(L.e, ("xsT", 1))
            else:
                full(L, ("U", k - 1, 3))
            x8_ready(L.e, 1, k)
            L.settle()
            for s in range(CH):
                ins = nc.vector.tensor_scalar(ub[0:NCC, :, s, :],
                                              x8[0:NCC, s, :].rearrange("p (g c) -> p g c", g=16),
                                              r8[0:NCC, s:s + 1], None, ALU.mult)
                L.did(ins, "x8_used" if s == CH - 1 else None)

        def v_batch(L, k):
            gs = slice(BG * k, BG * k + BG)
            for i in range(4):
                b = full(L, ("U", k, i))
                g0 = 16 * k + 4 * i
                free(L, ("U", k, i), nc.vector.tensor_tensor(
                    Ub[:, 4 * i:4 * i + 4, :], b[:, 0:4 * NCC].rearrange("p (g n) -> p g n", g=4),
                    gainU[:, g0:g0 + 4].unsqueeze(2).to_broadcast([P, 4, NCC]), ALU.mult))
            for i in (0, 2):
                b = full(L, ("Q", k, i))
                free(L, ("Q", k, i), nc.vector.tensor_copy(
                    Qt[:, i // 2, 4 * (i % 2):4 * (i % 2) + 4].rearrange("p g n -> p (g n)"), b[:, :]))
            if k == 0:
                v_ca(L, k)
                L.need("consts_ready", 1)
                full(L, ("kv", 0, 7))
                L.settle()
                for h in range(2):
                    L.did(nc.vector.memset(Kp[h][:, :, 0:7 * GC], 0.0))

            def taps(h):
                if k > 0:
                    L.need(f"toep{h}", 16 * CH * k)
                for i in (2 * h, 2 * h + 1):
                    o4 = Kp[h][:, i % 2::2]
                    g0 = 16 * k + 8 * h + i % 2
                    L.tt(skip, ident[0:GC, 0:GC].unsqueeze(1).to_broadcast([GC, 4, GC]),
                         Dd[0:GC, g0:g0 + 7:2].unsqueeze(2).to_broadcast([GC, 4, GC]), ALU.mult)
                    b = full(L, ("K", k, i))
                    L.need("taps_copied", 4 * k + i + 1)
                    L.settle()
                    free(L, ("K", k, i), nc.vector.tensor_tensor(
                        o4[:, :, 7 * GC:8 * GC], b[0:GC, :].rearrange("p (g n) -> p g n", g=4)[:, :, 0:GC], skip,
                        ALU.add))
            L.cp(D0, prm[:, 4, gs].unsqueeze(2).to_broadcast([P, BG, NC]))
            L.settle()
            L.did(nc.vector.memset(D0[:, :, 0:1], 0.0))
            W = [full(L, ("W", k, i))[:, 0:4 * NCC].rearrange("p (g n) -> p g n", g=4) for i in range(4)]
            fr_, fi_ = tA[:, 0:512].rearrange("p (g n) -> p g n", g=BG), tA[:, 512:].rearrange("p (g n) -> p g n", g=BG)
            w_, w2_ = tB[:, 0:512].rearrange("p (g n) -> p g n", g=BG), tB[:, 512:].rearrange("p (g n) -> p g n", g=BG)
            for q in range(2):
                wr, wi = W[2 * q], W[2 * q + 1]
                g4 = slice(4 * q, 4 * q + 4)
                G4 = slice(BG * k + 4 * q, BG * k + 4 * q + 4)
                L.tt(fr_[:, g4], wr[:, :, 0:NC], Rr[:, G4], ALU.mult)
                L.tt(w_[:, g4], wi[:, :, 0:NC], Ri[:, G4], ALU.mult)
                L.tt(fi_[:, g4], wi[:, :, 0:NC], Rr[:, G4], ALU.mult)
                L.tt(w2_[:, g4], wr[:, :, 0:NC], Ri[:, G4], ALU.mult)
                free(L, ("W", k, 2 * q), nc.vector.tensor_copy(ws[:, 0, G4], wr[:, :, NC:]))
                free(L, ("W", k, 2 * q + 1), nc.vector.tensor_copy(ws[:, 1, G4], wi[:, :, NC:]))
            L.tt(fr_, fr_, w_, ALU.add)
            L.tt(fi_, fi_, w2_, ALU.subtract)
            D0f = D0.rearrange("p g n -> p (g n)")
            L.settle()
            L.did(nc.vector.tensor_tensor_scan(tB[:, 0:512], D0f, tA[:, 0:512], 0.0, ALU.mult, ALU.add))
            L.did(nc.vector.tensor_tensor_scan(tB[:, 512:], D0f, tA[:, 512:], 0.0, ALU.mult, ALU.add))
            taps(0)
            L.tt(fr_, w_, Rr[:, gs], ALU.mult)
            L.tt(fi_, w2_, Ri[:, gs], ALU.mult)
            L.tt(Sr[:, :, 1:], fr_, fi_, ALU.subtract)
            L.tt(fr_, w_, Ri[:, gs], ALU.mult)
            L.tt(fi_, w2_, Rr[:, gs], ALU.mult)
            L.tt(Si[:, :, 1:], fr_, fi_, ALU.add, sem="states_ready")
            taps(1)
            L.cp(fst[:, 0, gs], Sr[:, :, NC])
            L.cp(fst[:, 1, gs], Si[:, :, NC])

        def a_batch(L, k):
            s = nc.scalar
            for i in (1, 3):
                b = full(L, ("Q", k, i))
                free(L, ("Q", k, i), s.activation(
                    Qt[:, i // 2, 4 * (i % 2):4 * (i % 2) + 4].rearrange("p g n -> p (g n)"), b[:, :], ACT.Copy))
            for i in range(4):
                if k > 0:
                    L.need(f"toep{i // 2}", 16 * CH * k)
                b = full(L, ("K", k, i))
                L.did(s.activation(Kp[i // 2][:, i % 2::2, 8 * GC:],
                                   b[0:GC, :].rearrange("p (g n) -> p g n", g=4)[:, :, GC:], ACT.Copy), "taps_copied")
            for i in range(4):
                b = full(L, ("Y", k, i))
                free(L, ("Y", k, i), s.activation(
                    yb[0:NCC, :, P * (i // 2):P * (i // 2) + P].rearrange("p s (g r c) -> p g s r c", g=4,
                                                                          r=2)[:, :, :, i % 2],
                    b[0:NCC, :].rearrange("p (g s c) -> p g s c", g=4, s=CH), ACT.Gelu_apprx_tanh))
            for f in range(2):
                for q in range(2):
                    b = full(L, ("yT", k, f, q))
                    v4 = b[:, 0:4 * NCC].rearrange("p (s n) -> p s n", s=4)
                    ft = 2 * k + f
                    ins = s.activation(hT[:, ft, 0:SEQ].rearrange("p (c s) -> p s c", s=CH)[:, 4 * q:4 * q + 4],
                                       v4[:, :, 0:NC], ACT.Copy)
                    if q == 0:
                        free(L, ("yT", k, f, q), ins)
                    else:
                        L.did(ins)
                        free(L, ("yT", k, f, q), s.activation(
                            hT[:, ft, SEQ:].rearrange("p (b s) -> p s b", s=DS), v4[:, :, NC:], ACT.Copy))

        def a_stats_mem(L):
            s = nc.scalar
            L.need("ld_mem", 16)
            for c in range(8):
                L.settle()
                L.did(s.activation(scr[:], mnat[:, c // 4, 256 * (c % 4):256 * (c % 4) + 256], ACT.Square,
                                   accum_out=mss[:, c:c + 1]))
            L.settle()
            L.did(s.activation(scr[0:1, 0:1], epst[0:1], ACT.Copy), "mss_ready")
            L.need("mss_ms", 1)
            L.did(s.activation(mss[:, 8:10], mss[:, 8:10], ACT.Sqrt), "mss_sqrt")

        def a_stats8(L, k):
            s = nc.scalar
            x8_ready(L.e, 0, k)
            for i in range(CH):
                L.settle()
                L.did(s.activation(scr[0:NCC, 0:256], x8[0:NCC, i], ACT.Square, accum_out=ss8[0:NCC, k, i:i + 1]),
                      ("x8_sq" if i == CH - 1 else None))
            if k == NB - 1:
                L.settle()
                L.did(s.activation(scr[0:1, 0:1], epst[0:1], ACT.Copy), "ss8_ready")

        def a_root8(L):
            L.need("r8_ms", 1)
            L.did(nc.scalar.activation(r8[0:NCC], r8[0:NCC], ACT.Sqrt), "r8_sqrt")

        scr = sb("scr", 256)

        def pe_setup(pe):
            t = nc.tensor
            pe.wait_ge(S("ident_ready"), 1)
            pe.wait_ge(S("par_rows"), 1)
            pe.wait_ge(S("ld_par"), 16 * N_PAR)
            b = fill(pe, ("par", 0))
            filled(("par", 0), t.transpose(b[:, 0:79], prow[0:79, :], ident[0:79, 0:79]))
            b = fill(pe, ("par", 1))
            for i in range(3):
                t.transpose(b[:, GP * i:GP * i + GP], lrow[0:GP, i, :], ident[0:GP, 0:GP])
            t.transpose(b[:, 96:160], grep[0:G].rearrange("p s c -> p (s c)"), ident[0:G, 0:G])
            filled(("par", 1), t.transpose(b[0:GC, 160:224], drow[0:G, 0:GC], ident[0:G, 0:G]))
            b = fill(pe, ("par", 2))
            for i in range(4):
                ins = t.transpose(b[:, P * i:P * i + P], hraw[:, i, :], ident[:])
            filled(("par", 2), ins)
            for i in range(2):
                b = fill(pe, ("cT", i))
                for q in range(4):
                    ins = t.transpose(b[:, P * q:P * q + P], craw[:, i, q, :], ident[:])
                filled(("cT", i), ins)
            pe.wait_ge(S("ld_x"), 32)
            for f in range(KT):
                b = fill(pe, ("xT", f))
                for q in range(4):
                    ins = t.transpose(b[:, P * q:P * q + P], xnat[:, q, P * f:P * f + P], ident[:])
                filled(("xT", f), ins)
            for f2 in range(2):
                b = fill(pe, ("xsT", f2))
                for f in range(4):
                    ins = t.transpose(b[:, NS * f:NS * f + NS], xsn[0:NS, P * (4 * f2 + f):P * (4 * f2 + f) + P],
                                      ident[0:NS, 0:NS])
                filled(("xsT", f2), ins)

        def a_xT(L):
            for f in range(KT):
                b = full(L, ("xT", f))
                free(L, ("xT", f), nc.scalar.activation(xT[:, f, 0:SEQ], b[:, :], ACT.Copy))
            for q in range(2):
                b = full(L, ("xsT", q))
                free(L, ("xsT", q), nc.scalar.activation(xT[:, 4 * q:4 * q + 4, SEQ:],
                                                         b[:, 0:4 * NS].rearrange("p (f n) -> p f n", f=4), ACT.Copy))

        def pe_batch(pe, k):
            t = nc.tensor
            CAr, CAi = CA[k % 2]
            pe.wait_ge(S("x8_used"), k + 1)
            for i in range(4):
                b = fill(pe, ("U", k, i))
                for g in range(4):
                    ins = t.transpose(b[:, NCC * g:NCC * g + NCC],
                                      ub[0:NCC, 4 * i + g].rearrange("p s c -> p (s c)"), ident[0:NCC, 0:NCC])
                filled(("U", k, i), ins)
            pe.wait_ge(S("qb_ready"), k + 1)
            for i in range(4):
                b = fill(pe, ("Q", k, i))
                for g in range(4):
                    ins = t.transpose(b[:, P * g:P * g + P],
                                      (QBr, QBi)[i // 2][:, 4 * (i % 2) + g].rearrange("p s c -> p (s c)"), ident[:])
                filled(("Q", k, i), ins)
            for i in range(4):
                landed(pe, ("Q", k, i))
                landed(pe, ("U", k, i))
            for i in range(4):
                b = fill(pe, ("W", k, i))
                for g in range(4):
                    gp = 4 * (i // 2) + g
                    for r in range(2):
                        ins = t.matmul(b[64 * r:64 * r + 64, NCC * g:NCC * g + NCC],
                                       Qt[:, i % 2, gp, 64 * r:64 * r + 64], Ub[:, 2 * gp + r, :],
                                       start=True, stop=True)
                filled(("W", k, i), ins)
            pe.wait_ge(S("ca_ready"), k + 1)
            pe.wait_ge(S("bbar_ready"), 1)
            for i in range(4):
                b = fill(pe, ("K", k, i))
                for g in range(4):
                    gp, r = 4 * (i // 2) + g, i % 2
                    q = slice(64 * r, 64 * r + 64)
                    for j, ca in enumerate((CAr, CAi)):
                        ins = t.matmul(b[0:GC, P * g:P * g + P], Bb[q, j, BG * k + gp, :],
                                       ca[q, gp, 0:CH].rearrange("p t c -> p (t c)"), start=(j == 0), stop=(j == 1))
                filled(("K", k, i), ins)
            if k == 0:
                landed(pe, ("par", 2))
            pe.wait_ge(S("states_ready"), k + 1)
            for i in range(4):
                if i % 2 == 0:
                    pe.wait_ge(S(f"toep{i // 2}"), 16 * CH * (k + 1))
                b = fill(pe, ("Y", k, i))
                for g in range(4):
                    gp, r = 4 * (i // 2) + g, i % 2
                    n = 2 * gp + r
                    q = slice(64 * r, 64 * r + 64)
                    t.matmul(b[0:NCC, P * g:P * g + P], Ub[:, n, :], Tt[:, n, :], start=True, stop=False,
                             skip_group_check=True)
                    for j, (s_, ca) in enumerate(((Sr, CAr), (Si, CAi))):
                        t.matmul(b[0:NC, P * g:P * g + P], s_[q, gp, 0:NC],
                                 ca[q, gp, 1:9].rearrange("p t c -> p (t c)"), start=False, stop=False,
                                 skip_group_check=True)
                        ins = t.matmul(b[NC:NCC, P * g + 64:P * g + P], h0[q, j, BG * k + gp, :],
                                       ca[q, gp, 1:5].rearrange("p t c -> p (t c)"), start=False, stop=(j == 1),
                                       skip_group_check=True)
                filled(("Y", k, i), ins)
            for i in range(4):
                landed(pe, ("Y", k, i))
            for f in range(2):
                for q in range(2):
                    b = fill(pe, ("yT", k, f, q))
                    for s in range(4):
                        ins = t.transpose(b[:, NCC * s:NCC * s + NCC],
                                          yb[0:NCC, 4 * q + s, P * f:P * f + P], ident[0:NCC, 0:NCC])
                    filled(("yT", k, f, q), ins)

        def v_final(L):
            m, w, w2 = [x.rearrange("p (g b) -> p g b", g=GP) for x in (tA[:, 0:256], tA[:, 256:512], tA[:, 512:768])]
            a4 = [apw[:, i, 4].unsqueeze(2).to_broadcast([P, GP, DB]) for i in range(2)]
            L.cmul(m, w2, h0[:, 0], h0[:, 1], a4[0], a4[1], w, tB[:, 0:256].rearrange("p (g b) -> p g b", g=GP))
            L.tt(ws[:, 0], ws[:, 0], m, ALU.add)
            L.tt(ws[:, 1], ws[:, 1], w2, ALU.add)
            L.cp(tB[:, 0:256].rearrange("p (b g) -> p g b", b=DB), ws[:, 0])
            L.cp(tB[:, 256:512].rearrange("p (b g) -> p g b", b=DB), ws[:, 1], sem="fin_ready")
            b = full(L, ("fin", 0))
            free(L, ("fin", 0), nc.vector.tensor_copy(tA[0:GP, 0:2 * P], b[0:GP, 0:2 * P]))
            b = full(L, ("fin", 1))
            free(L, ("fin", 1), nc.vector.tensor_copy(tA[:, 2 * P:6 * P], b[:, :]))

        def pe_final(pe):
            t = nc.tensor
            pe.wait_ge(S("fin_ready"), 1)
            b = fill(pe, ("fin", 0))
            for i in range(2):
                ins = t.transpose(b[0:GP, P * i:P * i + P], fst[:, i], ident[:])
            filled(("fin", 0), ins)
            b = fill(pe, ("fin", 1))
            for i in range(4):
                ins = t.transpose(b[:, P * i:P * i + P], tB[:, P * i:P * i + P], ident[:])
            filled(("fin", 1), ins)

        def sp_final(sp):
            q = S("out")
            landed(sp, ("fin", 0))
            for i in range(2):
                sp.dma_start(o[2 + i][0, 0].rearrange("(g r) p -> g (r p)", r=2), tA[0:GP, P * i:P * i + P]) \
                  .then_inc(q, 16)
            landed(sp, ("fin", 1))
            for i in range(2):
                v = o[12 + i][0].rearrange("b (g r) p -> (b g) (r p)", r=2)
                for t in range(2):
                    sp.dma_start(v[P * t:P * t + P], tA[:, P * (2 + 2 * i + t):P * (3 + 2 * i + t)]).then_inc(q, 16)
            n_out[0] += 6

        n_out = [0]
        sq = arena[:, 0:KT * T].rearrange("p (k t) -> p k t", k=KT)
        memT1 = arena[:, 4352:4352 + KT * NM].rearrange("p (f m) -> p f m", f=KT)
        kk = sb("kk", 1024)
        kraw = kk[:, 0:512].rearrange("p (c n) -> p c n", c=2)
        kout = kk[:, 512:1024].rearrange("p (c n) -> p c n", c=2)
        st = sb("st", 64)

        def mT(l):
            return (memT, memT1)[l]

        def v_mem_norm(L):
            L.need("mss_ready", 1)
            L.did(nc.vector.tensor_reduce(mss[:, 8:10], mss[:, 0:8].rearrange("p (c k) -> p c k", c=2), AX, ALU.add))
            L.ts(mss[:, 8:10], mss[:, 8:10], 1.0 / D, EPS, ALU.mult, ALU.add, sem="mss_ms")
            L.need("mss_sqrt", 1)
            L.recip(mss[:, 8:10], mss[:, 8:10])
            L.settle()
            for c in range(2):
                L.did(nc.vector.tensor_scalar(mnat[:, c], mnat[:, c], mss[:, 8 + c:9 + c], None, ALU.mult),
                      "mnat_ready" if c else None)

        def pe_memkv(pe, l):
            t = nc.tensor
            pe.wait_ge(S("mnat_ready"), 1)
            for f2 in range(KT // 2):
                b = fill(pe, ("memT", l, f2))
                for q in range(4):
                    f, c = 2 * f2 + q // 2, q % 2
                    ins = t.transpose(b[:, P * q:P * q + P], mnat[:, c, P * f:P * f + P], ident[:])
                filled(("memT", l, f2), ins)
            for f2 in range(KT // 2):
                landed(pe, ("memT", l, f2))
            for j in range(8):
                b = fill(pe, ("kv", l, j))
                uready(pe, ("kv", l, j))
                w = uslot(("kv", l, j), KT)
                for c in range(2):
                    for k in range(KT):
                        ins = t.matmul(b[:, 256 * c:256 * c + 256], mT(l)[:, k, P * c:P * c + P], w[:, k, :],
                                       start=(k == 0), stop=(k == KT - 1))
                filled(("kv", l, j), ins)
                if 1 <= j <= 4:
                    pe.wait_ge(S("mk_ready"), 4 * l + j)
                    b = fill(pe, ("mkT", l, j - 1))
                    for q in range(4):
                        ins = t.transpose(b[:, P * q:P * q + P], kout[:, q % 2, P * (q // 2):P * (q // 2) + P], ident[:])
                    filled(("mkT", l, j - 1), ins)

        def a_memkv(L, l):
            s = nc.scalar
            if l == 0:
                landed(L.e, ("par", 0))
            for f2 in range(KT // 2):
                b = full(L, ("memT", l, f2))
                L.did(s.activation(mT(l)[:, 2 * f2], b[:, 0:256], ACT.Copy, scale=g_memin(l, 2 * f2)))
                free(L, ("memT", l, f2), s.activation(mT(l)[:, 2 * f2 + 1], b[:, 256:512], ACT.Copy,
                                                      scale=g_memin(l, 2 * f2 + 1)))
            for j in range(8):
                if l == 1 and j == 4:
                    a_squares(L, "glu", 0)
                elif l == 0 and j == 5:
                    a_root8(L)
                b = full(L, ("kv", l, j))
                if j < 4:
                    if 4 * l + j > 0:
                        L.need("mk_ready", 4 * l + j)
                    free(L, ("kv", l, j), s.activation(kraw.rearrange("p c n -> p (c n)"), b[:, :], ACT.Copy))
                    L.settle()
                    for c in range(2):
                        L.settle()
                        L.did(s.activation(scr[:], kraw[:, c], ACT.Square, accum_out=st[:, c:c + 1]))
                    L.settle()
                    L.did(s.activation(st[:, 2:4], st[:, 0:2], ACT.Sqrt, bias=epst[:], scale=1.0 / MD), "mk_sqrt")
                    if l == 0:
                        a_stats8(L, j)
                else:
                    jj = j - 4
                    free(L, ("kv", l, j), s.activation(
                        mV[:, l, :, 256 * jj:256 * jj + 256], b[:, :].rearrange("p (c n) -> p c n", c=2), ACT.Copy))

        def v_memkv(L, l, between=()):
            v = nc.vector
            for j in range(4):
                L.need("mk_sqrt", 4 * l + j + 1)
                L.did(v.reciprocal(st[:, 4:6], st[:, 2:4]))
                if j + l > 0:
                    L.need("mk_out", 16 * (4 * l + j))
                    n = items[("mkT", l, j - 1) if j else ("mkT", 0, 3)]
                if l == 0 and j == 0:
                    L.need("ld_bc", 32)
                L.settle()
                for c in range(2):
                    L.did(v.scalar_tensor_tensor(out=kout[:, c], in0=kraw[:, c], scalar=st[:, 4 + c:5 + c],
                                                 in1=mkg[:, MD * l:MD * l + MD], op0=ALU.mult, op1=ALU.mult),
                          "mk_ready" if c else None)
                b = full(L, ("mkT", l, j))
                free(L, ("mkT", l, j), v.tensor_copy(mKT[:, l, 2 * j:2 * j + 2].rearrange("p f m -> p (f m)"), b[:, :]))
                if j < len(between):
                    between[j](L)

        def load_resid(sp, w, name, nu, kt):
            for j in range(4):
                for s in range(nu):
                    load_unit(sp, w, (name, j, s), kt, slice(P * kt * s, P * kt * (s + 1)), cols(j))

        def pe_resid(pe, name, kt, src):
            for j in range(4):
                uready(pe, (name, j, 0))
                w = uslot((name, j, 0), kt)
                for m in range(2):
                    for h in range(2):
                        key = (name, 2 * j + m, h)
                        b = fill(pe, key)
                        for k in range(kt):
                            ins = nc.tensor.matmul(b[:, 0:HT], w[:, k, P * m:P * m + P], src[:, k, half(h)],
                                                   start=(k == 0), stop=(k == kt - 1))
                        filled(key, ins)

        def v_resid(L, name, k):
            for m in range(KT):
                for h in range(2):
                    b = full(L, (name, m, h))
                    free(L, (name, m, h), nc.vector.tensor_tensor(xT[:, m, half(h)], xT[:, m, half(h)], b[:, 0:HT],
                                                                  ALU.add))
                if m >= 1:
                    v_sum_squares(L, k, m - 1)
            v_sum_squares(L, k, KT - 1)

        def v_sum_squares(L, k, m):
            if m >= 1:
                L.need("sq_ready", KT * k + m + 1)
                L.tt(rstd[:], sq[:, 0] if m == 1 else rstd[:], sq[:, m], ALU.add, sem="ssum_ready" if m == KT - 1 else None)

        def a_squares(L, name, k):
            for m in range(KT):
                if name == "glu":
                    L.need("x_glu", 2 * m + 2)
                else:
                    landed(L.e, (name, m, 0))
                    landed(L.e, (name, m, 1))
                if name == "fo0" and m == 0:
                    full(L, (name, KT - 1, 1))
                L.did(nc.scalar.activation(sq[:, m], xT[:, m], ACT.Square), "sq_ready")

        def pe_norm(pe, k):
            t = nc.tensor
            pe.wait_ge(S("ssum_ready"), k + 1)
            for h in range(2):
                b = fill(pe, ("ssq", k, h))
                filled(("ssq", k, h), t.matmul(b[:, 0:HT], ones[:], rstd[:, half(h)], start=True, stop=True))

        def a_norm(L, k):
            for h in range(2):
                b = full(L, ("ssq", k, h))
                free(L, ("ssq", k, h), nc.scalar.activation(rstd[:, half(h)], b[:, 0:HT], ACT.Sqrt, bias=epst[:],
                                                            scale=1.0 / D))

        def v_norm_split(L, k, gain):
            landed(L.e, ("ssq", k, 0))
            landed(L.e, ("ssq", k, 1))
            L.did(nc.vector.reciprocal(rstd[:], rstd[:]))
            L.settle()
            l = (1, 4).index(k)
            for m in range(KT + 1):
                if m < KT:
                    L.did(nc.vector.scalar_tensor_tensor(out=sq[:, m], in0=xT[:, m], scalar=gain(m), in1=rstd[:],
                                                         op0=ALU.mult, op1=ALU.mult), "hs_ready")
                if m >= 1:
                    L.need("h_hi", KT * l + m)
                    L.did(nc.vector.tensor_tensor(hlo[:, m - 1], sq[:, m - 1], hhi[:, m - 1].bitcast(F32),
                                                  ALU.subtract), "h_lo")

        def v_norm(L, k, gain):
            landed(L.e, ("ssq", k, 0))
            landed(L.e, ("ssq", k, 1))
            L.did(nc.vector.reciprocal(rstd[:], rstd[:]))
            L.settle()
            for m in range(KT):
                L.did(nc.vector.scalar_tensor_tensor(out=hT[:, m], in0=xT[:, m], scalar=gain(m), in1=rstd[:],
                                                     op0=ALU.mult, op1=ALU.mult), "h_ready")

        sgb = arena[:, 24592:24592 + 2 * T].rearrange("p (i t) -> p i t", i=2)

        def a_glu(L):
            for m in range(KT):
                for h in range(2):
                    b = full(L, ("glu", m, h))
                    n = 2 * m + h
                    if n >= 2:
                        L.need("x_glu", n - 1)
                    free(L, ("glu", m, h), nc.scalar.activation(sgb[:, h, 0:HT], b[:, 0:HT], ACT.Sigmoid, bias=b_glu(m)))

        def v_glu(L):
            for m in range(KT):
                for h in range(2):
                    landed(L.e, ("glu", m, h))
                    L.tt(sgb[:, h, 0:HT], sgb[:, h, 0:HT], hT[:, m, half(h)], ALU.mult, dep=False)
                    L.tt(xT[:, m, half(h)], xT[:, m, half(h)], sgb[:, h, 0:HT], ALU.add, sem="x_glu")

        ACT0 = KT * T
        act = arena[:, ACT0:ACT0 + FT * T].rearrange("p (k t) -> p k t", k=FT)
        mK_r, mV_r = rounded("mKT_r", "mKT", 2 * KT * NM), rounded("mV_r", "mV", 2 * 2 * D)
        hhi = rounded("h_hi_r", "hT", KT * T)[:].rearrange("p (k t) -> p k t", k=KT)
        hlo = rounded("h_lo_r", "arena", KT * T)[:].rearrange("p (k t) -> p k t", k=KT)
        alo = rounded("act_lo_r", "arena", FT * T, ACT0)[:].rearrange("p (k t) -> p k t", k=FT)
        WS0 = ACT0 + FT * T
        WP = KT * RUNIT
        wsp = rounded("w_parts_r", "arena", 4 * WP, WS0)[:].rearrange("p (s i n) -> p s i n", s=2, i=2)
        MR = KT * NM // T

        def ahi(l, k):
            if k < 2 * MR:
                base = (mK_r, mV_r)[k // MR]
                o_ = KT * NM * l + T * (k % MR)
                return base[:, o_:o_ + T]
            return hlo[:, k - 2 * MR] if k < 2 * MR + KT else hhi[:, k - 2 * MR - KT]

        def sp_ffn(sp, l):
            wv = a["ffn_w_in"][l].rearrange("(k p) (h n) -> p k h n", p=P, h=2)

            def put(u, n, i=None):
                lo = u * P if i is None else (2 * i + u) * P
                src = wv[:, :, :, lo:lo + P] if i is None else wv[:, :, :, bass.ts(2 * i + u, P)]
                for h in range(2):
                    sp.dma_start(ring[:, (n % 2) * UW:(n % 2) * UW + KT * RUNIT].rearrange(
                        "p (k h c) -> p k h c", k=KT, h=2)[:, :, h], src[:, :, h]).then_inc(S(f"w_full{n % 2}"), 8 * 2)
            for u in range(2):
                n = units[("fi", l, u)]
                sp.wait_ge(S(unit_end[n - 2][0]), unit_end[n - 2][1])
                put(u, n)
            with sp.Fori(1, FT // 2) as i:
                for u in range(2):
                    n = units[("fi", l, u)]
                    sem, v = unit_end[n]
                    sp.wait_ge(S(sem), i + (v - 1))
                    put(u, n, i)
            load_resid(sp, a["ffn_w_out"][l], f"fo{l}", 2, 11)

        def w_raw(l, key):
            if len(key) == 1:
                return uslot(("fi", l, key[0]), KT)
            return uslot((f"fo{l}", key[0], key[1]), FT // 2)[:, :, P * key[2]:P * key[2] + P]

        def w_part(q, i, key):
            kt, c = (KT, RUNIT) if len(key) == 1 else (FT // 2, P)
            return wsp[:, q % 2, i, 0:kt * c].rearrange("p (k c) -> p k c", k=kt)

        def piece_used(e, l, key, i=0):
            if len(key) == 1:
                m = items[("fi", l, key[0], 3)]
            elif key[1] == 1:
                m = items[(f"fo{l}", 2 * key[0] + key[2], 1)]
            else:
                e.wait_ge(S("half_used"), 8 * l + 2 * key[0] + key[2] + 1)
                return
            e.wait_ge(S(f"bank_full{m % 8}"), i + (m // 8 + 1))

        out_pieces = [(j, s, m) for j in range(4) for s in range(2) for m in range(2)]

        def a_split(L, l, key, i=0, reuse=True):
            q = piece(l, key)
            if len(key) == 1:
                n = units[("fi", l, key[0])]
                L.e.wait_ge(S(f"w_full{n % 2}"), 32 * i + wcount(n))
                if reuse:
                    m = items[("fi", l, key[0], 3)]
                    L.e.wait_ge(S(f"bank_full{m % 8}"), i + m // 8)
            else:
                uready(L.e, (f"fo{l}", key[0], key[1]))
                j = out_pieces.index(key)
                piece_used(L.e, l, out_pieces[j - 2] if j >= 2 else (FT - 2 + j,))
            nc.scalar.activation(w_part(q, 0, key), w_raw(l, key), ACT.Copy).then_inc(S(f"w_hi{q % 2}"), 1)

        def v_split(L, l, key, i=0):
            q = piece(l, key)
            L.e.wait_ge(S(f"w_hi{q % 2}"), i + (q // 2 + 1))
            nc.vector.tensor_tensor(w_part(q, 1, key), w_raw(l, key), w_part(q, 0, key).bitcast(F32), ALU.subtract) \
              .then_inc(S(f"w_split{q % 2}"), 1)

        def mm3(out, w, k, cs, xhi, xlo, start, stop):
            t = nc.tensor
            t.matmul(out, w[0][:, k, cs], xhi, start=start, stop=False)
            t.matmul(out, w[0][:, k, cs], xlo, start=False, stop=False)
            return t.matmul(out, w[1][:, k, cs], xhi, start=False, stop=stop)

        def pe_ffn(pe, l):
            with pe.Fori(0, FT // 2) as i:
                for u in range(2):
                    q = piece(l, (u,))
                    pe.wait_ge(S(f"w_split{q % 2}"), i + (q // 2 + 1))
                    w = [w_part(q, x, (u,)) for x in range(2)]
                    for j in range(4):
                        m = items[("fi", l, u, j)]
                        pe.wait_ge(S(f"bank_free{m % 8}"), i + m // 8)
                        for k in range(KT):
                            if u == 0 and j == 0:
                                pe.wait_ge(S("h_lo"), KT * l + k + 1)
                            ins = mm3(ps[:, m % 8, 0:HT], w, k, slice(P * (j // 2), P * (j // 2) + P),
                                      hhi[:, k, half(j % 2)], hlo[:, k, half(j % 2)], k == 0, k == KT - 1)
                        ins.then_inc(S(f"bank_full{m % 8}"), 1)
            for j, s, mm in out_pieces:
                q = piece(l, (j, s, mm))
                pe.wait_ge(S(f"w_split{q % 2}"), q // 2 + 1)
                w = [w_part(q, x, (j, s, mm)) for x in range(2)]
                for h in range(2):
                    key = (f"fo{l}", 2 * j + mm, h)
                    b = fill(pe, key) if s == 0 else ps[:, items[key] % 8, :]
                    for k in range(FT // 2):
                        tile = FT // 2 * s + k
                        if j == 0 and mm == 0 and h == 0:
                            pe.wait_ge(S("a_lo"), FT * l + tile + 1)
                        ins = mm3(b[:, 0:HT], w, k, slice(0, P), ahi(l, tile)[:, half(h)], alo[:, tile, half(h)],
                                  s == 0 and k == 0, s == 1 and k == FT // 2 - 1)
                    if s == 1:
                        filled(key, ins)
                if s == 0:
                    ins.then_inc(S("half_used"), 1)

        def a_ffn(L, l):
            last = FT // 2 - 1

            def unit_step(u, i, final=False):
                if u == 0:
                    a_split(L, l, (1,), i)
                elif final:
                    a_split(L, l, (0, 0, 0))
                else:
                    a_split(L, l, (0,), i + 1)
                for h in range(2):
                    m, m2 = items[("fi", l, u, h)], items[("fi", l, u, 2 + h)]
                    L.e.wait_ge(S(f"bank_full{m % 8}"), i + (m // 8 + 1))
                    L.e.wait_ge(S(f"bank_free{m2 % 8}"), i + m2 // 8)
                    nc.scalar.activation(sgb[:, u, half(h)], ps[:, m % 8, 0:HT], ACT.Silu) \
                      .then_inc(S(f"bank_free{m % 8}"), 1)
            for m in range(KT):
                L.need("hs_ready", KT * l + m + 1)
                L.did(nc.scalar.activation(hhi[:, m], sq[:, m], ACT.Copy), "h_hi")
            with L.e.Fori(0, last) as i:
                for u in range(2):
                    unit_step(u, i)
            for u in range(2):
                unit_step(u, last, True)
            for k in range(FT):
                if k == 0:
                    for h in range(2):
                        landed(L.e, ("fi", l, FT - 1, 2 + h))
                        landed(L.e, ("fi", l, FT - 2, 2 + h))
                L.did(nc.scalar.activation(ahi(l, k), act[:, k], ACT.Copy), "a_hi")
                if k == 5:
                    a_split(L, l, (0, 0, 1))
            for key in out_pieces[2:]:
                a_split(L, l, key)

        def v_ffn(L, l):
            last = FT // 2 - 1

            def unit_step(u, i, final=False):
                if u == 0:
                    v_split(L, l, (1,), i)
                elif final:
                    v_split(L, l, (0, 0, 0))
                else:
                    v_split(L, l, (0,), i + 1)
                for h in range(2):
                    m, m2 = items[("fi", l, u, h)], items[("fi", l, u, 2 + h)]
                    L.e.wait_ge(S(f"bank_free{m % 8}"), i + (m // 8 + 1))
                    L.e.wait_ge(S(f"bank_full{m2 % 8}"), i + (m2 // 8 + 1))
                    k = 2 * i + u
                    nc.vector.tensor_tensor(act[:, k, half(h)], ps[:, m2 % 8, 0:HT], sgb[:, u, half(h)],
                                            ALU.mult).then_inc(S(f"bank_free{m2 % 8}"), 1)
            with L.e.Fori(0, last) as i:
                for u in range(2):
                    unit_step(u, i)
            for u in range(2):
                unit_step(u, last, True)
            for k in range(FT):
                L.need("a_hi", FT * l + k + 1)
                L.did(nc.vector.tensor_tensor(alo[:, k], act[:, k], ahi(l, k).bitcast(F32), ALU.subtract), "a_lo")
                if k == 5:
                    v_split(L, l, (0, 0, 1))
            for n, (j, s, m) in enumerate(out_pieces):
                if n >= 1 and n + 1 < len(out_pieces):
                    v_split(L, l, out_pieces[n + 1])
                if s == 1:
                    for h in range(2):
                        key = (f"fo{l}", 2 * j + m, h)
                        b = full(L, key)
                        x = xT[:, 2 * j + m, half(h)]
                        free(L, key, nc.vector.tensor_tensor(x, x, b[:, 0:HT], ALU.add))

        wsum = {}

        def wcount(n):
            if not wsum:
                tot = [0, 0]
                for key, q in units.items():
                    tot[q % 2] += 32 if key[0] == "fi" else 16
                    wsum[q] = tot[q % 2]
            return wsum[n]

        M = Space(arena, AR, 0)
        qT = M.take(KT * T, "p (f t) -> p f t", f=KT)
        qraw = M.take(2 * 5 * MD, "p (i t n) -> p i t n", i=2, t=5)
        pm = M.take(2 * 4 * NM, "p (i t n) -> p i t n", i=2, t=4)
        pmT = M.take(2 * 2 * SEQ, "p (i c t) -> p i c t", i=2, c=2)
        KTs = M.take(2 * KT * NM, "p (i f m) -> p i f m", i=2, f=KT)
        sTs = M.take(2 * P, "p (c n) -> p c n", c=2)
        psm = M.take(2 * P)
        pTs = M.take(2 * P, "p (c n) -> p c n", c=2)
        qs = M.take(2 * 16, "p (i n) -> p i n", i=2)
        ms = M.take(2 * 16, "p (i n) -> p i n", i=2)
        M.at = 16400
        ck = M.take(4 * 2 * D, "p (i c n) -> p i c n", i=4, c=2)
        SC = float(MD) ** -0.5

        def rows(t):
            return P if t < 4 else NS

        def tsl(t):
            return slice(P * t, P * t + P) if t < 4 else slice(SEQ, T)

        def ck_ready(e, l, n):
            e.wait_ge(S(f"ck{n % 4}"), 16 * (4 * l + n // 4 + 1))

        def sp_cache(sp, l):
            for n in range(2 * DB):
                b = n % DB
                if n >= 4:
                    if n - 4 < DB:
                        m = items[("skT", l, n - 4, 3)]
                        sp.wait_ge(S(f"bank_full{m % 8}"), m // 8 + 1)
                    else:
                        sp.wait_ge(S("sv_used"), DB * l + n - 4 - DB + 1)
                elif n == 0 and l == 0:
                    for i in range(4):
                        landed(sp, ("yT", NB - 1, i // 2, i % 2))
                    landed(sp, ("fin", 1))
                elif n == 0:
                    landed(sp, ("wo", KT - 1, 1))
                src = a["cache_mem_k" if n < DB else "cache_mem_v"][l, b].rearrange("(c p) h n -> p c (h n)", p=P)
                sp.dma_start(ck[:, n % 4], src).then_inc(S(f"ck{n % 4}"), 16)

        def pe_memattn(pe, l):
            t = nc.tensor

            def turn(h):
                pe.wait_ge(S("qn_ready"), MH * l + h + 1)
                for d in range(2):
                    b = fill(pe, ("mqT", l, h, d))
                    for q in range(4):
                        ins = t.transpose(b[:, P * q:P * q + P], qraw[:, h % 2, q, P * d:P * d + P], ident[:])
                    filled(("mqT", l, h, d), ins)
                b = fill(pe, ("mqT", l, h, 2))
                for d in range(2):
                    ins = t.transpose(b[:, NS * d:NS * d + NS], qraw[0:NS, h % 2, 4, P * d:P * d + P],
                                      ident[0:NS, 0:NS])
                filled(("mqT", l, h, 2), ins)

            for h in range(MH):
                w = uslot(("mq", l, h), KT)
                for i in range(3):
                    b = fill(pe, ("mq", l, h, i))
                    if i == 0:
                        uready(pe, ("mq", l, h))
                    for c, tt in enumerate((2 * i, 2 * i + 1) if i < 2 else (4,)):
                        for k in range(KT):
                            if (h, i, c) == (0, 0, 0):
                                pe.wait_ge(S("h_ready"), KT * (0, 2)[l] + k + 1)
                            ins = t.matmul(b[0:rows(tt), 256 * c:256 * c + 256], hT[:, k, tsl(tt)], w[:, k, :],
                                           start=(k == 0), stop=(k == KT - 1))
                    filled(("mq", l, h, i), ins)
                if h >= 1:
                    turn(h - 1)
            turn(MH - 1)
            for h in range(MH):
                for i in range(3):
                    landed(pe, ("mqT", l, h, i))
                landed(pe, ("mkT", l, h))
                landed(pe, ("kv", l, 4 + h))

            def scores(h, q):
                b = fill(pe, ("ms", l, h, q))
                for c in range(2):
                    for d in range(2):
                        ins = t.matmul(b[:, 256 * c:256 * c + 256], qT[:, 2 * h + d, tsl(2 * q + c)],
                                       mKT[:, l, 2 * h + d, :], start=(d == 0), stop=(d == 1))
                filled(("ms", l, h, q), ins)
            for h in range(MH + 1):
                if h < MH:
                    scores(h, 0)
                if h >= 1:
                    g = h - 1
                    pe.wait_ge(S("mp_ready"), MH * l + h)
                    for c in range(2):
                        b = fill(pe, ("mp", l, g, c))
                        for q in range(4):
                            ins = t.transpose(b[:, P * q:P * q + P], pm[:, g % 2, q, P * c:P * c + P], ident[:])
                        filled(("mp", l, g, c), ins)
                if h < MH:
                    scores(h, 1)
                if h >= 1:
                    landed(pe, ("mp", l, g, 0))
                    landed(pe, ("mp", l, g, 1))
                    for d in range(2):
                        b = fill(pe, ("mo", l, g, d))
                        for c in range(2):
                            ins = t.matmul(b[:, :], mV[:, l, c, 256 * g + P * d:256 * g + P * d + P],
                                           pmT[:, g % 2, c, :], start=(c == 0), stop=(c == 1))
                        filled(("mo", l, g, d), ins)
            for nb in range(DB + 1):
                if nb < DB:
                    ck_ready(pe, l, nb)
                    for i in range(4):
                        b = fill(pe, ("skT", l, nb, i))
                        for q in range(4):
                            f, c = 2 * i + q // 2, q % 2
                            ins = t.transpose(b[:, P * q:P * q + P], ck[:, nb % 4, c, P * f:P * f + P], ident[:])
                        filled(("skT", l, nb, i), ins)
                if nb == 0:
                    continue
                bb = nb - 1
                for i in range(4):
                    landed(pe, ("skT", l, bb, i))
                b = fill(pe, ("ssT", l, bb))
                for c in range(2):
                    for h in range(MH):
                        for d in range(2):
                            ins = t.matmul(b[:, 4 * (MH * c + h):4 * (MH * c + h) + 4],
                                           KTs[:, bb % 2, 2 * h + d, P * c:P * c + P],
                                           qT[:, 2 * h + d, SEQ + DS * bb:SEQ + DS * bb + DS],
                                           start=(d == 0), stop=(d == 1))
                filled(("ssT", l, bb), ins)
            for bb in range(DB):
                landed(pe, ("ssT", l, bb))
            b = fill(pe, ("ss", l))
            for c in range(2):
                ins = t.transpose(b[:, P * c:P * c + P], sTs[:, c, :], ident[:])
            filled(("ss", l), ins)
            pe.wait_ge(S("sp_ready"), l + 1)
            b = fill(pe, ("sp", l))
            for c in range(2):
                ins = t.transpose(b[:, P * c:P * c + P], psm[:, P * c:P * c + P], ident[:])
            filled(("sp", l), ins)
            landed(pe, ("sp", l))
            b = fill(pe, ("so", l))
            for bb in range(DB):
                n = DB + bb
                ck_ready(pe, l, n)
                for f in range(KT):
                    for c in range(2):
                        h = f // 2
                        ins = t.matmul(b[:, NS * f + DS * bb:NS * f + DS * bb + DS],
                                       ck[:, n % 4, c, P * f:P * f + P],
                                       pTs[:, c, NS * h + DS * bb:NS * h + DS * bb + DS],
                                       start=(c == 0), stop=(c == 1))
                ins.then_inc(S("sv_used"), 1)
            pe.wait_ge(S("sv_used"), DB * (l + 1))
            t.transpose(b[:, 256:384], ident[:], ident[:]).then_inc(S(f"bank_full{items[('so', l)] % 8}"), 1)
            landed(pe, ("so", l))
            for g in range(MH):
                for d in range(2):
                    landed(pe, ("mo", l, g, d))
            pe_resid(pe, f"mo{l}", KT, hT)

        def a_memattn(L, l):
            s = nc.scalar
            L.need("qs_init", l + 1)
            for h in range(MH):
                if h >= 2:
                    landed(L.e, ("mqT", l, h - 2, 2))
                for i in range(3):
                    b = full(L, ("mq", l, h, i))
                    if i < 2:
                        free(L, ("mq", l, h, i), s.activation(qraw[:, h % 2, 2 * i:2 * i + 2].rearrange("p t n -> p (t n)"),
                                                              b[:, :], ACT.Copy))
                    else:
                        free(L, ("mq", l, h, i), s.activation(qraw[0:NS, h % 2, 4], b[0:NS, 0:256], ACT.Copy))
                L.settle()
                for tt in range(5):
                    r = rows(tt)
                    L.settle()
                    L.did(s.activation(scr[0:r], qraw[0:r, h % 2, tt], ACT.Square, accum_out=qs[0:r, h % 2, tt:tt + 1]))
                L.settle()
                L.did(s.activation(qs[:, h % 2, 5:10], qs[:, h % 2, 0:5], ACT.Sqrt, bias=epst[:], scale=1.0 / MD),
                      "qs_sqrt")
                if h >= 1:
                    b = full(L, ("mqT", l, h - 1, 1))
                    free(L, ("mqT", l, h - 1, 1), s.activation(qT[:, 2 * h - 1, 0:SEQ], b[:, :], ACT.Copy,
                                                               scale=g_mq(l, 1)))
            b = full(L, ("mqT", l, MH - 1, 1))
            free(L, ("mqT", l, MH - 1, 1), s.activation(qT[:, 2 * MH - 1, 0:SEQ], b[:, :], ACT.Copy, scale=g_mq(l, 1)))

            def turned_weights(g):
                b = full(L, ("mp", l, g, 1))
                free(L, ("mp", l, g, 1), s.activation(pmT[:, g % 2, 1], b[:, :], ACT.Copy))

            def finish(g):
                b = full(L, ("mo", l, g, 1))
                free(L, ("mo", l, g, 1), s.activation(hT[:, 2 * g + 1, 0:SEQ], b[:, :], ACT.Copy))
            for h in range(MH):
                if h >= 1:
                    turned_weights(h - 1)
                L.need("nmx_ready", MH * l + h + 1)
                for q in range(4):
                    b = full(L, ("ms", l, h, q // 2))
                    ins = s.activation(pm[:, h % 2, q], b[:, 256 * (q % 2):256 * (q % 2) + 256], ACT.Exp,
                                       bias=ms[:, h % 2, q:q + 1], scale=SC, accum_out=ms[:, h % 2, 4 + q:5 + q])
                    if q % 2:
                        free(L, ("ms", l, h, q // 2), ins)
                    else:
                        L.did(ins)
                if h >= 1:
                    finish(h - 1)
            turned_weights(MH - 1)
            finish(MH - 1)
            for bb in range(DB):
                if bb >= 2:
                    landed(L.e, ("ssT", l, bb - 2))
                for i in (1, 3):
                    b = full(L, ("skT", l, bb, i))
                    free(L, ("skT", l, bb, i), s.activation(KTs[:, bb % 2, 2 * i:2 * i + 2].rearrange("p f m -> p (f m)"),
                                                            b[:, :], ACT.Copy))
            L.need("snmx_ready", l + 1)
            b = full(L, ("ss", l))
            free(L, ("ss", l), s.activation(psm[:], b[:, 0:256], ACT.Exp, bias=st[:, 8:9], scale=SC,
                                            accum_out=st[:, 9:10]))
            b = full(L, ("so", l))
            free(L, ("so", l), s.activation(hT[:, :, SEQ:], b[:, 0:256].rearrange("p (f n) -> p f n", f=KT), ACT.Copy))

        def v_memattn(L, l):
            v = nc.vector
            L.did(v.memset(qs, 1.0), "qs_init")

            def turned(h):
                b = full(L, ("mqT", l, h, 0))
                free(L, ("mqT", l, h, 0), v.tensor_scalar(qT[:, 2 * h, 0:SEQ], b[:, :], g_mq(l, 0), None, ALU.mult))
                b = full(L, ("mqT", l, h, 2))
                L.did(v.tensor_scalar(qT[:, 2 * h, SEQ:], b[:, 0:NS], g_mq(l, 0), None, ALU.mult))
                free(L, ("mqT", l, h, 2), v.tensor_scalar(qT[:, 2 * h + 1, SEQ:], b[:, NS:2 * NS], g_mq(l, 1), None,
                                                          ALU.mult))
            for h in range(MH):
                L.need("qs_sqrt", MH * l + h + 1)
                L.did(v.reciprocal(qs[:, h % 2, 10:15], qs[:, h % 2, 5:10]))
                L.settle()
                for tt in range(5):
                    r = rows(tt)
                    L.did(v.tensor_scalar(qraw[0:r, h % 2, tt], qraw[0:r, h % 2, tt], qs[0:r, h % 2, 10 + tt:11 + tt],
                                          None, ALU.mult), "qn_ready" if tt == 4 else None)
                if h >= 1:
                    turned(h - 1)
            turned(MH - 1)

            def turned_weights(g):
                b = full(L, ("mp", l, g, 0))
                free(L, ("mp", l, g, 0), v.tensor_copy(pmT[:, g % 2, 0], b[:, :]))

            def finish(g):
                b = full(L, ("mo", l, g, 0))
                free(L, ("mo", l, g, 0), v.tensor_copy(hT[:, 2 * g, 0:SEQ], b[:, :]))

            def weights(g):
                landed(L.e, ("ms", l, g, 1))
                L.recip(ms[:, g % 2, 8:12], ms[:, g % 2, 4:8])
                L.settle()
                for q in range(4):
                    L.did(v.tensor_scalar(pm[:, g % 2, q], pm[:, g % 2, q], ms[:, g % 2, 8 + q:9 + q], None, ALU.mult),
                          "mp_ready" if q == 3 else None)
            for h in range(MH):
                if h >= 1:
                    weights(h - 1)
                for q in range(2):
                    if q == 1 and h >= 1:
                        turned_weights(h - 1)
                    b = full(L, ("ms", l, h, q))
                    L.did(v.tensor_reduce(ms[:, h % 2, 12 + 2 * q:14 + 2 * q], b[:, :].rearrange("p (c n) -> p c n", c=2),
                                          AX, ALU.max))
                L.ts(ms[:, h % 2, 0:4], ms[:, h % 2, 12:16], -SC, None, ALU.mult, sem="nmx_ready")
                if h >= 1:
                    finish(h - 1)
            weights(MH - 1)
            turned_weights(MH - 1)
            finish(MH - 1)
            for nb in range(DB + 1):
                if nb < DB:
                    for i in (0, 2):
                        b = full(L, ("skT", l, nb, i))
                        free(L, ("skT", l, nb, i),
                             v.tensor_copy(KTs[:, nb % 2, 2 * i:2 * i + 2].rearrange("p f m -> p (f m)"), b[:, :]))
                if nb == 0:
                    continue
                bb = nb - 1
                b = full(L, ("ssT", l, bb))
                free(L, ("ssT", l, bb), v.tensor_copy(
                    sTs.rearrange("p c (h n) -> p (c h) n", h=MH)[:, :, DS * bb:DS * bb + DS],
                    b[:, 0:32].rearrange("p (n t) -> p n t", t=DS)))
            b = full(L, ("ss", l))
            L.did(v.tensor_reduce(st[:, 10:11], b[:, 0:256], AX, ALU.max))
            L.ts(st[:, 8:9], st[:, 10:11], -SC, None, ALU.mult, sem="snmx_ready")
            landed(L.e, ("ss", l))
            L.recip(st[:, 11:12], st[:, 9:10])
            L.ts(psm[:], psm[:], st[:, 11:12], None, ALU.mult, sem="sp_ready")
            b = full(L, ("sp", l))
            free(L, ("sp", l), v.tensor_copy(pTs.rearrange("p c n -> p (c n)"), b[:, 0:256]))

        W_ = Space(arena, AR, 0)
        q2 = W_.take(NG * 4 * T, "p (g f t) -> p g f t", g=NG, f=4)
        k2 = W_.take(NG * 4 * T, "p (g f t) -> p g f t", g=NG, f=4)
        Vt = W_.take(5 * NG * SW, "p (t g n) -> p t g n", t=5, g=NG)
        u0 = W_.at
        raw = W_.take(2 * 5 * RUNIT, "p (i t n) -> p i t n", i=2, t=5)
        sqr = W_.take(5 * RUNIT, "p (t n) -> p t n", t=5)
        W2 = Space(arena, AR, u0)
        sc2 = W2.take(3 * 6 * P, "p (i n) -> p i n", i=3)
        pT2 = W2.take(2 * 6 * P, "p (i n) -> p i n", i=2)
        W3 = Space(arena, AR, u0)
        cb = W3.take(2 * 5 * SW, "p (i n) -> p i n", i=2)
        VS = 5 * SW + 2 * SW
        vring = [W_.b[:, VS * i:VS * i + VS] for i in range(2)]
        KW = Space(arena, AR, 2 * VS)
        qbd = W3.take(NG * 4 * DB * 2 * DS, "p (g f b h t) -> p g f b h t", g=NG, f=4, b=DB, h=2)
        M0 = mKT0[:, 0:515]
        M12 = mKT0[:, 516:516 + 256]
        m4 = mKT0[:, 780:784]
        KT1 = mKT0[:, 0:2048].rearrange("p (t f j) -> p t f j", t=4, f=4)
        KT0 = mV0[:, 0:512].rearrange("p (f j) -> p f j", f=4)
        KT2 = mV0[:, 512:1536].rearrange("p (t f j) -> p t f j", t=2, f=4)
        KTb = [(KT0, KT1, KT2), (KW.take(512, "p (f j) -> p f j", f=4), KW.take(2048, "p (t f j) -> p t f j", t=4, f=4),
                                 KW.take(1024, "p (t f j) -> p t f j", t=2, f=4))]
        tail = Space(hflat, KT * T, 4 * T)
        sT = tail.take(2 * 256, "p (g n) -> p g n", g=2)
        sT2 = tail.take(256)
        sTn = tail.take(NG * 256, "p (g n) -> p g n", g=NG)
        pT2s = tail.take(256)
        RW = 3 * P + NG * NS
        pR = kk[:, 0:2 * RW].rearrange("p (r n) -> p r n", r=2)
        pTc = pt[:].rearrange("p (g n) -> p g n", g=2)
        pTn = arena[:, u0 + 5120:u0 + 5120 + 768].rearrange("p (g n) -> p g n", g=NG)
        mk0 = sb("mk0", DS)
        mkn = sb("mkn", 2 * NS)
        sa = sb("sa", 64)
        q20 = sb("q20", 2 * 60)
        q20v = q20[:].rearrange("p (i n) -> p i n", i=2)
        SS = float(SD) ** -0.5

        def qcols(u):
            kind, g, hh = u // 6, (u % 6) // 2, u % 2
            return kind, g, hh, (kind * NG + g) * SW + RUNIT * hh

        def sp_qkv(sp):
            for u in range(18):
                kind, g, hh, c0 = qcols(u)
                load_unit(sp, a["attn_w_qkv"][0], ("qkv", u), KT, slice(0, D), slice(c0, c0 + RUNIT))

        def store_rows(sp, dst, g, hh, get, sem):
            c = slice(RUNIT * hh, RUNIT * hh + RUNIT)
            if g == 0:
                sp.dma_start(dst[0, 0].rearrange("p h n -> p (h n)")[:, c], get(slice(3, 4)).rearrange("p t n -> p (t n)")) \
                  .then_inc(S(sem), 16)
            else:
                sp.dma_start(dst[0, 0].rearrange("(j r) h n -> j r (h n)", r=4)[:, :, c], get(slice(0, 4))) \
                  .then_inc(S(sem), 16)

        def store_kv(sp, us):
            for u in us:
                kind, g, hh, c0 = qcols(u)
                c = slice(RUNIT * hh, RUNIT * hh + RUNIT)
                dst = o[4 + 2 * g + kind - 1]
                dsts = o[14 + 2 * g + kind - 1][0].rearrange("b t h n -> (b t) (h n)")[:, c]
                if kind == 1:
                    sp.wait_ge(S("k_ready"), u - 5)
                    get = lambda t, i=u % 2: raw[:, i, t]
                    srcs = raw[0:NS, u % 2, 4]
                else:
                    for i in range(3):
                        landed(sp, ("qkv", u, i))
                    get = lambda t, c=c, g=g: Vt[:, t, g, c]
                    srcs = Vt[0:NS, 4, g, c]
                sem = f"k_stored{u % 2}" if kind == 1 else "v_stored"
                store_rows(sp, dst, g, hh, get, sem)
                sp.dma_start(dsts, srcs).then_inc(S(sem), 16)

        def pool_masks(L):
            g = nc.gpsimd
            landed(L.e, ("fo0", KT - 1, 1))
            L.settle()
            L.did(g.memset(M0, 0.0))
            L.settle()
            L.did(g.memset(M12, 0.0))
            L.settle()
            L.did(g.memset(mk0[:], 0.0))
            L.settle()
            L.did(g.memset(mkn[:], 0.0))
            L.settle()
            L.settle()
            L.did(g.affine_select(out=M0, in_=M0, compare_op=ALU.is_ge, fill=BIG, base=3, pattern=[[-1, 515]],
                                  channel_multiplier=4))
            L.settle()
            L.did(g.affine_select(out=M12[:, 0:P], in_=M12[:, 0:P], compare_op=ALU.is_ge, fill=BIG, base=0,
                                  pattern=[[-1, P]], channel_multiplier=1))
            L.settle()
            L.did(g.affine_select(out=mk0[:], in_=mk0[:], compare_op=ALU.is_ge, fill=BIG, base=0,
                                  pattern=[[-1, DS]], channel_multiplier=1))
            n0 = mkn[0:NS, 0:NS].rearrange("p (b t) -> p b t", b=DB)
            L.settle()
            L.did(g.affine_select(out=n0, in_=n0, compare_op=ALU.is_ge, fill=BIG, base=0,
                                  pattern=[[-DS, DB], [0, DS]], channel_multiplier=1))
            n1 = mkn[0:NS, NS:2 * NS]
            L.settle()
            L.did(g.affine_select(out=n1, in_=n1, compare_op=ALU.is_equal, fill=BIG, base=0,
                                  pattern=[[-1, NS]], channel_multiplier=1))
            L.settle()
            L.did(g.affine_select(out=M0, in_=M0, compare_op=ALU.is_ge, fill=BIG, base=P - 3, pattern=[[1, 515]],
                                  channel_multiplier=-4))
            L.settle()
            L.did(g.affine_select(out=n0, in_=n0, compare_op=ALU.is_ge, fill=BIG, base=0,
                                  pattern=[[DS, DB], [1, DS]], channel_multiplier=-1), "masks_ready")

        def v_masks(L):
            L.need("masks_ready", 1)
            L.settle()
            L.did(nc.vector.tensor_reduce(m4, ident[:].rearrange("p (j r) -> p r j", r=4), AX, ALU.add))
            L.ts(m4, m4, -BIG, BIG, ALU.mult, ALU.add)
            L.tt(M12[:, P:].rearrange("p (j r) -> p j r", r=4), M12[:, 0:P].rearrange("p (j r) -> p j r", r=4),
                 m4.unsqueeze(1).to_broadcast([P, 32, 4]), ALU.add)

        def pe_qkv(pe):
            t = nc.tensor

            def turn(u):
                kind = u // 6
                if kind == 0:
                    pe.wait_ge(S("q_ready"), u + 1)
                else:
                    pe.wait_ge(S("k_ready"), u - 5)
                for d in range(2):
                    b = fill(pe, ("qkT", u, d))
                    for q in range(4):
                        ins = t.transpose(b[:, P * q:P * q + P], raw[:, u % 2, q, P * d:P * d + P], ident[:])
                    filled(("qkT", u, d), ins)
                b = fill(pe, ("qkT", u, 2))
                for d in range(2):
                    ins = t.transpose(b[:, NS * d:NS * d + NS], raw[0:NS, u % 2, 4, P * d:P * d + P], ident[0:NS, 0:NS])
                filled(("qkT", u, 2), ins)

            for u in range(18):
                kind, g, hh, _ = qcols(u)
                w = uslot(("qkv", u), KT)
                for i in range(3):
                    b = fill(pe, ("qkv", u, i))
                    if i == 0:
                        uready(pe, ("qkv", u))
                    for c, tt in enumerate((2 * i, 2 * i + 1) if i < 2 else (4,)):
                        sl = tsl(tt) if tt == 4 or (kind > 0 and g == 0) else slice(tt, SEQ, 4)
                        for k in range(KT):
                            if (u, i, c) == (0, 0, 0):
                                pe.wait_ge(S("h_ready"), KT + k + 1)
                            ins = t.matmul(b[0:rows(tt), 256 * c:256 * c + 256], hT[:, k, sl], w[:, k, :],
                                           start=(k == 0), stop=(k == KT - 1))
                    filled(("qkv", u, i), ins)
                if 1 <= u <= 12:
                    turn(u - 1)

        def a_qkv(L):
            s = nc.scalar
            L.need("q20_init", 1)

            def turned(u):
                kind, g, hh, _ = qcols(u)
                b = full(L, ("qkT", u, 1))
                if kind == 0:
                    ins = s.activation(q2[:, g, 2 * hh + 1, 0:SEQ], b[:, :], ACT.Copy, scale=g_sq(g))
                else:
                    ins = s.activation(k2[:, g, 2 * hh + 1, 0:SEQ], b[:, :], ACT.Copy)
                free(L, ("qkT", u, 1), ins)
            for u in range(18):
                kind, g, hh, _ = qcols(u)
                if kind < 2:
                    if u >= 2:
                        landed(L.e, ("qkT", u - 2, 2))
                        if u - 2 >= 6:
                            L.need(f"k_stored{u % 2}", 32 * ((u - 8) // 2 + 1))
                    dst = raw[:, u % 2]
                else:
                    dst = Vt[:, :, g, RUNIT * hh:RUNIT * hh + RUNIT]
                for i in range(3):
                    b = full(L, ("qkv", u, i))
                    if i < 2:
                        free(L, ("qkv", u, i), s.activation(dst[:, 2 * i:2 * i + 2],
                                                            b[:, :].rearrange("p (t n) -> p t n", t=2), ACT.Copy))
                    else:
                        free(L, ("qkv", u, i), s.activation(dst[0:NS, 4], b[0:NS, 0:256], ACT.Copy))
                if kind < 2:
                    L.settle()
                    if u >= 1:
                        L.need("sq_used", u)
                    L.did(s.activation(sqr[:, 0:4], raw[:, u % 2, 0:4], ACT.Square))
                    L.did(s.activation(sqr[0:NS, 4], raw[0:NS, u % 2, 4], ACT.Square), "sqr_ready")
                    L.need("sq_used", u + 1)
                    L.did(s.activation(q20v[:, u % 2, 20:40], q20v[:, u % 2, 0:20], ACT.Sqrt, bias=epst[:],
                                       scale=1.0 / SD), "q20_sqrt")
                if 1 <= u <= 12:
                    turned(u - 1)

        def v_qkv(L):
            v = nc.vector
            L.did(v.memset(q20[:], 1.0), "q20_init")

            def turned(u):
                kind, g, hh, _ = qcols(u)
                b = full(L, ("qkT", u, 0))
                dst = (q2, k2)[kind]
                if kind == 0:
                    free(L, ("qkT", u, 0), v.tensor_scalar(dst[:, g, 2 * hh, 0:SEQ], b[:, :], g_sq(g), None, ALU.mult))
                else:
                    free(L, ("qkT", u, 0), v.tensor_copy(dst[:, g, 2 * hh, 0:SEQ], b[:, :]))
                b = full(L, ("qkT", u, 2))
                src = b[:, 0:2 * NS].rearrange("p (f n) -> p f n", f=2)
                if kind == 0:
                    free(L, ("qkT", u, 2), v.tensor_scalar(dst[:, g, 2 * hh:2 * hh + 2, SEQ:], src, g_sq(g), None, ALU.mult))
                else:
                    free(L, ("qkT", u, 2), v.tensor_copy(dst[:, g, 2 * hh:2 * hh + 2, SEQ:], src))
            for u in range(13):
                if u < 12:
                    L.need("sqr_ready", u + 1)
                    qv = q20v[:, u % 2]
                    L.settle()
                    L.did(v.tensor_reduce(qv[:, 0:16], sqr[:, 0:4].rearrange("p t (h n) -> p (t h) n", h=4), AX, ALU.add))
                    L.did(v.tensor_reduce(qv[0:NS, 16:20], sqr[0:NS, 4].rearrange("p (h n) -> p h n", h=4), AX, ALU.add),
                          "sq_used")
                    L.need("q20_sqrt", u + 1)
                    L.recip(qv[:, 40:60], qv[:, 20:40])
                    L.settle()
                    x = raw[:, u % 2, 0:4].rearrange("p t (h n) -> p (t h) n", h=4)
                    L.did(v.tensor_tensor(x, x, qv[:, 40:56].unsqueeze(2).to_broadcast([P, 16, SD]), ALU.mult))
                    x = raw[0:NS, u % 2, 4].rearrange("p (h n) -> p h n", h=4)
                    L.did(v.tensor_tensor(x, x, qv[0:NS, 56:60].unsqueeze(2).to_broadcast([NS, 4, SD]), ALU.mult),
                          "q_ready" if u < 6 else "kn_ready")
                if u >= 1:
                    turned(u - 1)

        def pool_keys(L):
            g_ = nc.gpsimd
            for u in range(6, 12):
                _, g, hh, _ = qcols(u)
                L.need("kn_ready", u - 5)
                kb = kgb[:, SD * g:SD * g + SD]
                x = raw[:, u % 2, 0:4].rearrange("p t (h n) -> p (t h) n", h=4)
                L.settle()
                L.did(g_.tensor_tensor(x, x, kb.unsqueeze(1).to_broadcast([P, 16, SD]), ALU.mult))
                x = raw[0:NS, u % 2, 4].rearrange("p (h n) -> p h n", h=4)
                L.settle()
                L.did(g_.tensor_tensor(x, x, kb[0:NS].unsqueeze(1).to_broadcast([NS, 4, SD]), ALU.mult), "k_ready")
                store_kv(L.e, [u])
            store_kv(L.e, range(12, 18))

        def step(n):
            return n // 8, (n % 8) // 2, n % 2

        NA = SH * 4

        def pe_attn(pe):
            t = nc.tensor
            for u in range(12):
                for i in range(3):
                    landed(pe, ("qkT", u, i))
            for u in range(12, 18):
                for i in range(3):
                    landed(pe, ("qkv", u, i))
            for n in range(NA + 2):
                if n >= 2:
                    m = n - 2
                    pe.wait_ge(S("ap_ready"), m + 1)
                    b = fill(pe, ("ap", m, 0))
                    for c in range(4):
                        ins = t.transpose(b[:, P * c:P * c + P], sc2[:, m % 3, P * c:P * c + P], ident[:])
                    filled(("ap", m, 0), ins)
                    b = fill(pe, ("ap", m, 1))
                    for c in range(2):
                        ins = t.transpose(b[:, P * c:P * c + P], sc2[:, m % 3, P * (4 + c):P * (5 + c)], ident[:])
                    filled(("ap", m, 1), ins)
                if n < NA:
                    f, r, e = step(n)
                    q = slice(64 * e, 64 * e + 64)
                    b = fill(pe, ("as", n, 0))
                    ins = t.matmul(b[:, :], q2[q, 0, f, P * r:P * r + P], k2[q, 0, f, 0:SEQ], start=True, stop=True)
                    filled(("as", n, 0), ins)
                    b = fill(pe, ("as", n, 1))
                    for g in (1, 2):
                        ins = t.matmul(b[:, P * (g - 1):P * g], q2[q, g, f, P * r:P * r + P],
                                       k2[q, g, f, P * r:P * r + P], start=True, stop=True)
                    filled(("as", n, 1), ins)
                if n >= 2:
                    f, r, e = step(m)
                    landed(pe, ("ap", m, 0))
                    landed(pe, ("ap", m, 1))
                    b = fill(pe, ("ao", m))
                    hc = slice(SD * (2 * f + e), SD * (2 * f + e) + SD)
                    for c in range(6):
                        vv = Vt[:, c, 0, hc] if c < 4 else Vt[:, r, c - 3, hc]
                        ins = t.matmul(b[64 * e:64 * e + 64, 0:P], vv, pT2[:, m % 2, P * c:P * c + P],
                                       start=(c == 0), stop=(c == 5))
                    filled(("ao", m), ins)

        def v_attn(L):
            v = nc.vector
            for n in range(NA + 2):
                if n >= 2:
                    m = n - 2
                    b = full(L, ("ap", m, 1))
                    free(L, ("ap", m, 1), v.tensor_copy(pT2[:, m % 2, 512:768], b[:, 0:256]))
                if 1 <= n <= NA:
                    m = n - 1
                    x = 16 * (m % 3)
                    L.need("aexp", m + 1)
                    L.did(v.reciprocal(sa[:, x + 5:x + 6], sa[:, x + 4:x + 5]))
                    L.ts(sc2[:, m % 3], sc2[:, m % 3], sa[:, x + 5:x + 6], None, ALU.mult, sem="ap_ready")
                if n < NA:
                    f, r, e = step(n)
                    x = 16 * (n % 3)
                    if n >= 3:
                        m = items[("ap", n - 3, 1)]
                        L.e.wait_ge(S(f"bank_full{m % 8}"), m // 8 + 1)
                    elif n == 0:
                        L.need("k_stored0", 32 * 3)
                        L.need("k_stored1", 32 * 3)
                        L.settle()
                    b = full(L, ("as", n, 0))
                    free(L, ("as", n, 0), v.tensor_tensor_reduce(sc2[:, n % 3, 0:512], b[:, :], M0[:, 3 - r:515 - r],
                                                                 1.0, -3e38, ALU.add, ALU.max, sa[:, x:x + 1]))
                    b = full(L, ("as", n, 1))
                    free(L, ("as", n, 1), v.tensor_tensor_reduce(sc2[:, n % 3, 512:768], b[:, 0:256], M12, 1.0, -3e38,
                                                                 ALU.add, ALU.max, sa[:, x + 1:x + 2]))
                    L.tt(sa[:, x + 2:x + 3], sa[:, x:x + 1], sa[:, x + 1:x + 2], ALU.max)
                    L.ts(sa[:, x + 3:x + 4], sa[:, x + 2:x + 3], -SS, None, ALU.mult, sem="anmx_ready")
                if n >= 2:
                    m = n - 2
                    f, r, e = step(m)
                    b = full(L, ("ao", m))
                    h = slice(64 * e, 64 * e + 64)
                    free(L, ("ao", m), v.tensor_copy(hT[h, f, slice(r, SEQ, 4)], b[h, 0:P]))

        def a_attn(L):
            s = nc.scalar
            for n in range(NA + 2):
                if n >= 2:
                    m = n - 2
                    b = full(L, ("ap", m, 0))
                    free(L, ("ap", m, 0), s.activation(pT2[:, m % 2, 0:512], b[:, :], ACT.Copy))
                if n < NA:
                    x = 16 * (n % 3)
                    L.need("anmx_ready", n + 1)
                    L.did(s.activation(sc2[:, n % 3], sc2[:, n % 3], ACT.Exp, bias=sa[:, x + 3:x + 4], scale=SS,
                                       accum_out=sa[:, x + 4:x + 5]), "aexp")

        def swa_rows(sp, c, b, lo, hi, sem):
            if lo is not None:
                sp.dma_start(lo[:, 0:SW], a[f"cache_swa0_{c}"][0, b].rearrange("p h n -> p (h n)")).then_inc(sem, 16)
                sp.dma_start(lo[:, SW:5 * SW].rearrange("p (t n) -> p t n", t=4),
                             a[f"cache_swa1_{c}"][0, b].rearrange("(j t) h n -> j t (h n)", t=4)).then_inc(sem, 16)
            if hi is not None:
                src = a[f"cache_swa2_{c}"][0, b].rearrange("(j t) h n -> j t (h n)", t=16)
                for e in range(2):
                    sp.dma_start(hi[64 * e:64 * e + 64].rearrange("p (t n) -> p t n", t=2), src[:, e:4:2]) \
                      .then_inc(sem, 16)

        def sp_swacache(sp):
            for b in range(DB):
                for part in range(2):
                    if b == 0:
                        for i in range(2):
                            landed(sp, ("ap", NA - 1, i))
                        landed(sp, ("ao", NA - 1))
                    else:
                        m = items[("bkT", b - 1, (4, 6)[part])]
                        sp.wait_ge(S(f"bank_full{m % 8}"), m // 8 + 1)
                    lo, hi = (cb[:, 0], None) if part == 0 else (None, cb[:, 1, 0:2 * SW])
                    swa_rows(sp, "k", b, lo, hi, S(f"cb{part}"))
            for b in range(DB):
                if b < 2:
                    for i in range(2):
                        landed(sp, ("bn", i))
                    sp.wait_ge(S("qbd_ready"), 1)
                else:
                    m = items[("bo", b - 2)]
                    sp.wait_ge(S(f"bank_full{m % 8}"), m // 8 + 1)
                v = vring[b % 2]
                swa_rows(sp, "v", b, v[:, 0:5 * SW], v[:, 5 * SW:], S(f"vs{b % 2}"))

        def cb_ready(e, b, part):
            e.wait_ge(S(f"cb{part}"), 32 * (b + 1))

        def pe_sattn(pe):
            t = nc.tensor
            pe.wait_ge(S("qbd_ready"), 1)
            for i in range(2):
                b = fill(pe, ("bn", i))
                for g in range(NG):
                    for f in range(4):
                        q = slice(64 * i, 64 * i + 64)
                        c = P * g + NS * f
                        ins = t.matmul(b[0:NS, c:c + NS], k2[q, g, f, SEQ:], q2[q, g, f, SEQ:],
                                       start=True, stop=True)
                filled(("bn", i), ins)

            def turn_keys(b_):
                cb_ready(pe, b_, 0)
                for i in range(5):
                    b = fill(pe, ("bkT", b_, i))
                    for f in range(4):
                        ins = t.transpose(b[:, P * f:P * f + P], cb[:, 0, SW * i + P * f:SW * i + P * f + P], ident[:])
                    filled(("bkT", b_, i), ins)
                cb_ready(pe, b_, 1)
                for i in range(2):
                    b = fill(pe, ("bkT", b_, 5 + i))
                    for f in range(4):
                        ins = t.transpose(b[:, P * f:P * f + P], cb[:, 1, SW * i + P * f:SW * i + P * f + P], ident[:])
                    filled(("bkT", b_, 5 + i), ins)
            for nb in range(DB + 1):
                if nb < DB:
                    turn_keys(nb)
                if nb == 0:
                    continue
                b_ = nb - 1
                KT0, KT1, KT2 = KTb[b_ % 2]
                for i in range(7):
                    landed(pe, ("bkT", b_, i))
                b = fill(pe, ("bs", b_))
                for f in range(4):
                    t.matmul(b[:, 8 * f:8 * f + 8], KT0[:, f, :], qbd[:, 0, f, b_].rearrange("p h t -> p (h t)"),
                             start=True, stop=True)
                    for tt in range(4):
                        c = 32 + 8 * f + tt
                        t.matmul(b[:, c:c + 5:4], KT1[:, tt, f, :], qbd[:, 1, f, b_, :, tt], start=True, stop=True)
                    for tt in range(2):
                        o2 = b[:, 64 + 8 * f:72 + 8 * f].rearrange("p (h t) -> p h t", h=2)[:, :, 2 * tt:2 * tt + 2]
                        ins = t.matmul(o2, KT2[:, tt, f, :], qbd[:, 2, f, b_, :, 2 * tt:2 * tt + 2],
                                       start=True, stop=True)
                filled(("bs", b_), ins)
            for b_ in range(DB):
                landed(pe, ("bs", b_))
            landed(pe, ("bn", 0))
            landed(pe, ("bn", 1))
            for R in range(2):
                b = fill(pe, ("br", R))
                rc = slice(P * R, P * R + P)
                for g in range(2):
                    t.transpose(b[:, P * g:P * g + P], sT[:, g, rc], ident[:])
                t.transpose(b[:, 2 * P:3 * P], sT2[:, rc], ident[:])
                for g in range(NG):
                    ins = t.transpose(b[:, 3 * P + NS * g:3 * P + NS * g + NS], sTn[0:NS, g, rc], ident[0:NS, 0:NS])
                filled(("br", R), ins)
            pe.wait_ge(S("bp_ready"), 2)
            b = fill(pe, ("bp", 0))
            for g in range(2):
                for R in range(2):
                    ins = t.transpose(b[:, 256 * g + P * R:256 * g + P * R + P], pR[:, R, P * g:P * g + P], ident[:])
            filled(("bp", 0), ins)
            b = fill(pe, ("bp", 1))
            for R in range(2):
                t.transpose(b[:, P * R:P * R + P], pR[:, R, 2 * P:3 * P], ident[:])
            for R in range(2):
                ins = t.transpose(b[0:NS, 256 + P * R:256 + P * R + P], pR[:, R, 3 * P:3 * P + NS], ident[:])
            filled(("bp", 1), ins)
            b = fill(pe, ("bp", 2))
            for g in range(2):
                for R in range(2):
                    ins = t.transpose(b[0:NS, 256 * g + P * R:256 * g + P * R + P],
                                      pR[:, R, 3 * P + NS + NS * g:3 * P + 2 * NS + NS * g], ident[:])
            filled(("bp", 2), ins)
            for i in range(3):
                landed(pe, ("bp", i))

            def pcols(x, f, b_):
                return x.rearrange("p (h b t) -> p h b t", h=SH, b=DB)[:, 2 * f:2 * f + 2, b_]
            for b_ in range(DB):
                b = fill(pe, ("bo", b_))
                pe.wait_ge(S(f"vs{b_ % 2}"), 64 * (b_ // 2 + 1))
                vs = vring[b_ % 2]
                for f in range(4):
                    fc = slice(P * f, P * f + P)
                    for tt in range(4):
                        c = 8 * f + tt
                        v1 = vs[:, SW * (1 + tt) + P * f:SW * (1 + tt) + P * f + P]
                        t.matmul(b[:, c:c + 5:4], v1, pcols(pTc[:, 1], f, b_)[:, :, tt], start=(tt == 0),
                                 stop=False, skip_group_check=True)
                    for tt in range(2):
                        o2 = b[:, 8 * f:8 * f + 8].rearrange("p (h t) -> p h t", h=2)[:, :, 2 * tt:2 * tt + 2]
                        t.matmul(o2, vs[:, SW * (5 + tt) + P * f:SW * (5 + tt) + P * f + P],
                                 pcols(pT2s, f, b_)[:, :, 2 * tt:2 * tt + 2], start=False, stop=False,
                                 skip_group_check=True)
                    ins = t.matmul(b[:, 8 * f:8 * f + 8], vs[:, fc], pcols(pTc[:, 0], f, b_), start=False,
                                   stop=True, skip_group_check=True)
                filled(("bo", b_), ins)
            b = fill(pe, ("bo", "new"))
            for f in range(4):
                for g in range(NG):
                    ins = t.matmul(b[:, 64 * f:64 * f + 64], Vt[0:NS, 4, g, P * f:P * f + P],
                                   pTn[0:NS, g, 64 * f:64 * f + 64], start=(g == 0), stop=(g == NG - 1))
            filled(("bo", "new"), ins)
            for b_ in list(range(DB)) + ["new"]:
                landed(pe, ("bo", b_))
            for n in range(NA):
                if n >= NA - 8:
                    landed(pe, ("ao", n))

        def v_sattn(L):
            v = nc.vector
            L.did(v.memset(qbd.rearrange("p g f b h t -> p (g f b h t)"), 0.0))
            L.settle()
            L.did(v.memset(sT2, BIG))
            for g in range(NG):
                for h in range(2):
                    q = slice(64 * h, 64 * h + 64)
                    L.did(v.tensor_copy(qbd[q, g, :, :, h, :], q2[q, g, :, SEQ:].rearrange("p f (b t) -> p f b t", b=DB)),
                          "qbd_ready" if (g, h) == (NG - 1, 1) else None)

            def cols3(x, b_):
                return x.rearrange("p (h b t) -> p h b t", h=SH, b=DB)[:, :, b_]
            L.settle()
            for i in range(2):
                b = full(L, ("bn", i))
                for g in range(NG):
                    mk = mkn[0:NS, 0:NS] if g == 0 else mkn[0:NS, NS:]
                    ins = v.tensor_tensor(sTn[0:NS, g].rearrange("p (f e n) -> p f e n", f=4, e=2)[:, :, i],
                                          b[0:NS, P * g:P * g + P].rearrange("p (f n) -> p f n", f=4),
                                          mk.unsqueeze(1).to_broadcast([NS, 4, NS]), ALU.add)
                    if g < NG - 1:
                        L.did(ins)
                    else:
                        free(L, ("bn", i), ins)
            for nb in range(DB + 1):
                if nb < DB:
                    KT0, KT1, KT2 = KTb[nb % 2]
                    if nb >= 2:
                        full(L, ("bs", nb - 2))
                    for i in (0, 2, 4, 6):
                        b = full(L, ("bkT", nb, i))
                        dst = (KT0[:, :] if i == 0 else KT1[:, i - 1] if i < 5 else KT2[:, 1])
                        free(L, ("bkT", nb, i), v.tensor_copy(dst.rearrange("p f j -> p (f j)"), b[:, :]))
                if nb == 0:
                    continue
                b_ = nb - 1
                b = full(L, ("bs", b_))

                def src(c, q=P):
                    return b[0:q, 32 * c:32 * c + 32].rearrange("p (h t) -> p h t", t=DS)
                L.did(v.tensor_tensor(cols3(sT[:, 0], b_), src(0), mk0[:].unsqueeze(1).to_broadcast([P, SH, DS]), ALU.add))
                L.did(v.tensor_copy(cols3(sT[:, 1], b_), src(1)))
                for e in range(2):
                    q = slice(64 * e, 64 * e + 64)
                    ins = v.tensor_copy(cols3(sT2[q], b_)[:, :, e::2],
                                        b[q, 64:96].rearrange("p (h t) -> p h t", t=DS)[:, :, e::2])
                    if e:
                        free(L, ("bs", b_), ins)
                    else:
                        L.did(ins)
            for R in range(2):
                b = full(L, ("br", R))
                L.did(v.tensor_reduce(sa[:, 40 + R:41 + R], b[:, 0:RW], AX, ALU.max))
            L.ts(sa[:, 42:44], sa[:, 40:42], -SS, None, ALU.mult, sem="bnmx_ready")
            landed(L.e, ("br", 0))
            landed(L.e, ("br", 1))
            L.recip(sa[:, 46:48], sa[:, 44:46])
            L.settle()
            for R in range(2):
                L.did(v.tensor_scalar(pR[:, R], pR[:, R], sa[:, 46 + R:47 + R], None, ALU.mult), "bp_ready")
            b = full(L, ("bp", 0))
            free(L, ("bp", 0), v.tensor_copy(pTc.rearrange("p g n -> p (g n)"), b[:, :]))
            b = full(L, ("bp", 1))
            L.did(v.tensor_copy(pT2s, b[:, 0:256]))
            free(L, ("bp", 1), v.tensor_copy(pTn[0:NS, 0], b[0:NS, 256:512]))
            b = full(L, ("bp", 2))
            free(L, ("bp", 2), v.tensor_copy(pTn[0:NS, 1:3].rearrange("p g n -> p (g n)"), b[0:NS, :]))
            for b_ in range(DB):
                b = full(L, ("bo", b_))
                for h in range(2):
                    q = slice(64 * h, 64 * h + 64)
                    ins = v.tensor_copy(hT[q, 0:4, SEQ + DS * b_:SEQ + DS * b_ + DS],
                                        b[q, 0:32].rearrange("p (f h t) -> p f h t", f=4, h=2)[:, :, h])
                    if h:
                        free(L, ("bo", b_), ins)
                    else:
                        L.did(ins)
            b = full(L, ("bo", "new"))
            L.settle()
            for h in range(2):
                q = slice(64 * h, 64 * h + 64)
                x = hT[q, 0:4, SEQ:]
                ins = v.tensor_tensor(x, x, b[q, 0:256].rearrange("p (f h n) -> p f h n", f=4, h=2)[:, :, h], ALU.add)
                if h:
                    free(L, ("bo", "new"), ins)
                else:
                    L.did(ins)

        def a_sattn(L):
            s = nc.scalar
            landed(L.e, ("as", NA - 1, 0))
            landed(L.e, ("as", NA - 1, 1))
            for b_ in range(DB):
                KT0, KT1, KT2 = KTb[b_ % 2]
                if b_ >= 2:
                    full(L, ("bs", b_ - 2))
                for i in (1, 3, 5):
                    b = full(L, ("bkT", b_, i))
                    dst = KT1[:, i - 1] if i < 5 else KT2[:, 0]
                    free(L, ("bkT", b_, i), s.activation(dst.rearrange("p f j -> p (f j)"), b[:, :], ACT.Copy))
            L.need("bnmx_ready", 1)
            for R in range(2):
                b = full(L, ("br", R))
                free(L, ("br", R), s.activation(pR[:, R], b[:, 0:RW], ACT.Exp, bias=sa[:, 42 + R:43 + R], scale=SS,
                                                accum_out=sa[:, 44 + R:45 + R]))

        yo = arena[:, 17000:17000 + 2 * D].rearrange("p (i n) -> p i n", i=2)

        def pe_out(pe):
            for m in range(KT):
                for h in range(2):
                    landed(pe, ("fo1", m, h))
            for tt in range(5):
                for q in range(2):
                    b = fill(pe, ("out", tt, q))
                    for f in range(4):
                        ins = nc.tensor.transpose(b[0:rows(tt), P * f:P * f + P], xT[:, 4 * q + f, tsl(tt)], ident[:])
                    filled(("out", tt, q), ins)

        def a_out(L):
            for tt in range(5):
                if tt >= 2:
                    L.need(f"y_out{tt % 2}", 16 * (tt // 2))
                b = full(L, ("out", tt, 0))
                free(L, ("out", tt, 0), nc.scalar.activation(yo[0:rows(tt), tt % 2, 0:512], b[0:rows(tt), :], ACT.Copy))

        def v_out(L):
            for tt in range(5):
                if tt >= 2:
                    L.need(f"y_out{tt % 2}", 16 * (tt // 2))
                b = full(L, ("out", tt, 1))
                free(L, ("out", tt, 1), nc.vector.tensor_copy(yo[0:rows(tt), tt % 2, 512:], b[0:rows(tt), :]))

        def sp_out(sp):
            for tt in range(5):
                landed(sp, ("out", tt, 0))
                landed(sp, ("out", tt, 1))
                dst = o[0][0, P * tt:P * tt + P] if tt < 4 else o[1].rearrange("b t n -> (b t) n")
                sp.dma_start(dst, yo[0:rows(tt), tt % 2]).then_inc(S(f"y_out{tt % 2}"), 16)

        block = ctx.enter_context(nc.Block())

        @block.sync
        def _(sp):
            sp_params(sp)
            sp_x8(sp, 0, 0)
            load_unit(sp, a["mem_w_kv"][0], ("kv", 0, 0), KT, slice(0, D), cols(0))
            load_unit(sp, a["mem_w_kv"][0], ("kv", 0, 1), KT, slice(0, D), cols(1))
            for j in range(2, 8):
                if j < NB + 1:
                    sp_x8(sp, 0, j - 1)
                elif j == NB + 1:
                    sp_x8(sp, 1, 0)
                load_unit(sp, a["mem_w_kv"][0], ("kv", 0, j), KT, slice(0, D), cols(j))
                if j < 6:
                    sp.wait_ge(S("mk_ready"), j - 1)
                    sp.dma_start(o[10][0, 0].rearrange("(c p) h n -> p c h n", p=P)[:, :, j - 2], kout) \
                      .then_inc(S("mk_out"), 16)
            load_unit(sp, a["ssm_w_glu"][0], ("glu", 0, 0), KT, slice(0, D), cols(0))
            for k in range(NB):
                if k + 1 < NB:
                    sp_x8(sp, 1, k + 1)
                sp_toeplitz(sp, k)
            for i in range(2):
                landed(sp, ("yT", NB - 1, 1, i))
            load_unit(sp, a["ssm_w_glu"][0], ("glu", 1, 0), KT, slice(0, D), cols(1))
            sp_final(sp)
            for j in (2, 3):
                load_unit(sp, a["ssm_w_glu"][0], ("glu", j, 0), KT, slice(0, D), cols(j))
            for j in range(8):
                load_unit(sp, a["mem_w_kv"][1], ("kv", 1, j), KT, slice(0, D), cols(j))
                if 2 <= j < 6:
                    sp.wait_ge(S("mk_ready"), 4 + j - 1)
                    sp.dma_start(o[10][1, 0].rearrange("(c p) h n -> p c h n", p=P)[:, :, j - 2], kout) \
                      .then_inc(S("mk_out"), 16)
            for l in range(2):
                if l == 1:
                    sp_qkv(sp)
                    load_resid(sp, a["attn_w_o"][0], "wo", 1, 4)
                for h in range(MH):
                    load_unit(sp, a["mem_w_q"][l], ("mq", l, h), KT, slice(0, D), cols(h))
                load_resid(sp, a["mem_w_o"][l], f"mo{l}", 1, KT)
                sp_ffn(sp, l)
            sp_out(sp)
            sp.wait_ge(S("y_out0"), 16 * 3)
            sp.wait_ge(S("y_out1"), 16 * 2)
            sp.wait_ge(S("out"), 16 * n_out[0])
            sp.wait_ge(S("mk_out"), 16 * 8)

        @block.gpsimd
        def _(pool):
            L = Lane(pool, "pool_done")
            pool_consts(L)
            for k in range(NB):
                pool_qb(L, k)
            for l in range(2):
                for j in range(4, 8):
                    landed(pool, ("kv", l, j))
                pool.dma_start(o[11][l, 0].rearrange("(c p) h n -> p c (h n)", p=P), mV[:, l]).then_inc(S("mv_out"), 16)
            sp_cache(pool, 0)
            pool.wait_ge(S("mv_out"), 32)
            pool_masks(L)
            pool_keys(L)
            sp_swacache(pool)
            sp_cache(pool, 1)
            pool.wait_ge(S("v_stored"), 32 * 6)
            pool.wait_ge(S("k_stored0"), 32 * 3)
            pool.wait_ge(S("k_stored1"), 32 * 3)

        @block.scalar
        def _(sc):
            L = Lane(sc, "act_done")
            act_loads(sc)
            L.need("consts_ready", 1)
            a_stats_mem(L)
            a_xT(L)
            a_memkv(L, 0)
            for k in range(NB):
                a_batch(L, k)
            a_glu(L)
            a_memkv(L, 1)
            a_norm(L, 0)
            a_memattn(L, 0)
            a_squares(L, "mo0", 1)
            a_split(L, 0, (0,), reuse=False)
            a_norm(L, 1)
            a_ffn(L, 0)
            a_squares(L, "fo0", 2)
            a_norm(L, 2)
            a_qkv(L)
            a_attn(L)
            a_sattn(L)
            a_squares(L, "wo", 3)
            a_norm(L, 3)
            a_memattn(L, 1)
            a_squares(L, "mo1", 4)
            a_split(L, 1, (0,), reuse=False)
            a_norm(L, 4)
            a_ffn(L, 1)
            a_out(L)

        @block.vector
        def _(vv):
            L = Lane(vv, "dve_done")
            vec(L)
            v_mem_norm(L)
            v_params_early(L)
            v_params_turned(L)
            v_params(L)
            v_memkv(L, 0, (v_powers, v_bbar, v_decay))
            v_stats8(L)
            for k in range(NB + 1):
                if k >= 1:
                    v_batch(L, k - 1)
                if k < NB:
                    v_norm8(L, k)
                    if k == 0:
                        v_rotations(L)
                    else:
                        v_ca(L, k)
            v_final(L)
            v_glu(L)
            v_memkv(L, 1)
            for m in range(KT):
                v_sum_squares(L, 0, m)
            v_norm(L, 0, lambda m: g_mem(0, m))
            v_memattn(L, 0)
            v_resid(L, "mo0", 1)
            v_split(L, 0, (0,))
            v_norm_split(L, 1, lambda m: g_ffn(0, m))
            v_ffn(L, 0)
            for m in range(KT):
                v_sum_squares(L, 2, m)
            v_norm(L, 2, lambda m: g_mix(1, m))
            v_masks(L)
            v_qkv(L)
            v_attn(L)
            v_sattn(L)
            v_resid(L, "wo", 3)
            v_norm(L, 3, lambda m: g_mem(1, m))
            v_memattn(L, 1)
            v_resid(L, "mo1", 4)
            v_split(L, 1, (0,))
            v_norm_split(L, 4, lambda m: g_ffn(1, m))
            v_ffn(L, 1)
            v_out(L)

        @block.tensor
        def _(pe):
            pe.wait_ge(S("consts_ready"), 1)
            pe_setup(pe)
            pe_memkv(pe, 0)
            for k in range(NB):
                pe_batch(pe, k)
            pe_final(pe)
            for f in range(2):
                for i in range(2):
                    landed(pe, ("yT", NB - 1, f, i))
            pe_resid(pe, "glu", KT, hT)
            pe_memkv(pe, 1)
            pe_norm(pe, 0)
            pe_memattn(pe, 0)
            pe_norm(pe, 1)
            pe_ffn(pe, 0)
            pe_norm(pe, 2)
            pe_qkv(pe)
            pe_attn(pe)
            pe_sattn(pe)
            pe_resid(pe, "wo", 4, hT)
            pe_norm(pe, 3)
            pe_memattn(pe, 1)
            pe_norm(pe, 4)
            pe_ffn(pe, 1)
            pe_out(pe)


_SWA_OUT = [(1, 1, 128, 8, 64)] * 2 + [(1, 1, 512, 8, 64)] * 4
_OUTS = ([(1, 512, 1024), (8, 4, 1024), (1, 1, 64, 64), (1, 1, 64, 64)] + _SWA_OUT
         + [(2, 1, 256, 4, 256)] * 2 + [(1, 8, 64, 64)] * 2 + [(1, 8, 4, 8, 64)] * 6)


def kernel(**inputs):
    import numpy as _np
    import concourse.bacc as _bacc
    from concourse import mybir as _mybir
    from concourse.bass_utils import run_bass_kernel_spmd as _run

    nc = _bacc.Bacc("TRN2", target_bir_lowering=False, num_devices=1)
    arrays, args = {}, {}
    for name, value in inputs.items():
        v = _np.ascontiguousarray(value)
        arrays[f"in_{name}_dram"] = v
        args[name] = nc.dram_tensor(f"in_{name}_dram", v.shape, _mybir.dt.from_np(v.dtype), kind="ExternalInput").ap()
    outs = [nc.dram_tensor(f"out_{i}_dram", shape, _mybir.dt.float32, kind="ExternalOutput").ap()
            for i, shape in enumerate(_OUTS)]
    hybrid_step(nc, args, outs)
    r = _run(nc, [arrays], core_ids=[0])
    return tuple(r.results[0][f"out_{i}_dram"] for i in range(len(_OUTS)))
```
